# Optimizing a Trainium2 kernel written in Bass

```python
import math
import jax, jax.numpy as jnp
from jax import lax
import numpy as np

D_MODEL = 1024
BATCH = 1
SEQ = 256
DEPTH = 1

HEAD_DIM = 64
BRANCH_WIDTH = D_MODEL // 2
N_BRANCHES = 4
Q_BLOCK = 128
FOX_HEADS = BRANCH_WIDTH // HEAD_DIM
LRU_BLOCKS = 8
LRU_BLOCK_DIM = BRANCH_WIDTH // LRU_BLOCKS
CONV_WIDTH = 4
LRU_C = 8.0
NSA_HEADS = BRANCH_WIDTH // HEAD_DIM
NSA_KV_HEADS = 2
NSA_GROUP = NSA_HEADS // NSA_KV_HEADS
NSA_KV_WIDTH = NSA_KV_HEADS * HEAD_DIM
CMP_BLOCK = 32
CMP_STRIDE = 16
CMP_HIDDEN = 2 * HEAD_DIM
SLC_BLOCK = 64
SLC_TOPK = 16
SLC_LOCAL = 2
SLC_FORCE_SCORE = 1e6
WINDOW = 512
SG_CHUNK = 128
SG_GROUPS = 8
SG_GROUP_DIM = BRANCH_WIDTH // SG_GROUPS

NORM_EPS = 1e-6
NEG_INF = -1e30


def _in_split_sizes():
    W = BRANCH_WIDTH
    return (W, W, W, FOX_HEADS, W,
            W, W,
            W, NSA_KV_WIDTH, NSA_KV_WIDTH, NSA_KV_WIDTH,
            NSA_KV_WIDTH, NSA_KV_WIDTH, NSA_KV_WIDTH,
            3 * NSA_HEADS, W,
            W, W, W,
            N_BRANCHES * D_MODEL)

def rms_norm(x, g):
    x32 = x.astype(jnp.float32)
    y = x32 * lax.rsqrt(jnp.mean(x32 * x32, axis=-1, keepdims=True) + NORM_EPS)
    return (y * g.astype(jnp.float32)).astype(x.dtype)

def layer_norm(x, g):
    x32 = x.astype(jnp.float32)
    mu = jnp.mean(x32, axis=-1, keepdims=True)
    xc = x32 - mu
    y = xc * lax.rsqrt(jnp.mean(xc * xc, axis=-1, keepdims=True) + NORM_EPS)
    return (y * g.astype(jnp.float32)).astype(x.dtype)

def masked_softmax(s, mask):
    p = jax.nn.softmax(jnp.where(mask, s, NEG_INF), axis=-1)
    return jnp.where(mask, p, 0.0)

def fox_attention(q, k, v, f_logit):
    B, S, H, dh = q.shape
    n_blk = S // Q_BLOCK
    scale = 1.0 / math.sqrt(dh)
    c = jnp.cumsum(jax.nn.log_sigmoid(f_logit.astype(jnp.float32)), axis=1)
    c_k = c.transpose(0, 2, 1)[:, :, None, :]
    qb = q.reshape(B, n_blk, Q_BLOCK, H, dh).transpose(1, 0, 2, 3, 4)
    cb = c.reshape(B, n_blk, Q_BLOCK, H).transpose(1, 0, 2, 3)
    pos_k = jnp.arange(S)

    def block(args):
        q_i, c_i, i = args
        t = i * Q_BLOCK + jnp.arange(Q_BLOCK)
        s = jnp.einsum('bqhd,bkhd->bhqk', q_i, k).astype(jnp.float32) * scale
        s = s + c_i.transpose(0, 2, 1)[..., None] - c_k
        p = masked_softmax(s, pos_k[None, :] <= t[:, None])
        return jnp.einsum('bhqk,bkhd->bqhd', p.astype(v.dtype), v)

    out = lax.map(block, (qb, cb, jnp.arange(n_blk)))
    return out.transpose(1, 0, 2, 3, 4).reshape(B, S, H, dh)

def rg_lru(xb, conv_w, conv_b, w_a, b_a, w_x, b_x, lam):
    B, S, W = xb.shape
    xc = lax.conv_general_dilated(
        xb, conv_w.reshape(CONV_WIDTH, 1, W).astype(xb.dtype), window_strides=(1,),
        padding=[(CONV_WIDTH - 1, 0)], dimension_numbers=('NWC', 'WIO', 'NWC'),
        feature_group_count=W) + conv_b
    xh = xc.reshape(B, S, LRU_BLOCKS, LRU_BLOCK_DIM)
    r = jax.nn.sigmoid((jnp.einsum('bsnd,nde->bsne', xh, w_a).reshape(B, S, W) + b_a).astype(jnp.float32))
    i_g = jax.nn.sigmoid((jnp.einsum('bsnd,nde->bsne', xh, w_x).reshape(B, S, W) + b_x).astype(jnp.float32))
    log_a = -LRU_C * r * jax.nn.softplus(-lam.astype(jnp.float32))
    a = jnp.exp(log_a)
    b = jnp.sqrt(-jnp.expm1(2.0 * log_a)) * (i_g * xc.astype(jnp.float32))

    def combine(left, right):
        a_l, b_l = left
        a_r, b_r = right
        return a_l * a_r, a_r * b_l + b_r

    _, h = lax.associative_scan(combine, (a, b), axis=1)
    return h.astype(xb.dtype)

def _cmp_slc_overlap(n_cmp, n_slc):
    c0 = np.arange(n_cmp) * CMP_STRIDE
    s0 = np.arange(n_slc) * SLC_BLOCK
    ov = np.minimum(c0[:, None] + CMP_BLOCK, s0[None, :] + SLC_BLOCK) - np.maximum(c0[:, None], s0[None, :])
    return (np.clip(ov, 0, None) / CMP_BLOCK).astype(np.float32)

def nsa_attention(q, k_cmp, v_cmp, k_slc, v_slc, k_win, v_win, gates,
                  kn_g, cmp_pos, wk1, wk2, wv1, wv2):
    B, S, H, dh = q.shape
    G, R = NSA_KV_HEADS, NSA_GROUP
    scale = 1.0 / math.sqrt(dh)
    n_cmp = (S - CMP_BLOCK) // CMP_STRIDE + 1
    blk_idx = np.arange(n_cmp)[:, None] * CMP_STRIDE + np.arange(CMP_BLOCK)[None, :]
    cmp_end = jnp.asarray(blk_idx[:, -1])

    def compress(t, w1, w2):
        tb = t[:, blk_idx] + cmp_pos[None, None, :, None, :]
        tb = tb.transpose(0, 1, 3, 2, 4).reshape(B, n_cmp, G, CMP_BLOCK * dh)
        return jax.nn.silu(tb @ w1) @ w2

    k_c = rms_norm(compress(k_cmp, wk1, wk2), kn_g)
    v_c = compress(v_cmp, wv1, wv2)
    n_slc = S // SLC_BLOCK
    top_k = min(SLC_TOPK, n_slc)
    overlap = jnp.asarray(_cmp_slc_overlap(n_cmp, n_slc))
    ks_blk = rms_norm(k_slc, kn_g).reshape(B, n_slc, SLC_BLOCK, G, dh).transpose(0, 3, 1, 2, 4)
    vs_blk = v_slc.reshape(B, n_slc, SLC_BLOCK, G, dh).transpose(0, 3, 1, 2, 4)
    kw_pad = jnp.pad(rms_norm(k_win, kn_g), ((0, 0), (WINDOW, 0), (0, 0), (0, 0)))
    vw_pad = jnp.pad(v_win, ((0, 0), (WINDOW, 0), (0, 0), (0, 0)))
    span = WINDOW + Q_BLOCK

    n_blk = S // Q_BLOCK
    qg = q.reshape(B, n_blk, Q_BLOCK, G, R, dh).transpose(1, 0, 2, 3, 4, 5)
    gb = gates.reshape(B, n_blk, Q_BLOCK, 3, H).transpose(1, 0, 2, 3, 4)
    b_ix = jnp.arange(B)[:, None, None, None]
    g_ix = jnp.arange(G)[None, :, None, None]
    j = jnp.arange(n_slc)

    def block(args):
        q_i, g_i, i = args
        t = i * Q_BLOCK + jnp.arange(Q_BLOCK)
        s_c = jnp.einsum('bqgrd,bcgd->bgrqc', q_i, k_c).astype(jnp.float32) * scale
        p_c = masked_softmax(s_c, cmp_end[None, :] <= t[:, None])
        o_c = jnp.einsum('bgrqc,bcgd->bqgrd', p_c.astype(v_c.dtype), v_c)
        imp = jnp.einsum('bgrqc,cj->bgqj', p_c, overlap)
        jt = t // SLC_BLOCK
        valid = j[None, :] <= jt[:, None]
        forced = (j[None, :] == 0) | (valid & (j[None, :] > jt[:, None] - SLC_LOCAL))
        score = jnp.where(forced, SLC_FORCE_SCORE, jnp.where(valid, imp, -1.0))
        top_val, top_idx = lax.top_k(score, top_k)
        k_sel = ks_blk[b_ix, g_ix, top_idx]
        v_sel = vs_blk[b_ix, g_ix, top_idx]
        key_pos = top_idx[..., None] * SLC_BLOCK + jnp.arange(SLC_BLOCK)
        m_s = (top_val >= 0.0)[..., None] & (key_pos <= t[None, None, :, None, None])
        s_s = jnp.einsum('bqgrd,bgqkld->bgrqkl', q_i, k_sel).astype(jnp.float32) * scale
        n_sel = top_k * SLC_BLOCK
        p_s = masked_softmax(s_s.reshape(B, G, R, Q_BLOCK, n_sel), m_s.reshape(B, G, 1, Q_BLOCK, n_sel))
        o_s = jnp.einsum('bgrqn,bgqnd->bqgrd', p_s.astype(v_sel.dtype),
                         v_sel.reshape(B, G, Q_BLOCK, n_sel, dh))
        k_wi = lax.dynamic_slice_in_dim(kw_pad, i * Q_BLOCK, span, axis=1)
        v_wi = lax.dynamic_slice_in_dim(vw_pad, i * Q_BLOCK, span, axis=1)
        pos_w = i * Q_BLOCK - WINDOW + jnp.arange(span)
        m_w = (pos_w[None, :] >= 0) & (pos_w[None, :] <= t[:, None]) & (pos_w[None, :] > t[:, None] - WINDOW)
        s_w = jnp.einsum('bqgrd,bkgd->bgrqk', q_i, k_wi).astype(jnp.float32) * scale
        p_w = masked_softmax(s_w, m_w)
        o_w = jnp.einsum('bgrqk,bkgd->bqgrd', p_w.astype(v_wi.dtype), v_wi)
        g = g_i.reshape(B, Q_BLOCK, 3, G, R)[..., None]
        return g[:, :, 0] * o_c + g[:, :, 1] * o_s + g[:, :, 2] * o_w

    out = lax.map(block, (qg, gb, jnp.arange(n_blk)))
    return out.transpose(1, 0, 2, 3, 4, 5).reshape(B, S, H * dh)

def spatial_gating(u, v, ln_g, w_s, b_s):
    B, S, W = u.shape
    n_chunk = S // SG_CHUNK
    u = jax.nn.gelu(u, approximate=False)
    v = layer_norm(jax.nn.gelu(v, approximate=False), ln_g)
    vc = v.reshape(B, n_chunk, SG_CHUNK, SG_GROUPS, SG_GROUP_DIM)
    causal = jnp.tril(jnp.ones((SG_CHUNK, SG_CHUNK), dtype=w_s.dtype))
    mixed = jnp.einsum('gts,bcsgd->bctgd', w_s * causal, vc) + b_s.T[None, None, :, :, None]
    return u * mixed.reshape(B, S, W)

def hybrid_layer(x, norm_g, w_in, b_forget, qn_a, kn_a, conv_w, conv_b, w_rg_a, b_rg_a,
                 w_rg_x, b_rg_x, lru_lambda, qn_c, kn_c, cmp_pos, cmp_k_w1, cmp_k_w2,
                 cmp_v_w1, cmp_v_w2, ln_v_g, w_spatial, b_spatial, w_branch, w_out):
    B, S, D = x.shape
    W = BRANCH_WIDTH
    xn = rms_norm(x, norm_g)
    z = xn @ w_in
    split_at = np.cumsum(_in_split_sizes())[:-1].tolist()
    (qa, ka, va, fa, ga, xb, gb, qc, kcc, vcc, ksc, vsc, kwc, vwc, gate_c, gc,
     ud, vd, gd, mg) = jnp.split(z, split_at, axis=-1)
    heads = lambda t, n: t.reshape(B, S, n, HEAD_DIM)
    y_a = fox_attention(rms_norm(heads(qa, FOX_HEADS), qn_a), rms_norm(heads(ka, FOX_HEADS), kn_a),
                        heads(va, FOX_HEADS), fa + b_forget).reshape(B, S, W)
    y_b = rg_lru(xb, conv_w, conv_b, w_rg_a, b_rg_a, w_rg_x, b_rg_x, lru_lambda)
    y_c = nsa_attention(rms_norm(heads(qc, NSA_HEADS), qn_c),
                        heads(kcc, NSA_KV_HEADS), heads(vcc, NSA_KV_HEADS),
                        heads(ksc, NSA_KV_HEADS), heads(vsc, NSA_KV_HEADS),
                        heads(kwc, NSA_KV_HEADS), heads(vwc, NSA_KV_HEADS),
                        jax.nn.sigmoid(gate_c).reshape(B, S, 3, NSA_HEADS),
                        kn_c, cmp_pos, cmp_k_w1, cmp_k_w2, cmp_v_w1, cmp_v_w2)
    y_d = spatial_gating(ud, vd, ln_v_g, w_spatial, b_spatial)
    ys = jnp.stack([y_a * jax.nn.silu(ga), y_b * jax.nn.silu(gb),
                    y_c * jax.nn.silu(gc), y_d * jax.nn.silu(gd)], axis=2)
    proj = jnp.einsum('bsnw,nwd->bsnd', ys, w_branch)
    merged = jnp.sum(jax.nn.sigmoid(mg.reshape(B, S, N_BRANCHES, D)) * proj, axis=2)
    return x + merged @ w_out

def first_inputs(seed: int = 0) -> dict:
    key = jax.random.key(seed)
    ks = iter(jax.random.split(key, 32))
    L, D, W, dh = DEPTH, D_MODEL, BRANCH_WIDTH, HEAD_DIM

    def nrm(shape, scale):
        return jax.random.normal(next(ks), shape, jnp.float32) * scale

    w_in_width = sum(_in_split_sizes())
    x = nrm((BATCH, SEQ, D), 1.0)
    norm_g = 1.0 + nrm((L, D), 0.05)
    w_in = nrm((L, D, w_in_width), D ** -0.5)
    b_forget = 3.0 + nrm((L, FOX_HEADS), 0.5)
    qn_a = 1.0 + nrm((L, dh), 0.05)
    kn_a = 1.0 + nrm((L, dh), 0.05)
    conv_w = nrm((L, CONV_WIDTH, W), CONV_WIDTH ** -0.5)
    conv_b = nrm((L, W), 0.01)
    w_rg_a = nrm((L, LRU_BLOCKS, LRU_BLOCK_DIM, LRU_BLOCK_DIM), LRU_BLOCK_DIM ** -0.5)
    b_rg_a = nrm((L, W), 0.01)
    w_rg_x = nrm((L, LRU_BLOCKS, LRU_BLOCK_DIM, LRU_BLOCK_DIM), LRU_BLOCK_DIM ** -0.5)
    b_rg_x = nrm((L, W), 0.01)
    a_c = jax.random.uniform(next(ks), (L, W), jnp.float32, 0.9, 0.999)
    a0 = a_c ** (1.0 / LRU_C)
    lru_lambda = jnp.log(a0) - jnp.log1p(-a0)
    qn_c = 1.0 + nrm((L, dh), 0.05)
    kn_c = 1.0 + nrm((L, dh), 0.05)
    cmp_pos = nrm((L, CMP_BLOCK, dh), 0.02)
    cmp_k_w1 = nrm((L, CMP_BLOCK * dh, CMP_HIDDEN), (CMP_BLOCK * dh) ** -0.5)
    cmp_k_w2 = nrm((L, CMP_HIDDEN, dh), CMP_HIDDEN ** -0.5)
    cmp_v_w1 = nrm((L, CMP_BLOCK * dh, CMP_HIDDEN), (CMP_BLOCK * dh) ** -0.5)
    cmp_v_w2 = nrm((L, CMP_HIDDEN, dh), CMP_HIDDEN ** -0.5)
    ln_v_g = 1.0 + nrm((L, W), 0.05)
    w_spatial = nrm((L, SG_GROUPS, SG_CHUNK, SG_CHUNK), SG_CHUNK ** -0.5)
    b_spatial = 1.0 + nrm((L, SG_GROUPS, SG_CHUNK), 0.1)
    w_branch = nrm((L, N_BRANCHES, W, D), W ** -0.5)
    w_out = nrm((L, D, D), D ** -0.5)
    return {"x": x, "norm_g": norm_g, "w_in": w_in, "b_forget": b_forget, "qn_a": qn_a,
            "kn_a": kn_a, "conv_w": conv_w, "conv_b": conv_b, "w_rg_a": w_rg_a,
            "b_rg_a": b_rg_a, "w_rg_x": w_rg_x, "b_rg_x": b_rg_x, "lru_lambda": lru_lambda,
            "qn_c": qn_c, "kn_c": kn_c, "cmp_pos": cmp_pos, "cmp_k_w1": cmp_k_w1,
            "cmp_k_w2": cmp_k_w2, "cmp_v_w1": cmp_v_w1, "cmp_v_w2": cmp_v_w2,
            "ln_v_g": ln_v_g, "w_spatial": w_spatial, "b_spatial": b_spatial,
            "w_branch": w_branch, "w_out": w_out}

def first_block(x, norm_g, w_in, b_forget, qn_a, kn_a, conv_w, conv_b, w_rg_a, b_rg_a,
              w_rg_x, b_rg_x, lru_lambda, qn_c, kn_c, cmp_pos, cmp_k_w1, cmp_k_w2,
              cmp_v_w1, cmp_v_w2, ln_v_g, w_spatial, b_spatial, w_branch, w_out):
    for l in range(DEPTH):
        x = hybrid_layer(x, norm_g[l], w_in[l], b_forget[l], qn_a[l], kn_a[l], conv_w[l],
                         conv_b[l], w_rg_a[l], b_rg_a[l], w_rg_x[l], b_rg_x[l], lru_lambda[l],
                         qn_c[l], kn_c[l], cmp_pos[l], cmp_k_w1[l], cmp_k_w2[l], cmp_v_w1[l],
                         cmp_v_w2[l], ln_v_g[l], w_spatial[l], b_spatial[l], w_branch[l], w_out[l])
    return x


GRID_W = 64
CTX_LEN = 256

D_HY = D_MODEL // 4
D_HG = D_MODEL // 2
D_FN = D_MODEL // 4
D_MIX = D_HY + D_HG + D_FN

HY_ORDER = 2
HY_SHORT_CONV = 3
HY_BANDS = 16
HY_EMB_DIM = 1 + 2 * HY_BANDS
HY_FILTER_HIDDEN = 64
HY_DECAY_TARGET = 1e-2
HY_FAST_DECAY_PCT = 0.3
HY_SLOW_DECAY_PCT = 1.5
D_HY_PROJ = (HY_ORDER + 1) * D_HY

HG_HEAD_DIM = 128
HG_HEADS = D_HG // HG_HEAD_DIM
HG_CHUNK = 64
HG_PROJ = 5 * D_HG

FN_GROUPS = 4
FN_GROUP_DIM = D_FN // FN_GROUPS

D_PROJ = D_HY_PROJ + HG_PROJ + D_FN

N_EXPERTS = 16
N_GROUPS = 4
EXPERTS_PER_GROUP = N_EXPERTS // N_GROUPS
TOP_K = 2
D_EXPERT = 512

N_MOD = 6
RMS_EPS = 1e-6
POS_BASE = 10000.0


def rmsnorm(x, g):
    xf = x.astype(jnp.float32)
    y = xf * lax.rsqrt(jnp.mean(xf * xf, axis=-1, keepdims=True) + RMS_EPS)
    return (y * g.astype(jnp.float32)).astype(x.dtype)

def modulate(h, shift, scale):
    return h * (1 + scale) + shift

def ada_modulation(cond, w, b):
    return jnp.split(jax.nn.silu(cond) @ w + b, N_MOD, axis=-1)

def grid_sincos(n_tok):
    rows = n_tok // GRID_W
    row = jnp.repeat(jnp.arange(rows, dtype=jnp.float32), GRID_W)
    col = jnp.tile(jnp.arange(GRID_W, dtype=jnp.float32), rows)
    quarter = D_MODEL // 4
    omega = 1.0 / (POS_BASE ** (jnp.arange(quarter, dtype=jnp.float32) / quarter))
    ar = row[:, None] * omega
    ac = col[:, None] * omega
    return jnp.concatenate([jnp.sin(ar), jnp.cos(ar), jnp.sin(ac), jnp.cos(ac)], axis=-1)

def short_conv3(u, w, b):
    up = jnp.pad(u, ((0, 0), (1, 1), (0, 0)))
    return up[:, :-2] * w[0] + up[:, 1:-1] * w[1] + up[:, 2:] * w[2] + b

def hyena_deltas():
    max_decay = math.log(HY_DECAY_TARGET) / HY_FAST_DECAY_PCT
    min_decay = math.log(HY_DECAY_TARGET) / HY_SLOW_DECAY_PCT
    return jnp.linspace(min_decay, max_decay, D_HY, dtype=jnp.float32)

def hyena_filters(L, w1, b1, w2, b2, w3, freq):
    f32 = jnp.float32
    t = jnp.linspace(0.0, 1.0, L, dtype=f32)[:, None]
    w = 2.0 * math.pi * jnp.arange(L, dtype=f32)[:, None] / L
    bands = jnp.linspace(1e-4, HY_BANDS - 1, HY_BANDS, dtype=f32)[None, :]
    z = jnp.concatenate([t, jnp.cos(bands * w), -jnp.sin(bands * w)], axis=-1)
    fr = freq.astype(f32)
    h = jnp.sin(fr * (z @ w1.astype(f32) + b1.astype(f32)))
    h = jnp.sin(fr * (h @ w2.astype(f32) + b2.astype(f32)))
    h = (h @ w3.astype(f32)).reshape(L, 2 * HY_ORDER, D_HY)
    decay = jnp.exp(-t[:, :, None] * jnp.abs(hyena_deltas()))
    return h * decay

def bidir_fftconv(u, h_fwd, h_bwd, skip):
    L, C = h_fwd.shape
    k = jnp.concatenate([h_fwd, jnp.zeros((1, C), jnp.float32), h_bwd[1:][::-1]], axis=0)
    uf = jnp.fft.rfft(u.astype(jnp.float32), n=2 * L, axis=1)
    kf = jnp.fft.rfft(k, n=2 * L, axis=0)
    y = jnp.fft.irfft(uf * kf[None], n=2 * L, axis=1)[:, :L]
    return (y + u.astype(jnp.float32) * skip.astype(jnp.float32)).astype(u.dtype)

def hyena_mixer(z, conv_w, conv_b, w1, b1, w2, b2, w3, freq, bias, norm_g):
    L = z.shape[1]
    u = short_conv3(z, conv_w, conv_b)
    v, x1, x2 = jnp.split(u, HY_ORDER + 1, axis=-1)
    h = hyena_filters(L, w1, b1, w2, b2, w3, freq)
    y = x1 * bidir_fftconv(v, h[:, 0], h[:, 1], bias[0])
    y = x2 * bidir_fftconv(y, h[:, 2], h[:, 3], bias[1])
    return rmsnorm(y, norm_g)

def fourier_mixer(z, w, b, norm_g):
    B, L, _ = z.shape
    zg = z.astype(jnp.float32).reshape(B, L, FN_GROUPS, FN_GROUP_DIM)
    y = jnp.fft.fftn(zg, axes=(1, 3), norm="ortho").real
    y = jnp.einsum("blgc,gcd->blgd", y, w.astype(jnp.float32)).reshape(B, L, D_FN) + b.astype(jnp.float32)
    return rmsnorm(y.astype(z.dtype), norm_g)

def hgrn_lower_bounds(raw):
    cs = jnp.cumsum(jax.nn.softmax(raw.astype(jnp.float32), axis=0), axis=0)
    return cs - cs[0:1]

def hgrn2_inputs(z, lb):
    B, L, _ = z.shape
    q, f_fwd, f_bwd, i, g = jnp.split(z.astype(jnp.float32), 5, axis=-1)
    heads = lambda t: t.reshape(B, L, HG_HEADS, HG_HEAD_DIM)
    q = heads(jax.nn.silu(q)) * (HG_HEAD_DIM ** -0.5)
    dirs = []
    for d, f_raw in enumerate((f_fwd, f_bwd)):
        lbd = lb[d]
        forget = lbd + (1.0 - lbd) * jax.nn.sigmoid(f_raw)
        dirs.append((heads(1.0 - forget), heads(jnp.log(forget))))
    return q, heads(i), g, dirs

def to_chunks(t):
    B, L, H, d = t.shape
    return t.reshape(B, L // HG_CHUNK, HG_CHUNK, H, d).transpose(1, 0, 3, 2, 4)

def from_chunks(t):
    n, B, H, C, d = t.shape
    return t.transpose(1, 0, 3, 2, 4).reshape(B, n * C, H, d)

def gla_chunk_scan(q, k, v, logf, s0):
    causal = jnp.tril(jnp.ones((HG_CHUNK, HG_CHUNK), dtype=bool))

    def step(s, inp):
        qc, kc, vc, gc = inp
        b = jnp.cumsum(gc, axis=2)
        o_inter = jnp.einsum("bhtd,bhdv->bhtv", qc * jnp.exp(b), s)
        diff = b[:, :, :, None, :] - b[:, :, None, :, :]
        decay = jnp.exp(jnp.where(causal[:, :, None], diff, -jnp.inf))
        scores = jnp.einsum("bhtd,bhsd,bhtsd->bhts", qc, kc, decay)
        o_intra = jnp.einsum("bhts,bhsv->bhtv", scores, vc)
        b_end = b[:, :, -1, :]
        s_new = jnp.exp(b_end)[..., None] * s + jnp.einsum(
            "bhsd,bhsv->bhdv", kc * jnp.exp(b_end[:, :, None, :] - b), vc)
        return s_new, o_inter + o_intra

    s_fin, o = lax.scan(step, s0, (to_chunks(q), to_chunks(k), to_chunks(v), to_chunks(logf)))
    return s_fin, from_chunks(o)

def hgrn2_bidir(q, v, dirs, s0_fwd, s0_bwd):
    (k_f, g_f), (k_b, g_b) = dirs
    s_f, o_f = gla_chunk_scan(q, k_f, v, g_f, s0_fwd)
    flip = lambda t: t[:, ::-1]
    s_b, o_b = gla_chunk_scan(flip(q), flip(k_b), flip(v), flip(g_b), s0_bwd)
    return s_f, s_b, o_f + flip(o_b)

def hgrn2_readout(o, g, norm_g):
    B, L, H, d = o.shape
    on = o * lax.rsqrt(jnp.mean(o * o, axis=-1, keepdims=True) + RMS_EPS)
    return on.reshape(B, L, D_HG) * norm_g.astype(jnp.float32) * jax.nn.silu(g)

def mixer_output(z, o_hg, g_hg, w_out, conv_w, conv_b, w1, b1, w2, b2, w3, freq,
                 hy_bias, hy_norm_g, hg_norm_g, fn_w, fn_b, fn_norm_g):
    y_hy = hyena_mixer(z[..., :D_HY_PROJ], conv_w, conv_b, w1, b1, w2, b2, w3, freq, hy_bias, hy_norm_g)
    y_hg = hgrn2_readout(o_hg, g_hg, hg_norm_g).astype(z.dtype)
    y_fn = fourier_mixer(z[..., D_HY_PROJ + HG_PROJ:], fn_w, fn_b, fn_norm_g)
    return jnp.concatenate([y_hy, y_hg, y_fn], axis=-1) @ w_out

def moe_ffn(h, router_w, router_b, w_gate, w_up, w_down):
    N = h.shape[0]
    probs = jax.nn.softmax(h.astype(jnp.float32) @ router_w.astype(jnp.float32), axis=-1)
    sel = probs + router_b.astype(jnp.float32)
    group_score = lax.top_k(sel.reshape(N, N_GROUPS, EXPERTS_PER_GROUP), TOP_K)[0].sum(-1)
    best_group = jnp.argmax(group_score, axis=-1)
    in_group = (jnp.arange(N_EXPERTS) // EXPERTS_PER_GROUP)[None, :] == best_group[:, None]
    _, idx = lax.top_k(jnp.where(in_group, sel, -jnp.inf), TOP_K)
    gp = jnp.take_along_axis(probs, idx, axis=-1)
    gp = gp / jnp.sum(gp, axis=-1, keepdims=True)
    combine = jnp.sum(jax.nn.one_hot(idx, N_EXPERTS, dtype=jnp.float32) * gp[..., None], axis=1)
    out = jnp.zeros(h.shape, jnp.float32)
    for e in range(N_EXPERTS):
        he = (jax.nn.silu(h @ w_gate[e]) * (h @ w_up[e])) @ w_down[e]
        out = out + combine[:, e:e + 1] * he.astype(jnp.float32)
    return out.astype(h.dtype)

def second_inputs(seed: int = 0) -> dict:
    key = jax.random.key(seed)
    ks = jax.random.split(key, 32)
    f32 = jnp.float32
    nrm = lambda k, shape, s: s * jax.random.normal(k, shape, f32)
    D = D_MODEL
    return {
        "x": nrm(ks[0], (BATCH, SEQ, D), 1.0),
        "c": nrm(ks[1], (BATCH, D), 1.0),
        "ctx": nrm(ks[2], (BATCH, CTX_LEN, D), 1.0),
        "c_ctx": nrm(ks[3], (D,), 1.0),
        "ada_w": nrm(ks[4], (DEPTH, D, N_MOD * D), 0.5 * D ** -0.5),
        "ada_b": nrm(ks[5], (DEPTH, N_MOD * D), 0.02),
        "norm1_g": 1.0 + nrm(ks[6], (DEPTH, D), 0.1),
        "norm2_g": 1.0 + nrm(ks[7], (DEPTH, D), 0.1),
        "w_in": nrm(ks[8], (DEPTH, D, D_PROJ), D ** -0.5),
        "w_out": nrm(ks[9], (DEPTH, D_MIX, D), D_MIX ** -0.5),
        "hy_conv_w": nrm(ks[10], (DEPTH, HY_SHORT_CONV, D_HY_PROJ), 0.5),
        "hy_conv_b": nrm(ks[11], (DEPTH, D_HY_PROJ), 0.02),
        "hy_filt_w1": nrm(ks[12], (DEPTH, HY_EMB_DIM, HY_FILTER_HIDDEN), HY_EMB_DIM ** -0.5),
        "hy_filt_b1": nrm(ks[13], (DEPTH, HY_FILTER_HIDDEN), 0.02),
        "hy_filt_w2": nrm(ks[14], (DEPTH, HY_FILTER_HIDDEN, HY_FILTER_HIDDEN), HY_FILTER_HIDDEN ** -0.5),
        "hy_filt_b2": nrm(ks[15], (DEPTH, HY_FILTER_HIDDEN), 0.02),
        "hy_filt_w3": nrm(ks[16], (DEPTH, HY_FILTER_HIDDEN, 2 * HY_ORDER * D_HY), HY_FILTER_HIDDEN ** -0.5),
        "hy_filt_freq": 1.0 + nrm(ks[17], (DEPTH, HY_FILTER_HIDDEN), 0.1),
        "hy_bias": nrm(ks[18], (DEPTH, HY_ORDER, D_HY), 0.5),
        "hy_norm_g": 1.0 + nrm(ks[19], (DEPTH, D_HY), 0.1),
        "hg_lower_bounds": nrm(ks[20], (DEPTH, 2, D_HG), 1.0),
        "hg_norm_g": 1.0 + nrm(ks[21], (DEPTH, D_HG), 0.1),
        "fn_w": nrm(ks[22], (DEPTH, FN_GROUPS, FN_GROUP_DIM, FN_GROUP_DIM), FN_GROUP_DIM ** -0.5),
        "fn_b": nrm(ks[23], (DEPTH, D_FN), 0.02),
        "fn_norm_g": 1.0 + nrm(ks[24], (DEPTH, D_FN), 0.1),
        "router_w": nrm(ks[25], (D, N_EXPERTS), D ** -0.5),
        "router_b": nrm(ks[26], (N_EXPERTS,), 0.01),
        "moe_w_gate": nrm(ks[27], (DEPTH, N_EXPERTS, D, D_EXPERT), D ** -0.5),
        "moe_w_up": nrm(ks[28], (DEPTH, N_EXPERTS, D, D_EXPERT), D ** -0.5),
        "moe_w_down": nrm(ks[29], (DEPTH, N_EXPERTS, D_EXPERT, D), D_EXPERT ** -0.5),
        "final_norm_g": 1.0 + nrm(ks[30], (D,), 0.1),
    }

def second_block(x, c, ctx, c_ctx, ada_w, ada_b, norm1_g, norm2_g, w_in, w_out, hy_conv_w, hy_conv_b,
              hy_filt_w1, hy_filt_b1, hy_filt_w2, hy_filt_b2, hy_filt_w3, hy_filt_freq, hy_bias, hy_norm_g,
              hg_lower_bounds, hg_norm_g, fn_w, fn_b, fn_norm_g, router_w, router_b,
              moe_w_gate, moe_w_up, moe_w_down, final_norm_g):
    B, L, D = x.shape
    n_ctx = ctx.shape[1]
    lower_bounds = hgrn_lower_bounds(hg_lower_bounds)
    x = x + grid_sincos(L).astype(x.dtype)[None]
    cond_x = c[:, None, :]
    cond_c = c_ctx[None, None, :]
    s_zero = jnp.zeros((B, HG_HEADS, HG_HEAD_DIM, HG_HEAD_DIM), jnp.float32)
    hg_lo, hg_hi = D_HY_PROJ, D_HY_PROJ + HG_PROJ
    for layer in range(DEPTH):
        last = layer == DEPTH - 1
        mod_x = ada_modulation(cond_x, ada_w[layer], ada_b[layer])
        mod_c = ada_modulation(cond_c, ada_w[layer], ada_b[layer])
        mix_params = (w_out[layer], hy_conv_w[layer], hy_conv_b[layer], hy_filt_w1[layer], hy_filt_b1[layer],
                      hy_filt_w2[layer], hy_filt_b2[layer], hy_filt_w3[layer], hy_filt_freq[layer],
                      hy_bias[layer], hy_norm_g[layer], hg_norm_g[layer], fn_w[layer], fn_b[layer], fn_norm_g[layer])
        hx = modulate(rmsnorm(x, norm1_g[layer]), mod_x[0], mod_x[1])
        hc = modulate(rmsnorm(ctx, norm1_g[layer]), mod_c[0], mod_c[1])
        zx = hx @ w_in[layer]
        zc = hc @ w_in[layer]
        q_c, v_c, g_c, dirs_c = hgrn2_inputs(zc[..., hg_lo:hg_hi], lower_bounds[layer])
        s_f, s_b, o_c = hgrn2_bidir(q_c, v_c, dirs_c, s_zero, s_zero)
        q_x, v_x, g_x, dirs_x = hgrn2_inputs(zx[..., hg_lo:hg_hi], lower_bounds[layer])
        _, _, o_x = hgrn2_bidir(q_x, v_x, dirs_x, s_f, s_b)
        x = x + mod_x[2] * mixer_output(zx, o_x, g_x, *mix_params)
        hx2 = modulate(rmsnorm(x, norm2_g[layer]), mod_x[3], mod_x[4])
        if last:
            ff_x = moe_ffn(hx2.reshape(B * L, D), router_w, router_b,
                           moe_w_gate[layer], moe_w_up[layer], moe_w_down[layer])
        else:
            ctx = ctx + mod_c[2] * mixer_output(zc, o_c, g_c, *mix_params)
            hc2 = modulate(rmsnorm(ctx, norm2_g[layer]), mod_c[3], mod_c[4])
            ff = moe_ffn(jnp.concatenate([hc2.reshape(B * n_ctx, D), hx2.reshape(B * L, D)], axis=0),
                         router_w, router_b, moe_w_gate[layer], moe_w_up[layer], moe_w_down[layer])
            ctx = ctx + mod_c[5] * ff[:B * n_ctx].reshape(B, n_ctx, D)
            ff_x = ff[B * n_ctx:]
        x = x + mod_x[5] * ff_x.reshape(B, L, D)
    return rmsnorm(x, final_norm_g)


def setup_inputs(seed=0):
    out = dict(first_inputs(seed))
    for name, value in second_inputs(seed + 1).items():
        if name != "x":
            out[name + "_2"] = value
    return out


def reference(
    x, norm_g, w_in, b_forget, qn_a, kn_a, conv_w, conv_b, w_rg_a, b_rg_a, w_rg_x, b_rg_x,
    lru_lambda, qn_c, kn_c, cmp_pos, cmp_k_w1, cmp_k_w2, cmp_v_w1, cmp_v_w2, ln_v_g, w_spatial,
    b_spatial, w_branch, w_out, c_2, ctx_2, c_ctx_2, ada_w_2, ada_b_2, norm1_g_2, norm2_g_2,
    w_in_2, w_out_2, hy_conv_w_2, hy_conv_b_2, hy_filt_w1_2, hy_filt_b1_2, hy_filt_w2_2,
    hy_filt_b2_2, hy_filt_w3_2, hy_filt_freq_2, hy_bias_2, hy_norm_g_2, hg_lower_bounds_2,
    hg_norm_g_2, fn_w_2, fn_b_2, fn_norm_g_2, router_w_2, router_b_2, moe_w_gate_2, moe_w_up_2,
    moe_w_down_2, final_norm_g_2,
):
    x = first_block(
        x, norm_g, w_in, b_forget, qn_a, kn_a, conv_w, conv_b, w_rg_a, b_rg_a, w_rg_x, b_rg_x,
        lru_lambda, qn_c, kn_c, cmp_pos, cmp_k_w1, cmp_k_w2, cmp_v_w1, cmp_v_w2, ln_v_g,
        w_spatial, b_spatial, w_branch, w_out,
    )
    return second_block(
        x, c_2, ctx_2, c_ctx_2, ada_w_2, ada_b_2, norm1_g_2, norm2_g_2, w_in_2, w_out_2,
        hy_conv_w_2, hy_conv_b_2, hy_filt_w1_2, hy_filt_b1_2, hy_filt_w2_2, hy_filt_b2_2,
        hy_filt_w3_2, hy_filt_freq_2, hy_bias_2, hy_norm_g_2, hg_lower_bounds_2, hg_norm_g_2,
        fn_w_2, fn_b_2, fn_norm_g_2, router_w_2, router_b_2, moe_w_gate_2, moe_w_up_2,
        moe_w_down_2, final_norm_g_2,
    )


_drawn_inputs = setup_inputs


def setup_inputs(seed=0):
    import zlib

    import numpy as np

    out = dict(_drawn_inputs(seed))
    spreads = {}
    factors = {'qn_a': 8.0,
     'kn_a': 8.0,
     'conv_b': 4.267,
     'b_rg_a': 199.177,
     'b_rg_x': 124.938,
     'qn_c': 8.0,
     'kn_c': 8.0,
     'cmp_pos': 8.0,
     'ln_v_g': 5.621,
     'ctx_2': 91.44,
     'c_ctx_2': 21.354,
     'hy_conv_b_2': 8.0,
     'hy_filt_b1_2': 2.67,
     'hy_filt_b2_2': 4.775,
     'hy_filt_freq_2': 2.723,
     'hy_bias_2': 3.667,
     'hy_norm_g_2': 4.08,
     'hg_norm_g_2': 3.4,
     'fn_b_2': 8.0,
     'fn_norm_g_2': 2.927,
     'b_spatial': 2.687,
     'router_b_2': 3.241}
    for name, (base, spread) in spreads.items():
        noise = np.random.default_rng([zlib.crc32(name.encode()), seed]).standard_normal(out[name].shape)
        drawn = base * np.exp(spread * noise) if base else spread * noise
        out[name] = __import__('jax').numpy.asarray(drawn.astype(out[name].dtype))
    for name, factor in factors.items():
        out[name] = (out[name] * factor).astype(out[name].dtype)
    return out
```

```python
import math
from collections import deque
from contextlib import ExitStack

import numpy as np
import concourse.bass as bass
from concourse import mybir

F32 = mybir.dt.float32
U8 = mybir.dt.uint8
ALU = mybir.AluOpType
ACT = mybir.ActivationFunctionType
AX_X = mybir.AxisListType.X

P = 128
S = 256
NT = S // P
D = 1024
KT = D // P
W = 512
WT = W // P
HD = 64
NH = W // HD
EPS = 1e-6
NEG = -1e30
N_EXPERTS = 16
D_EXPERT = 512
HG_HEADS = 4
LEVELS = 7
MAGIC = 1.5 * 2.0 ** 23

_SPLITS = (W, W, W, NH, W, W, W, W, 128, 128, 128, 128, 128, 128, 3 * NH, W, W, W, W, 4 * D)
_NAMES = "qa ka va fa ga xb gb qc kcc vcc ksc vsc kwc vwc gate gc ud vd gd mg".split()
COL = dict(zip(_NAMES, np.cumsum((0,) + _SPLITS[:-1]).tolist()))
W_IN_COLS = sum(_SPLITS)

_PARAMS = [("norm_g", 8), ("qn_a", 1), ("kn_a", 1), ("qn_c", 1), ("kn_c", 1), ("conv_w", 16), ("conv_b", 4),
           ("b_rg_a", 4), ("b_rg_x", 4), ("lam", 4), ("cmp_pos", 16), ("b_forget", 1), ("cond", 16),
           ("ada_b", 48), ("norm1_g", 8), ("norm2_g", 8), ("hy_conv_w", 18), ("hy_conv_b", 6),
           ("hy_norm_g", 2), ("hg_norm_g", 4), ("fn_b", 2), ("fn_norm_g", 2), ("final_g", 8),
           ("filt_b1", 1), ("filt_b2", 1), ("filt_fr", 1), ("filt_w1", 64), ("filt_w2", 64)]
PARAM_AT = {}
_o = 0
for _n, _c in _PARAMS:
    PARAM_AT[_n] = (_o, _o + _c)
    _o += _c
N_PARAM = _o


class Program:

    def __init__(self, nc, ctx):
        self.nc, self.ctx = nc, ctx
        self.queues = {n: [] for n in ("pe", "act", "dve", "pool", "sp")}
        self.done = {n: ctx.enter_context(nc.semaphore(f"done_{n}")) for n in self.queues}
        self.count = dict.fromkeys(self.queues, 0)
        self.waited = {n: {} for n in self.queues}
        self.n_sems = 0

    def semaphore(self, name):
        return self.ctx.enter_context(self.nc.semaphore(name))

    def wait(self, eng, after):
        seen = self.waited[eng]
        need = {}
        for sem, value in after:
            if seen.get(id(sem), 0) < value:
                need[id(sem)] = (sem, max(value, need.get(id(sem), (sem, 0))[1]))
        for key, (sem, value) in need.items():
            seen[key] = value
            self.queues[eng].append(lambda e, sem=sem, value=value: e.wait_ge(sem, value))

    def op(self, eng, instruction, after=(), signal=True):
        self.wait(eng, after)
        if not signal:
            self.queues[eng].append(instruction)
            return None
        self.count[eng] += 1
        self.queues[eng].append(lambda e: instruction(e).then_inc(self.done[eng], 1))
        return (self.done[eng], self.count[eng])

    def dma(self, eng, out, in_, sem, count, after=()):
        self.wait(eng, after)
        self.queues[eng].append(lambda e: e.dma_start(out, in_).then_inc(sem, 16))
        return (sem, 16 * count)

    def now(self):
        return [(self.done[n], c) for n, c in self.count.items() if c]

    def load(self, eng, out, in_, name, after=()):
        return self.dma(eng, out, in_, self.semaphore(name), 1, after)

    def mm(self, out, lhsT, rhs, start, stop, after=(), signal=False, loose=False):
        return self.op("pe", lambda e: e.matmul(out, lhsT, rhs, start=start, stop=stop,
                                                skip_group_check=loose), after, signal)

    def transpose(self, out, in_, ident, after=(), signal=False):
        return self.op("pe", lambda e: e.transpose(out, in_, ident), after, signal)

    def act(self, out, in_, func, after=(), **kw):
        return self.op("act", lambda e: e.activation(out, in_, func, **kw), after)

    def tt(self, out, a, b, op, after=(), eng="dve"):
        return self.op(eng, lambda e: e.tensor_tensor(out, a, b, op), after)

    def ts(self, out, a, s1, s2, op0, op1=None, after=(), eng="dve"):
        if op1 is None:
            return self.op(eng, lambda e: e.tensor_scalar(out, a, s1, None, op0), after)
        return self.op(eng, lambda e: e.tensor_scalar(out, a, s1, s2, op0, op1), after)

    def stt(self, out, a, s, b, op0, op1, after=()):
        return self.op("dve", lambda e: e.scalar_tensor_tensor(out=out, in0=a, scalar=s, in1=b, op0=op0, op1=op1),
                       after)

    def copy(self, out, in_, after=(), eng="dve"):
        return self.op(eng, lambda e: e.tensor_copy(out, in_), after)

    def reduce(self, out, in_, op, after=(), negate=False):
        return self.op("dve", lambda e: e.tensor_reduce(out, in_, AX_X, op, negate=negate), after)

    def recip(self, out, in_, after=()):
        return self.op("dve", lambda e: e.reciprocal(out, in_), after)


def bcast(ap, dim, n):
    shape = list(ap.shape)
    shape.insert(dim, n)
    return ap.unsqueeze(dim).to_broadcast(shape)


def run_together(*streams):
    streams = deque(streams)
    while streams:
        stream = streams.popleft()
        try:
            next(stream)
            streams.append(stream)
        except StopIteration:
            pass


class WeightRing:

    def __init__(self, p, slots):
        self.p, self.slots, self.sems, self.uses = p, [], [], []
        self.free = deque()
        for s in slots:
            self.add(s, [])

    def add(self, slot, after):
        self.free.append((len(self.slots), after))
        self.sems.append(self.p.semaphore(f"weights_in_slot{len(self.slots)}"))
        self.slots.append(slot)
        self.uses.append(0)

    def drop(self, i):
        self.free = deque(x for x in self.free if x[0] != i)

    def load(self, src):
        i, readers = self.free.popleft()
        self.uses[i] += 1
        _, a, b = src.shape
        view = self.slots[i][:, 0:a * b].rearrange("p (a b) -> p a b", a=a)
        return view, self.p.dma("sp", view, src, self.sems[i], self.uses[i], readers), i

    def release(self, i, tok):
        self.free.append((i, [tok]))


class Banks:

    def __init__(self, tensors):
        self.free = deque((t, []) for t in tensors)

    def take(self):
        return self.free.popleft()

    def give(self, bank, *readers):
        self.free.append((bank, list(readers)))


class Arena:

    def __init__(self, tensor, size):
        self.t, self.size, self.at = tensor, size, 0

    def take(self, *dims):
        n = int(np.prod(dims))
        assert self.at + n <= self.size, (self.at + n, self.size)
        v = self.t[:, self.at:self.at + n]
        self.at += n
        if len(dims) == 2:
            v = v.rearrange("p (a b) -> p a b", a=dims[0])
        elif len(dims) == 3:
            v = v.rearrange("p (a b c) -> p a b c", a=dims[0], b=dims[1])
        elif len(dims) == 4:
            v = v.rearrange("p (a b c d) -> p a b c d", a=dims[0], b=dims[1], c=dims[2])
        return v


N_SLOTS = 3
ARENA = 35200


def build(nc, d, out, dump):
    with ExitStack() as ctx:
        p = Program(nc, ctx)

        def sb(name, shape, dt=F32):
            return ctx.enter_context(nc.sbuf_tensor(name, shape, dt))

        ring = WeightRing(p, [sb(f"slot{i}", [P, 4096]) for i in range(N_SLOTS)])
        banks = Banks([ctx.enter_context(nc.psum_tensor(f"bank{i}", [P, 512], F32)) for i in range(8)])
        arena = sb("arena", [P, ARENA])

        par = sb("par", [P, N_PARAM])
        ident = sb("ident", [P, P])
        ones = sb("ones", [P, P])
        xT = sb("xT", [P, KT, S])
        hT = sb("hT", [P, KT, S])
        rms = sb("rms", [P, 3, S])
        mods = sb("mods", [P, 48, 2])

        def par_of(name, i=0, n=1, rows=P):
            a = PARAM_AT[name][0] + i
            return par[0:rows, a:a + n]

        t_par = p.load("sp", par[:, :], d["params"], "params_in")
        t_x = p.load("sp", xT[:, :, :], d["xT"].rearrange("(k p) s -> p k s", p=P), "x_in")
        t_ident = p.load("act", ident[:, :], d["ident"], "ident_in")
        t_ones = p.op("dve", lambda e: e.memset(ones[:, :], 1.0))

        dumps = []

        def show(name, ap, after):
            if dump is None:
                return
            t = nc.dram_tensor("dump_" + name, tuple(ap.shape), F32, kind="ExternalOutput").ap()
            dump.append(("dump_" + name, tuple(ap.shape)))
            dumps.append(p.load("sp", t, ap, "s_" + name, after))

        def rsqrt(v, r, scratch, after):
            t1 = p.act(r, v, ACT.Ln, after=after)
            t2 = p.act(r, r, ACT.Exp, after=[t1], scale=-0.5)
            t3 = p.tt(scratch, v, r, ALU.mult, after=[t2])
            t4 = p.stt(scratch, scratch, -0.5, r, ALU.mult, ALU.mult, after=[t3])
            return p.stt(r, scratch, 1.5, r, ALU.add, ALU.mult, after=[t4])

        def channel_stats(src, n, sq, after, width=None):
            bank, free = banks.take()
            t = p.act(sq, src, ACT.Square, after=after)
            for k in range(n):
                t_s = p.mm(bank[:, 0:S], ones[:, :], sq[:, k, :], k == 0, k == n - 1,
                           after=[t, t_ones] + free, signal=k == n - 1)
            t1 = p.ts(rms[:, 0, :], bank[:, 0:S], 1.0 / (width or n * P), EPS, ALU.mult, ALU.add, after=[t_s])
            banks.give(bank, t1)
            return p_rms(t1)

        def p_rms(t1):
            return rsqrt(rms[:, 0, :], rms[:, 1, :], rms[:, 2, :], [t1])

        def head_norm(src, heads, dst_list, sq, ss, after, gains=None):
            a = src.shape[1]
            t1 = p.tt(sq, src, src, ALU.mult, after=after)
            n = a * heads
            v, r, scratch = ss[:, 0, 0:n], ss[:, 1, 0:n], ss[:, 2, 0:n]
            t2 = p.reduce(v, sq.rearrange("p a h d -> p (a h) d"), ALU.add, after=[t1])
            t3 = p.ts(v, v, 1.0 / HD, EPS, ALU.mult, ALU.add, after=[t2])
            t4 = rsqrt(v, r, scratch, [t3])
            rb = bcast(r.rearrange("p (a h) -> p a h", a=a), 3, HD)
            return [p.tt(dst, src, rb, ALU.mult, after=[t4]) for dst in dst_list][-1]

        def proj_tokens(h, w, c0, n, tt, after):
            bank, free = banks.take()
            k_n = w.shape[1]
            for k in range(k_n):
                t = p.mm(bank[:, 0:n], h[:, k, tt * P:(tt + 1) * P], w[:, k, c0:c0 + n], k == 0, k == k_n - 1,
                         after=after + free, signal=k == k_n - 1)
            return bank, t

        def proj_channels(h, w, c0, bank, at, after, m=P):
            k_n = w.shape[1]
            for k in range(k_n):
                t = p.mm(bank[0:m, at:at + S], w[:, k, c0:c0 + m], h[:, k, :], k == 0, k == k_n - 1,
                         after=after, signal=k == k_n - 1)
            return t

        w_in = d["w_in"].rearrange("(k p) n -> p k n", p=P)

        def token_block(h, col, evac, src=w_in, n=512):
            w, t_w, slot = ring.load(src[:, :, col:col + n])
            for tt in range(NT):
                bank, t = proj_tokens(h, w, 0, n, tt, [t_w] + t_h_of[id(h)])
                banks.give(bank, *evac(tt, bank, t))
                yield
            ring.release(slot, t)

        def channel_block(h, col, evac, src=w_in, n_tiles=4):
            w, t_w, slot = ring.load(src[:, :, col:col + n_tiles * P])
            for pair in range(n_tiles // 2):
                bank, free = banks.take()
                for u in range(2):
                    t = proj_channels(h, w, (2 * pair + u) * P, bank, u * S, [t_w] + t_h_of[id(h)] + free)
                    if u == 0:
                        yield
                banks.give(bank, *evac(pair, bank, t))
                yield
            ring.release(slot, t)

        A = Arena(arena, ARENA)
        ysT = A.take(4, WT, S)
        merged = A.take(KT, S)
        t_rstd = channel_stats(xT[:, :, :], KT, merged, [t_x])
        for k in range(KT):
            t = p.stt(hT[:, k, :], xT[:, k, :], par_of("norm_g", k), rms[:, 1, :], ALU.mult, ALU.mult,
                      after=[t_rstd, t_par])
        t_h = [t]
        t_h_of = {id(hT): t_h}

        t_pos = p.load("act", merged, d["posT"].rearrange("(k p) s -> p k s", p=P), "position_in", [t])
        t_pos = p.tt(xT[:, :, :], xT[:, :, :], merged, ALU.add, after=[t_pos])

        causal_add = A.take(2 * P)
        causal_T = A.take(P)
        cmp_add = A.take(NT, 32)
        cmp_keep = A.take(NT, 32)
        sel, copy_of = A.take(8), A.take(4)
        lnv_row = A.take(512)
        b_sp = A.take(4, P)
        wsT = A.take(8, P)
        w_rg = A.take(2, 4, P)
        w_cmp2 = A.take(2, HD)
        w_f = A.take(KT, P)
        w_gate = A.take(KT, 3 * NH)
        t_c = []
        for view, src in ((causal_add, d["causal_add"]), (causal_T, d["causal_T"]),
                          (cmp_add, d["cmp_add"]), (cmp_keep, d["cmp_keep"]), (sel, d["sel"]), (copy_of, d["copy_of"])):
            t_c.append(p.load("act", view, src, f"const{len(t_c)}_in"))
        t_lnv = p.load("act", lnv_row, d["ln_v_g"].to_broadcast([P, 512]), "ln_v_g_in")
        t_bsp = []
        for u in range(2):
            src = d["b_spatial"][u::2, :].unsqueeze(0).to_broadcast([HD, 4, P])
            t_bsp.append(p.load("act", b_sp[u * HD:(u + 1) * HD], src, f"b_spatial{u}_in"))
        t_ws = p.load("act", wsT, d["w_spatial_T"], "w_spatial_in")
        t_rgw = []
        t_rgz = p.op("pool", lambda e: e.memset(w_rg, 0.0))
        for u in range(2):
            for i, name in enumerate(("w_rg_a", "w_rg_x")):
                t_rgw.append(p.load("act", w_rg[u * HD:(u + 1) * HD, i, :, u * HD:(u + 1) * HD],
                                    d[name].rearrange("(j u) k n -> u k j n", u=2)[u], f"{name}{u}_in", [t_rgz]))
        t_cw2 = [p.load("act", w_cmp2[:, i], d[n], n + "_in") for i, n in enumerate(("cmp_k_w2", "cmp_v_w2"))]
        t_z = p.op("dve", lambda e: e.memset(w_f, 0.0))
        t_wf = [p.load("act", w_f[:, :, c:c + NH], w_in[:, :, COL["fa"]:COL["fa"] + NH], f"w_fa{c}_in", [t_z])
                for c in (0, 32, 64, 96)]
        t_wg = p.load("act", w_gate, w_in[:, :, COL["gate"]:COL["gate"] + 3 * NH], "w_gate_in")

        q_tm, k_tm, v_tm = A.take(NT, NH, HD), A.take(NT, NH, HD), A.take(NT, W)
        qaT, kaT = A.take(WT, 2, S), A.take(WT, 2, S)
        sq = A.take(NT, NH, HD)
        head_ss = A.take(3, 16)
        sched = {}

        t_zero = {id(qaT): t_ones, id(kaT): t_ones}

        def heads_to_channels(src_tm, dst, gain, after):
            for pair in range(2):
                bank, free = banks.take()
                for u in range(2):
                    for tt in range(NT):
                        i = 2 * u + tt
                        hp = 2 * pair + u
                        t = p.transpose(bank[:, i * P:(i + 1) * P], src_tm[:, tt, 2 * hp:2 * hp + 2, :].rearrange("p h d -> p (h d)"),
                                        ident[:, :], after=[after, t_ident] + free, signal=i == 3)
                src = bank[:, :].rearrange("p (a s) -> p a s", a=2)
                pairs = slice(2 * pair, 2 * pair + 2)
                if len(dst.shape) == 3:
                    t = p.ts(dst[:, pairs, :], src, gain, None, ALU.mult, after=[t, t_par])
                    banks.give(bank, t)
                else:
                    ts_ = [p.ts(dst[r, pairs, j, :], src[r], gain[r], None, ALU.mult, after=[t, t_par, t_zero[id(dst)]])
                           for j, r in enumerate((slice(0, HD), slice(HD, P)))]
                    banks.give(bank, *ts_)
                    t = ts_[1]
                yield
            sched[id(dst)] = t

        def to_tokens(dst, n=512):
            def evac(tt, bank, t):
                sched[id(dst), tt] = p.act(dst[:, tt, 0:n], bank[:, 0:n], ACT.Copy, after=[t])
                return [sched[id(dst), tt]]
            return evac

        def flat(v):
            return v.rearrange("p a h d -> p a (h d)")

        def gate_block(n, name):
            def evac(pair, bank, t):
                t = p.act(ysT[:, n, 2 * pair:2 * pair + 2, :], bank[:, :].rearrange("p (a s) -> p a s", a=2),
                          ACT.Silu, after=[t])
                sched["gate", n, pair] = t
                return [t]
            return channel_block(hT, COL[name], evac)

        class Lane:

            def __init__(self):
                self.s, self.pT, self.stat = A.take(2, S), A.take(4, P), A.take(4, 2)
                self.s_free, self.pT_free = [], []

        def attend(lane, hp, qt, q_T, k_of, v_of, acc, after, first, last, gate=None):
            n_k = (qt + 1) * P
            cols = slice(qt * P, (qt + 1) * P)
            bank, free = banks.take()
            for j in range(2):
                o = bank[:, j * S:j * S + n_k]
                t = p.mm(o, q_T[:, hp, j, cols], k_of(j)[:, 0:n_k], True, True, after=after + free, signal=j == 1)
            yield
            s = lane.s[:, :, 0:n_k]
            neg_max, total, inv = lane.stat[:, 0], lane.stat[:, 1], lane.stat[:, 2]
            mask = bcast(causal_add[:, 2 * P - n_k:2 * P], 1, 2)
            t = p.stt(s, bank[:, :].rearrange("p (j k) -> p j k", j=2)[:, :, 0:n_k], HD ** -0.5, mask,
                      ALU.mult, ALU.add, after=[t, t_c[0]] + lane.s_free)
            banks.give(bank, t)
            t = p.reduce(neg_max, s, ALU.max, after=[t], negate=True)
            t_e = [p.act(s[:, j, :], s[:, j, :], ACT.Exp, after=[t], bias=neg_max[:, j:j + 1],
                         accum_out=total[:, j:j + 1]) for j in range(2)]
            t = p.recip(inv, total, after=t_e)
            if gate is not None:
                t = p.tt(inv, inv, gate, ALU.mult, after=[t])
            t = p.tt(s, s, bcast(inv, 2, n_k), ALU.mult, after=[t])
            yield
            bank, free = banks.take()
            n_kt = qt + 1
            for i in range(2 * n_kt):
                j, kt = divmod(i, n_kt)
                t1 = p.transpose(bank[:, i * P:(i + 1) * P], s[:, j, kt * P:(kt + 1) * P], ident[:, :],
                                 after=[t] + free, signal=i == 2 * n_kt - 1)
            lane.s_free = [t1]
            pT = lane.pT[:, 0:2 * n_kt, :]
            t = p.act(pT, bank[:, 0:2 * n_kt * P].rearrange("p (a b) -> p a b", b=P), ACT.Copy,
                      after=[t1] + lane.pT_free)
            banks.give(bank, t)
            yield
            for i in range(2 * n_kt):
                j, kt = divmod(i, n_kt)
                t1 = p.mm(acc[0][j * HD:(j + 1) * HD, cols], v_of(kt, j), pT[:, i, :],
                          first and kt == 0 and qt == 0, last and kt == n_kt - 1, after=[t] + after + acc[1],
                          signal=i == 2 * n_kt - 1, loose=True)
            lane.pT_free = [t1]
            lane.last = t1

        def finish_head_pair(n, hp, acc, t):
            t = p.tt(ysT[:, n, hp, :], ysT[:, n, hp, :], acc[0][:, 0:S], ALU.mult,
                     after=[t, sched["gate", n, hp // 2]])
            banks.give(acc[0], t)
            sched["ys", n, hp] = t

        def fox_decay():
            bank, free = banks.take()
            t = proj_channels(hT, w_f, 0, bank, 0, t_wf + t_h + free)
            yield
            f, u, c = fox_f[:, 0], fox_f[:, 1], fox_f[:, 2]
            t1 = p.ts(f, bank[:, 0:S], par_of("b_forget"), None, ALU.add, after=[t, t_par])
            banks.give(bank, t1)
            t = p.stt(u, f, -1.0, f, ALU.mult, ALU.max, after=[t1])
            t = p.act(u, u, ACT.Exp, after=[t], scale=-1.0)
            t = p.act(u, u, ACT.Ln, after=[t], bias=1.0)
            t = p.stt(u, f, 0.0, u, ALU.min, ALU.subtract, after=[t])
            t = p.op("dve", lambda e: e.tensor_tensor_scan(c, ones_row, u, 0.0, ALU.mult, ALU.add),
                     after=[t, t_ones_row])
            tq = [p.op("dve", lambda e: e.memset(f, 1.0), after=[t])]
            tk = [p.op("dve", lambda e: e.memset(u, 1.0), after=[t])]
            for r in (0, HD):
                tq.append(p.ts(f[r + 32:r + HD], c[r + 32:r + HD], 8.0, None, ALU.mult, after=[t, tq[0]]))
                tk.append(p.ts(u[r:r + 32], c[r:r + 32], -8.0, None, ALU.mult, after=[t, tk[0]]))
            t_a = []
            for j, rows in enumerate((slice(HD, P), slice(0, HD))):
                own = sel[rows].rearrange("p (h j) -> p h j", j=2)[:, :, j]
                t_a.append(p.tt(qaT[rows, :, j, :], bcast(own, 2, S), bcast(f[rows], 1, WT), ALU.mult,
                                after=tq + [t_c[4]]))
                t_a.append(p.copy(kaT[rows, :, j, :], bcast(u[rows], 1, WT), after=tk))
            sched["aug"] = t_a

        ones_row = A.take(S)
        t_ones_row = p.op("dve", lambda e: e.memset(ones_row, 1.0))
        fox_f = A.take(3, S)
        lanes = [Lane(), Lane(), Lane()]

        def until(*keys):
            while not all(k in sched for k in keys):
                yield

        def fox(lane, hp):
            acc = banks.take()
            for qt in range(NT):
                yield from attend(lane, hp, qt, qaT, lambda j: kaT[:, hp, j, :],
                                  lambda kt, j: v_tm[:, kt, (2 * hp + j) * HD:(2 * hp + j + 1) * HD], acc,
                                  sched["aug"] + [sched[id(qaT)], sched[id(kaT)]]
                                  + [sched[id(v_tm), tt] for tt in range(NT)], True, True)
            finish_head_pair(0, hp, acc, lane.last)

        qc_tm, kv_tm = A.take(NT, NH, HD), A.take(NT, 4, 2, HD)
        k_dup = A.take(2, NT, 2, 2 * HD).rearrange("p a b c (d e) -> p a b c d e", d=2)
        qcT = A.take(WT, 2, S)
        t_zero[id(qcT)] = p.op("pool", lambda e: e.memset(qcT, 0.0))
        kT2 = A.take(2, 2, S)
        two_xb = A.take(WT * (3 + S))
        two = two_xb[:, 0:4 * S].rearrange("p (i g s) -> p i g s", i=2, g=2)
        blocks_cmp = A.take(2 * 16 * 30 + 2 * P)
        cmp_tm = blocks_cmp[:, 960:].rearrange("p (i n) -> p i n", i=2)
        blocks = blocks_cmp[:, 0:960].rearrange("p (i r g b) -> p i r g b", i=2, r=16, g=2)
        cmp_h = A.take(2, 2, 4, 32)
        vc, vcz = A.take(2, HD), A.take(2, 4, HD)
        kc = A.take(2, 2, HD)
        kc_n = A.take(2, 2, HD)
        kcT = A.take(2, 32)
        gates = A.take(NT, 3 * NH)
        p_c = A.take(NH, 32)
        p_cT = A.take(2, S)
        c_stat = A.take(3, NH)
        n_cmp = 15

        def gates_c():
            for tt in range(NT):
                bank, t = proj_tokens(hT, w_gate, 0, 3 * NH, tt, [t_wg] + t_h)
                t = p.act(gates[:, tt, :], bank[:, 0:3 * NH], ACT.Sigmoid, after=[t])
                sched["gates", tt] = t
                banks.give(bank, t)
                yield

        def compress():
            def evac(pair, bank, t):
                t_e = []
                for i in range(2):
                    for g in range(2):
                        src = bank[g * HD:(g + 1) * HD, i * S:(i + 1) * S]
                        t_e.append(p.act(two[0:HD, i, g, :], src, ACT.Copy, after=[t]))
                        t_e.append(p.act(two[HD:P, i, g, 0:S - 1], src[:, 1:S], ACT.Copy, after=[t]))
                sched["two"] = t_e
                return t_e
            yield from channel_block(hT, COL["kcc"], evac, n_tiles=2)
            t_b = []
            pos = bcast(par_of("cmp_pos", 0, 16), 2, n_cmp)
            for i in range(2):
                for g in range(2):
                    for first in range(2):
                        src = two[:, i, g, 16 * first:16 * first + 240].rearrange("p (b r u) -> p r b u", r=8, u=2)
                        r = slice(8 * first, 8 * first + 8)
                        t_b.append(p.tt(blocks[:, i, r, g, :], src[:, :, :, 0], pos[:, r, :], ALU.add,
                                        after=sched["two"] + [t_par]))
            sched["blocks"] = t_b
            t_z = p.op("dve", lambda e: e.memset(cmp_h, 0.0))
            for i, name in enumerate(("cmp_k_w1", "cmp_v_w1")):
                w1, t_w, slot = ring.load(d[name].rearrange("(r k) n -> k r n", k=P))
                bank, free = banks.take()
                for r in range(16):
                    t = p.mm(bank[0:30, 0:P], blocks[:, i, r, :, :].rearrange("p g b -> p (g b)"), w1[:, r, :], r == 0,
                             r == 15, after=[t_w] + t_b + free, signal=r == 15)
                ring.release(slot, t)
                yield
                t = p.act(cmp_tm[0:30, i], bank[0:30, 0:P], ACT.Silu, after=[t])
                banks.give(bank, t)
                bank, free = banks.take()
                t = p.transpose(bank[:, 0:30], cmp_tm[0:30, i], ident[0:30, 0:30], after=[t] + free, signal=True)
                yield
                t_s = [p.act(cmp_h[:, i, g, :, 0:n_cmp], bcast(bank[:, 15 * g:15 * g + 15], 1, 4), ACT.Copy,
                             after=[t, t_z]) for g in range(2)]
                banks.give(bank, *t_s)
                sched["cmp_h", i] = t_s
            bank, free = banks.take()
            for g in range(2):
                t = p.mm(bank[0:32, g * HD:(g + 1) * HD], cmp_h[:, 0, g, 0, :], w_cmp2[:, 0, :], True, True,
                         after=sched["cmp_h", 0] + sched["cmp_h", 1] + t_cw2 + free)
            for g in range(2):
                t = p.mm(bank[:, P + g * HD:P + (g + 1) * HD], cmp_h[:, 1, g, :, :].rearrange("p a b -> p (a b)"),
                         w_cmp2[:, 1, :], True, True, signal=g == 1)
            yield
            t1 = p.copy(kc[0:32, 0], bank[0:32, 0:P].rearrange("p (g d) -> p g d", g=2), after=[t])
            t2 = p.copy(vc, bank[:, P:2 * P].rearrange("p (g d) -> p g d", g=2), after=[t])
            banks.give(bank, t1, t2)
            sched["vc"] = [p.tt(vcz[:, g], bcast(vc[:, g], 1, 4), bcast(copy_of, 2, HD), ALU.mult, after=[t2, t_c[5]])
                           for g in range(2)]
            t = head_norm(kc[0:32, 0:1], 2, [kc_n[0:32, :, c, :].unsqueeze(1) for c in range(2)],
                          kc[0:32, 1:2], c40[0:32], [t1])
            bank, free = banks.take()
            for g in range(2):
                t1 = p.transpose(bank[:, g * 32:(g + 1) * 32], kc_n[0:32, g].rearrange("p c d -> p (c d)"),
                                 ident[0:32, 0:32], after=[t] + free, signal=g == 1)
            yield
            t = p.ts(kcT, bank[:, 0:64].rearrange("p (g b) -> p g b", g=2), par_of("kn_c"), None, ALU.mult, after=[t1])
            banks.give(bank, t)
            sched["kcT"] = t

        c40 = A.take(3, 16)

        def keys_to_channels():
            for kind in range(2):
                src = kv_tm[:, :, 2 * kind, :, :]
                t = head_norm(src, 2, [k_dup[:, kind, :, :, c, :] for c in range(2)],
                              flat(sq)[:, 0, 0:2 * P].rearrange("p (a h d) -> p a h d", a=2, h=2), head_ss,
                              [sched[id(kv_tm), tt] for tt in range(NT)])
                bank, free = banks.take()
                for g in range(2):
                    for tt in range(NT):
                        i = 2 * g + tt
                        t1 = p.transpose(bank[:, i * P:(i + 1) * P], k_dup[:, kind, tt, g].rearrange("p c d -> p (c d)"),
                                         ident[:, :], after=[t] + free, signal=i == 3)
                yield
                t = p.ts(kT2[:, kind], bank[:, :].rearrange("p (g s) -> p g s", g=2), par_of("kn_c"), None,
                         ALU.mult, after=[t1, t_par])
                banks.give(bank, t)
                sched["kT2", kind] = t

        def nsa_compressed_weights():
            t_p = p.op("dve", lambda e: e.memset(p_c, 0.0))
            t_done = [t_p]
            for tt in range(NT):
                bank, free = banks.take()
                for h in range(NH):
                    t = p.mm(bank[:, h * 32:(h + 1) * 32], qcT[:, h // 2, h % 2, tt * P:(tt + 1) * P],
                             kcT[:, h // 4, :], True, True, after=[sched[id(qcT)], sched["kcT"]] + free,
                             signal=h == NH - 1)
                yield
                s3 = bank[:, 0:S].rearrange("p (h b) -> p h b", b=32)
                t = p.stt(p_c, s3, HD ** -0.5, bcast(cmp_add[:, tt], 1, NH), ALU.mult, ALU.add,
                          after=[t] + t_c + t_done)
                banks.give(bank, t)
                t = p.reduce(c_stat[:, 0], p_c, ALU.max, after=[t], negate=True)
                t = p.tt(p_c, p_c, bcast(c_stat[:, 0], 2, 32), ALU.add, after=[t])
                t = p.act(p_c, p_c, ACT.Exp, after=[t])
                t = p.reduce(c_stat[:, 1], p_c, ALU.add, after=[t])
                t = p.recip(c_stat[:, 2], c_stat[:, 1], after=[t])
                t = p.tt(c_stat[:, 2], c_stat[:, 2], gates[:, tt, 0:NH], ALU.mult, after=[t, sched["gates", tt]])
                t = p.tt(p_c, p_c, bcast(c_stat[:, 2], 2, 32), ALU.mult, after=[t])
                t = p.tt(p_c, p_c, bcast(cmp_keep[:, tt], 1, NH), ALU.mult, after=[t])
                bank, free = banks.take()
                for g in range(2):
                    t1 = p.transpose(bank[:, g * P:(g + 1) * P], p_c[:, 4 * g:4 * g + 4].rearrange("p h b -> p (h b)"),
                                     ident[:, :], after=[t] + free, signal=g == 1)
                t_done = [t1]
                yield
                t = p.copy(p_cT[:, :, tt * P:(tt + 1) * P], bank[:, 0:2 * P].rearrange("p (g q) -> p g q", g=2),
                           after=[t1])
                banks.give(bank, t)
                sched["p_cT", tt] = t

        def nsa(lane, hp):
            yield from until(("p_cT", 1), ("kT2", 1))
            g = hp // 2
            acc = banks.take()
            for j in range(2):
                p.mm(acc[0][j * HD:(j + 1) * HD, 0:S], vcz[:, g, (2 * hp + j) % 4, :], p_cT[:, g, :], True, False,
                     after=acc[1] + sched["vc"] + [sched["p_cT", 0], sched["p_cT", 1]], loose=True)
            for kind in range(2):
                for qt in range(NT):
                    yield from attend(lane, hp, qt, qcT, lambda j: kT2[:, kind, g, :],
                                      lambda kt, j: kv_tm[:, kt, 2 * kind + 1, g, :], acc,
                                      [sched[id(qcT)], sched["kT2", kind]]
                                      + [sched[id(kv_tm), tt] for tt in range(NT)],
                                      False, kind == 1,
                                      gate=gates[:, qt, (1 + kind) * NH + 2 * hp:(1 + kind) * NH + 2 * hp + 2])
            finish_head_pair(2, hp, acc, lane.last)

        xb = two_xb.rearrange("p (a s) -> p a s", a=WT)
        def as_tiles(v):
            return v.rearrange("p a h d -> p (a h d)").rearrange("p (a s) -> p a s", a=WT)
        xc, la, lr, li = as_tiles(q_tm), as_tiles(k_tm), merged[:, 0:4, :], merged[:, 4:8, :]
        sp4 = A.take(3, 4)

        def lru_softplus():
            u, s, acc_ = sp4[:, 0], sp4[:, 1], sp4[:, 2]
            lam = par_of("lam", 0, 4)
            t = p.stt(s, lam, -1.0, lam, ALU.mult, ALU.max, after=[t_par])
            t = p.act(u, s, ACT.Exp, after=[t], scale=-1.0)
            t = p.ts(s, u, 2.0, None, ALU.add, after=[t])
            t = p.recip(s, s, after=[t])
            t = p.tt(u, u, s, ALU.mult, after=[t])
            t = p.tt(s, u, u, ALU.mult, after=[t])
            t = p.ts(acc_, s, 1 / 15, 1 / 13, ALU.mult, ALU.add, after=[t])
            for c in (1 / 11, 1 / 9, 1 / 7, 1 / 5, 1 / 3, 1.0):
                t = p.tt(acc_, acc_, s, ALU.mult, after=[t])
                t = p.ts(acc_, acc_, c, None, ALU.add, after=[t])
            t = p.stt(acc_, acc_, 8.0, u, ALU.mult, ALU.mult, after=[t])
            t = p.ts(s, lam, -1.0, 0.0, ALU.mult, ALU.max, after=[t])
            t = p.stt(u, s, 4.0, acc_, ALU.mult, ALU.add, after=[t])
            sched["sp4"] = t

        def lru():
            t_z = p.op("dve", lambda e: e.memset(xb[:, :, 0:3], 0.0), after=sched["blocks"])

            def evac(pair, bank, t):
                t = p.act(xb[:, 2 * pair:2 * pair + 2, 3:3 + S], bank[:, :].rearrange("p (a s) -> p a s", a=2),
                          ACT.Copy, after=[t] + sched["blocks"])
                sched["xb", pair] = t
                return [t]
            yield from channel_block(hT, COL["xb"], evac)
            t_x = [t_z, sched["xb", 0], sched["xb", 1], t_par]
            t_c4 = []
            for j in range(WT):
                t = p.ts(xc[:, j, :], xb[:, j, 0:S], par_of("conv_w", j), par_of("conv_b", j), ALU.mult, ALU.add,
                         after=t_x + [sched[id(qaT)]])
                for tap in range(1, 4):
                    t = p.stt(xc[:, j, :], xb[:, j, tap:tap + S], par_of("conv_w", 4 * tap + j), xc[:, j, :],
                              ALU.mult, ALU.add, after=[t])
                t_c4.append(t)
            t_g = []
            for i, (dst, b) in enumerate(((lr, "b_rg_a"), (li, "b_rg_x"))):
                for j in range(WT):
                    bank, free = banks.take()
                    t = p.mm(bank[:, 0:S], w_rg[:, i, j, :], xc[:, j, :], True, True,
                             after=t_rgw + [t_c4[j]] + free, signal=True)
                    yield
                    t = p.act(dst[:, j, :], bank[:, 0:S], ACT.Sigmoid, after=[t], bias=par_of(b, j))
                    banks.give(bank, t)
                    t_g.append(t)
            t_t = [p.act(lr[:, j, :], lr[:, j, :], ACT.Tanh, after=t_g + [sched["sp4"]], scale=sp4[:, 0, j:j + 1])
                   for j in range(WT)]
            yield
            t1 = p.ts(la, lr, 1.0, None, ALU.add, after=t_t + [sched[id(kaT)]])
            t1 = p.recip(la, la, after=[t1])
            yield
            t2 = p.act(lr, lr, ACT.Sqrt, after=t_t + [t1])
            t = p.tt(li, li, xc, ALU.mult, after=t_g)
            t = p.tt(li, li, la, ALU.mult, after=[t, t1])
            yield
            t = p.stt(li, lr, 2.0, li, ALU.mult, ALU.mult, after=[t, t2])
            t1 = p.ts(la, la, 2.0, -1.0, ALU.mult, ALU.add, after=[t])
            yield
            for j in range(WT):
                t = p.op("dve", lambda e, j=j: e.tensor_tensor_scan(xc[:, j, :], la[:, j, :], li[:, j, :], 0.0,
                                                                   ALU.mult, ALU.add), after=[t1, t])
            t = p.tt(ysT[:, 1], ysT[:, 1], xc, ALU.mult, after=[t, sched["gate", 1, 0], sched["gate", 1, 1]])
            for j in range(WT):
                sched["ys", 1, j] = t

        uT = k_dup.rearrange("p a b c d e -> p (a b c d e)").rearrange("p (a s) -> p a s", a=WT)
        vd = flat(qc_tm)
        bn = A.take(NT, 12)

        def spatial():
            t_m = p.tt(wsT, wsT, bcast(causal_T, 1, 8), ALU.mult, after=[t_ws, t_c[1]])

            def evac_u(pair, bank, t):
                sched["u", pair] = p.act(uT[:, 2 * pair:2 * pair + 2, :], bank[:, :].rearrange("p (a s) -> p a s", a=2),
                                         ACT.Gelu, after=[t, sched["kT2", 0], sched["kT2", 1]])
                return [sched["u", pair]]

            def evac_v(tt, bank, t):
                sched["v", tt] = p.act(vd[:, tt, :], bank[:, :], ACT.Gelu, after=[t, sched[id(qcT)]])
                return [sched["v", tt]]
            yield from channel_block(hT, COL["ud"], evac_u)
            yield from token_block(hT, COL["vd"], evac_v)
            t_n = []
            for tt in range(NT):
                st, mv = bn[:, tt, 0:6], bn[:, tt, 6:8]
                t = p.op("dve", lambda e, tt=tt, st=st: e.bn_stats(st, vd[:, tt, :]), after=[sched["v", tt]])
                t = p.op("dve", lambda e, st=st, mv=mv: e.bn_aggr(mv, st), after=[t])
                t = p.ts(bn[:, tt, 8:9], bn[:, tt, 7:8], EPS, None, ALU.add, after=[t])
                t = rsqrt(bn[:, tt, 8:9], bn[:, tt, 9:10], bn[:, tt, 10:11], [t])
                t = p.ts(vd[:, tt, :], vd[:, tt, :], bn[:, tt, 6:7], bn[:, tt, 9:10], ALU.subtract, ALU.mult, after=[t])
                t_n.append(p.tt(vd[:, tt, :], vd[:, tt, :], lnv_row, ALU.mult, after=[t, t_lnv]))
            yield
            for j in range(WT):
                bank, free = banks.take()
                for tt in range(NT):
                    for u in range(2):
                        g = 2 * j + u
                        t = p.mm(bank[u * HD:(u + 1) * HD, tt * P:(tt + 1) * P], vd[:, tt, g * HD:(g + 1) * HD],
                                 wsT[:, g, :], True, True, after=[t_m] + t_n + free,
                                 signal=tt == NT - 1 and u == 1)
                yield
                t1 = p.tt(uT[:, j, :], uT[:, j, :], ysT[:, 3, j, :], ALU.mult,
                          after=[sched["u", j // 2], sched["gate", 3, j // 2]])
                t = p.tt(ysT[:, 3, j, :].rearrange("p (a t) -> p a t", a=NT),
                         bank[:, 0:S].rearrange("p (a t) -> p a t", a=NT), bcast(b_sp[:, j], 1, NT), ALU.add,
                         after=[t, t1] + t_bsp)
                banks.give(bank, t)
                sched["ys", 3, j] = p.tt(ysT[:, 3, j, :], ysT[:, 3, j, :], uT[:, j, :], ALU.mult, after=[t])

        ada_row = blocks_cmp[:, 0:1024].rearrange("p (a n) -> p a n", a=2)

        def ada():
            cond = par_of("cond", 0, 16).rearrange("p (k c) -> p k c", c=2)
            t_s = p.act(cond, cond, ACT.Silu, after=[t_par])
            t_row = [[], []]
            ada_w = d["ada_w"].rearrange("(k p) n -> p k n", p=P)
            for c in range(12):
                w, t_w, slot = ring.load(ada_w[:, :, c * 512:(c + 1) * 512])
                bank, free = banks.take()
                for k in range(KT):
                    t = p.mm(bank[0:2, :], cond[:, k, :], w[:, k, :], k == 0, k == KT - 1, after=[t_w, t_s] + free,
                             signal=k == KT - 1)
                ring.release(slot, t)
                yield
                row = ada_row[0:2, c % 2]
                t = p.copy(row, bank[0:2, :], after=[t] + t_row[c % 2])
                banks.give(bank, t)
                bank, free = banks.take()
                for i in range(4):
                    t1 = p.transpose(bank[:, 2 * i:2 * i + 2], row[:, i * P:(i + 1) * P], ident[0:2, 0:2],
                                     after=[t, t_ident] + free, signal=i == 3)
                t_row[c % 2] = [t1]
                t = p.tt(mods[:, 4 * c:4 * c + 4, :], bank[:, 0:8].rearrange("p (a c) -> p a c", c=2),
                         bcast(par_of("ada_b", 4 * c, 4), 2, 2), ALU.add, after=[t1])
                banks.give(bank, t)
                sched["mods", c] = t
                yield

        def chain(*streams):
            for s_ in streams:
                yield from s_

        def qk_fox():
            for src, dst, g in ((q_tm, qaT, "qn_a"), (k_tm, kaT, "kn_a")):
                t = head_norm(src, NH, [src], sq, head_ss, [sched[id(src), tt] for tt in range(NT)])
                yield
                yield from heads_to_channels(src, dst, par_of(g), t)

        def q_nsa():
            t = head_norm(qc_tm, NH, [qc_tm], sq, head_ss, [sched[id(qc_tm), tt] for tt in range(NT)])
            yield
            yield from heads_to_channels(qc_tm, qcT, par_of("qn_c"), t)

        def tokens_of(dst, name, n=512):
            def evac(tt, bank, t):
                target = dst[:, tt]
                if len(target.shape) == 3:
                    target = target.rearrange("p a b -> p (a b)")
                elif len(target.shape) == 4:
                    target = target.rearrange("p a b c -> p (a b c)")
                sched[id(dst), tt] = p.act(target, bank[:, 0:n], ACT.Copy, after=[t])
                return [sched[id(dst), tt]]
            return token_block(hT, COL[name], evac)

        for _ in chain(tokens_of(q_tm, "qa"), tokens_of(k_tm, "ka"), tokens_of(v_tm, "va"), fox_decay()):
            pass
        run_together(chain(gate_block(0, "ga"), gates_c(), tokens_of(qc_tm, "qc"), tokens_of(kv_tm, "ksc"), gate_block(1, "gb")),
                     qk_fox())
        lru_softplus()
        run_together(chain(gate_block(2, "gc"), gate_block(3, "gd")), q_nsa(), keys_to_channels())
        jobs = deque([(fox, hp) for hp in range(WT)] + [(nsa, hp) for hp in range(WT)])

        def work(lane):
            while jobs:
                job, hp = jobs.popleft()
                yield from job(lane, hp)

        modulations = ada()
        run_together(chain(compress(), nsa_compressed_weights(), lru(), spatial(), modulations), *map(work, lanes))
        for n in range(4):
            show(f"ys{n}", ysT[:, n], [sched["ys", n, j] for j in range(WT)])

        B = Arena(arena, ARENA)
        cat, qk_set0 = B.take(KT, S), B.take(2, HG_HEADS, S)
        scratch8 = B.take(KT, S)
        KF = B.take(2, 2, 2 * 256)
        s_ctx = B.take(2, HG_HEADS, P)
        m_tmp = [(B.take(2, S), []), (B.take(2, S), [])]
        gs = B.take(KT, 2)
        zero = B.take(1)
        ones2 = B.take(S)
        x_region = B.at
        w_in2 = d["w_in_2"].rearrange("(k p) n -> p k n", p=P)
        HY, HG, FN = 0, 768, 3328
        t_zero1 = [None]

        def modulated_norm(src, dst, which, gain, part, sq, after):
            t_r = channel_stats(src, KT, sq, after)
            t = p.ts(gs[:, :, which], mods[:, 8 * (part + 1):8 * (part + 2), which], 1.0, None, ALU.add,
                     after=[sched["mods", c] for c in range(12)] + [t_r])
            t = p.tt(gs[:, :, which], gs[:, :, which], par_of(gain, 0, KT), ALU.mult, after=[t])
            ts_ = []
            for k in range(KT):
                t1 = p.stt(dst[:, k, :], src[:, k, :], gs[:, k, which:which + 1], rms[:, 1, :], ALU.mult, ALU.mult,
                           after=[t])
                ts_.append(p.act(dst[:, k, :], dst[:, k, :], ACT.Identity, after=[t1],
                                 bias=mods[:, 8 * part + k, which:which + 1]))
            return ts_

        def context():
            C = Arena(arena, ARENA)
            C.at = x_region
            ctxT, hc = C.take(KT, S), C.take(KT, S)
            f, e = C.take(2 * HG_HEADS, S), C.take(2 * HG_HEADS, S)
            v = C.take(NT, W)
            ke = ctxT.rearrange("p k s -> p (k s)").rearrange("p (t n) -> p t n", t=NT)
            start = p.now()
            t_ctx = p.load("act", ctxT, d["ctxT"].rearrange("(k p) s -> p k s", p=P), "ctx_in", start)
            yield
            while ("mods", 11) not in sched:
                yield
            t_hc = modulated_norm(ctxT, hc, 1, "norm1_g", 0, hc, [t_ctx])
            t_h_of[id(hc)] = t_hc
            yield

            def evac_f(direction):
                def evac(pair, bank, t):
                    a = 4 * direction + 2 * pair
                    t = p.act(f[:, a:a + 2, :], bank[:, :].rearrange("p (a s) -> p a s", a=2), ACT.Sigmoid, after=[t] + start)
                    sched["cf", direction, pair] = t
                    return [t]
                return evac

            def evac_v(tt, bank, t):
                sched["cv", tt] = p.act(v[:, tt, :], bank[:, :], ACT.Copy, after=[t] + start)
                return [sched["cv", tt]]
            t_e1 = p.op("dve", lambda e_: e_.memset(e[:, 0:4, S - 1:S], 1.0), after=start)
            t_e1 = p.op("dve", lambda e_: e_.memset(e[:, 4:8, 0:1], 1.0))
            for direction in range(2):
                yield from channel_block(hc, HG + 512 * (1 + direction), evac_f(direction), src=w_in2)
                for h in range(HG_HEADS):
                    a = 4 * direction + h
                    if direction == 0:
                        o, i_ = e[:, a, S - 2::-1], f[:, a, S - 1:0:-1]
                    else:
                        o, i_ = e[:, a, 1:S], f[:, a, 0:S - 1]
                    t = p.op("dve", lambda e_, o=o, i_=i_: e_.tensor_tensor_scan(
                        o, i_, zero.to_broadcast([P, S - 1]), 1.0, ALU.mult, ALU.add),
                        after=[sched["cf", direction, h // 2], t_e1, t_zero1[0]])
                a = slice(4 * direction, 4 * direction + 4)
                t = p.tt(f[:, a, :], f[:, a, :], e[:, a, :], ALU.mult, after=[t])
                t = p.tt(e[:, a, :], e[:, a, :], f[:, a, :], ALU.subtract, after=[t])
                yield
                for tt in range(NT):
                    bank, free = banks.take()
                    for h in range(HG_HEADS):
                        t1 = p.transpose(bank[:, h * P:(h + 1) * P], e[:, 4 * direction + h, tt * P:(tt + 1) * P],
                                         ident[:, :], after=[t] + free, signal=h == 3)
                    t2 = p.act(ke[:, tt, 512 * direction:512 * direction + 512], bank[:, :], ACT.Copy, after=[t1] + t_hc)
                    banks.give(bank, t2)
                    sched["ke", direction, tt] = t2
                    yield
            yield from token_block(hc, HG + 512 * 3, evac_v, src=w_in2)
            for direction in range(2):
                bank, free = banks.take()
                for h in range(HG_HEADS):
                    for tt in range(NT):
                        n = 512 * direction + h * P
                        t = p.mm(bank[:, h * P:(h + 1) * P], ke[:, tt, n:n + P], v[:, tt, h * P:(h + 1) * P],
                                 tt == 0, tt == NT - 1,
                                 after=free + [sched["ke", direction, tt], sched["cv", tt]],
                                 signal=h == 3 and tt == NT - 1)
                yield
                t = p.act(s_ctx[:, direction], bank[:, :].rearrange("p (h v) -> p h v", h=HG_HEADS), ACT.Copy,
                          after=[t])
                banks.give(bank, t)
                sched["s_ctx", direction] = t
            sched["ctx_done"] = [t]

        X = Arena(arena, ARENA)
        X.at = x_region
        cosF, sinF = X.take(NT, 256), X.take(NT, 256)
        icos, isin = X.take(2, S), X.take(2, S)
        cosL, sinL = X.take(NT, S), X.take(NT, S)
        csC = X.take(2, P)
        fn_w = X.take(2, P)
        xh_region = X.at
        decay = X.take(NT, 256)
        embT, h1, h2, red = X.take(S), X.take(S), X.take(S), X.take(S)
        w3 = X.take(1024)
        skip = X.take(512)
        hfb = X.take(2, 256)
        plus, minus = X.take(NT, 2, 256), X.take(NT, 2, 256)

        def filters():
            start = p.now()
            t_f = {n: p.load("act", v, src, n + "_in", start) for n, v, src in (
                ("cosF", cosF, d["cosF"]), ("sinF", sinF, d["sinF"]), ("icos", icos, d["icos"]),
                ("isin", isin, d["isin"]), ("cosL", cosL, d["cosL"]), ("sinL", sinL, d["sinL"]),
                ("csC", csC, d["csC"]), ("decay", decay, d["decay"]), ("embT", embT[0:33], d["embT"]),
                ("w3", w3[0:HD], d["filt_w3"]), ("skip", skip[0:1], d["hy_bias"]))}
            t_z = p.op("pool", lambda e: e.memset(fn_w, 0.0), after=start)
            sched["fn_w"] = [p.load("act", fn_w[u * HD:(u + 1) * HD, :, u * HD:(u + 1) * HD],
                                    d["fn_w"].rearrange("(j u) k n -> u k j n", u=2)[u], f"fn_w{u}_in", [t_z])
                             for u in range(2)]
            sched["dft"] = [t_f[n] for n in ("cosF", "sinF", "icos", "isin")]
            sched["dftL"] = [t_f[n] for n in ("cosL", "sinL", "csC")]
            yield
            t_in, rhs = [t_f["embT"]], embT[0:33]
            for layer, (w, b, out_) in enumerate((("filt_w1", "filt_b1", h1), ("filt_w2", "filt_b2", h2))):
                rows = 33 if layer == 0 else HD
                bank, free = banks.take()
                t = p.mm(bank[0:HD, 0:S], par_of(w, 0, HD, rows), rhs, True, True, after=t_in + [t_par] + free,
                         signal=True)
                yield
                o, r = out_[0:HD], red[0:HD]
                t = p.ts(o, bank[0:HD, 0:S], par_of(b, rows=HD), par_of("filt_fr", rows=HD), ALU.add, ALU.mult,
                         after=[t] + start)
                banks.give(bank, t)
                t = p.ts(r, o, 1 / (2 * math.pi), MAGIC, ALU.mult, ALU.add, after=[t])
                t = p.ts(r, r, MAGIC, None, ALU.subtract, after=[t])
                t = p.stt(o, r, -6.28125, o, ALU.mult, ALU.add, after=[t])
                t = p.stt(o, r, -(2 * math.pi - 6.28125), o, ALU.mult, ALU.add, after=[t])
                t = p.ts(o, o, 3.1415925, -3.1415925, ALU.min, ALU.max, after=[t])
                t = p.act(o, o, ACT.Sin, after=[t])
                t_in, rhs = [t], o
            t_pm = []
            t_used = list(start)
            for tt in range(NT):
                for o in range(2):
                    bank, free = banks.take()
                    t = p.mm(bank[:, :], h2[0:HD, tt * P:(tt + 1) * P], w3[0:HD, 512 * o:512 * o + 512], True, True,
                             after=t_in + [t_f["w3"]] + free, signal=True)
                    yield
                    t = p.tt(hfb, bank[:, :].rearrange("p (d c) -> p d c", d=2), bcast(decay[:, tt, :], 1, 2), ALU.mult,
                             after=[t, t_f["decay"]] + t_used)
                    banks.give(bank, t)
                    if tt == 0:
                        t1 = p.op("dve", lambda e: e.memset(hfb[0:1, 1, :], 0.0), after=[t])
                        t = p.tt(hfb[0:1, 0, :], hfb[0:1, 0, :], skip[0:1, 256 * o:256 * o + 256], ALU.add,
                                 after=[t, t1, t_f["skip"]])
                    t1 = p.tt(plus[:, tt, o, :], hfb[:, 0, :], hfb[:, 1, :], ALU.add, after=[t] + start)
                    t2 = p.tt(minus[:, tt, o, :], hfb[:, 0, :], hfb[:, 1, :], ALU.subtract, after=[t])
                    t_used = [t1, t2]
                    t_pm += t_used
            for ft in range(2):
                for ri, (mat, taps) in enumerate(((cosF, plus), (sinF, minus))):
                    bank, free = banks.take()
                    for tt in range(NT):
                        t = p.mm(bank[:, :], mat[:, tt, ft * P:(ft + 1) * P],
                                 taps[:, tt].rearrange("p o c -> p (o c)"), tt == 0, tt == NT - 1,
                                 after=t_pm + sched["dft"] + free, signal=tt == NT - 1)
                    yield
                    t = p.act(KF[:, ft, ri, :], bank[:, :], ACT.Copy, after=[t])
                    banks.give(bank, t)
                    sched["KF", ft, ri] = t
            sched["filters_done"] = [sched["KF", ft, ri] for ft in range(2) for ri in range(2)]

        def merge():
            t_m = {}
            step = 0
            for n in range(4):
                t_y = [sched["ys", n, j] for j in range(WT)]
                wb, t_wb, slot_b = ring.load(d["w_branch"][n].rearrange("(k p) n -> p k n", p=P))
                for half in range(2):
                    col = COL["mg"] + n * D + half * 512
                    wm, t_wm, slot_m = ring.load(w_in[:, :, col:col + 512])
                    for i in range(4):
                        dt = 4 * half + i
                        bank, free = banks.take()
                        proj_channels(hT, wm, i * P, bank, 0, [t_wm] + free)
                        for k in range(WT):
                            t = p.mm(bank[:, S:2 * S], wb[:, k, dt * P:(dt + 1) * P], ysT[:, n, k, :], k == 0,
                                     k == WT - 1, after=[t_wb] + t_y, signal=k == WT - 1)
                        tmp, tmp_free = m_tmp[step % 2]
                        t1 = p.act(tmp[:, 0, :], bank[:, 0:S], ACT.Sigmoid, after=[t] + t_all + tmp_free)
                        if n == 0:
                            t2 = p.tt(merged[:, dt, :], tmp[:, 0, :], bank[:, S:2 * S], ALU.mult, after=[t1])
                            m_tmp[step % 2] = (tmp, [t2])
                            banks.give(bank, t2)
                        else:
                            t2 = p.tt(tmp[:, 1, :], tmp[:, 0, :], bank[:, S:2 * S], ALU.mult, after=[t1])
                            banks.give(bank, t2)
                            t2 = p.tt(merged[:, dt, :], merged[:, dt, :], tmp[:, 1, :], ALU.add, after=[t2, t_m[dt]])
                            m_tmp[step % 2] = (tmp, [t2])
                        t_m[dt] = t2
                        step += 1
                        yield
                    ring.release(slot_m, t)
                ring.release(slot_b, t)
            sched["merged"] = list(t_m.values())
        t_all = p.now()
        t_zero1[0] = p.op("dve", lambda e: e.memset(zero, 0.0), after=t_all)
        for n in range(3):
            ring.add(arena[:, ARENA - 4096 * (n + 1):ARENA - 4096 * n], t_all)
        run_together(merge(), chain(context(), filters()))
        t_res = []
        w_out = d["w_out"].rearrange("(k p) n -> p k n", p=P)
        for half in range(2):
            w, t_w, slot = ring.load(w_out[:, :, half * 512:(half + 1) * 512])
            for i in range(4):
                bank, free = banks.take()
                t = proj_channels(merged, w, i * P, bank, 0, [t_w] + sched["merged"] + free)
                dt = 4 * half + i
                t1 = p.tt(xT[:, dt, :], xT[:, dt, :], bank[:, 0:S], ALU.add, after=[t])
                banks.give(bank, t1)
                t_res.append(t1)
            ring.release(slot, t)
        show("x1", xT[:, :, :], t_res)
        t_h_of[id(hT)] = modulated_norm(xT[:, :, :], hT, 0, "norm1_g", 0, scratch8, t_res)
        start2 = p.now()
        for n in range(3):
            ring.drop(N_SLOTS + n)

        X.at = xh_region
        z_hy = X.take(6, S + 2)
        u_hy = X.take(6, S)
        v_tok, x1_tok = X.take(NT, 256), X.take(NT, 256)
        Uf, Yf = X.take(2, 2, 256), X.take(2, 2, 256)
        prod = X.take(2, 2, 256)
        z_fn = X.take(2, S)
        f1 = X.take(NT, 2, 256)
        y_fn = X.take(2, S)
        hg_region = X.at
        Y = Arena(arena, ARENA)
        Y.at = hg_region
        q_hg = Y.take(HG_HEADS, S)
        pq = [Y.take(HG_HEADS, S) for _ in range(2)]
        pk = [Y.take(HG_HEADS, S) for _ in range(2)]
        k_hg = [Y.take(HG_HEADS, S) for _ in range(2)]
        v_hg = Y.take(NT, W)
        qk_set1 = Y.take(2, HG_HEADS, S)
        masks = Y.take(8 * P // 4).bitcast(U8).rearrange("p (l t) -> p l t", l=8)
        sc = scratch8.rearrange("p k s -> p (k s)").rearrange("p (c h t) -> p c h t", c=4, h=HG_HEADS)

        def channel_norm(src, n, dst, gain, sq, r3, after):
            bank, free = banks.take()
            t = p.act(sq, src, ACT.Square, after=after)
            for k in range(n):
                t1 = p.mm(bank[:, 0:S], ones[:, :], sq[:, k, :], k == 0, k == n - 1, after=[t] + free,
                          signal=k == n - 1)
            t = p.ts(r3[0], bank[:, 0:S], 1.0 / (n * P), EPS, ALU.mult, ALU.add, after=[t1])
            banks.give(bank, t)
            t = rsqrt(r3[0], r3[1], r3[2], [t])
            return [p.stt(dst[:, k, :], src[:, k, :], par_of(gain, k), r3[1], ALU.mult, ALU.mult, after=[t])
                    for k in range(n)]

        def hyena_z():
            t_z = [p.op("pool", lambda e, c=c: e.memset(z_hy[:, :, c:c + 1], 0.0), after=start2) for c in (0, S + 1)]

            def evac(base):
                def f(pair, bank, t):
                    a = base + 2 * pair
                    t = p.act(z_hy[:, a:a + 2, 1:S + 1], bank[:, :].rearrange("p (a s) -> p a s", a=2), ACT.Copy,
                              after=[t] + start2)
                    sched["z", a // 2] = t
                    return [t]
                return f
            yield from channel_block(hT, HY, evac(0), src=w_in2)
            yield from channel_block(hT, HY + 512, evac(4), src=w_in2, n_tiles=2)
            for j in range(6):
                t = p.ts(u_hy[:, j, :], z_hy[:, j, 0:S], par_of("hy_conv_w", j), par_of("hy_conv_b", j), ALU.mult,
                         ALU.add, after=t_z + [sched["z", j // 2]])
                for tap in (1, 2):
                    t = p.stt(u_hy[:, j, :], z_hy[:, j, tap:tap + S], par_of("hy_conv_w", 6 * tap + j), u_hy[:, j, :],
                              ALU.mult, ALU.add, after=[t])
                sched["u_hy", j] = t

        def hyena():
            for n, dst in enumerate((v_tok, x1_tok)):
                bank, free = banks.take()
                for tt in range(NT):
                    for j in range(2):
                        t = p.transpose(bank[:, (2 * tt + j) * P:(2 * tt + j + 1) * P],
                                        u_hy[:, 2 * n + j, tt * P:(tt + 1) * P], ident[:, :],
                                        after=[sched["u_hy", 2 * n + j]] + free, signal=tt == 1 and j == 1)
                t = p.act(dst, bank[:, :].rearrange("p (t c) -> p t c", t=NT), ACT.Copy, after=[t] + start2)
                banks.give(bank, t)
                sched["tok", n] = t
                yield
            t_in = [sched["tok", 0]]
            t_pr = list(start2)
            for o in range(2):
                t_y = []
                for ft in range(2):
                    bank, free = banks.take()
                    for ri, mat in enumerate((cosF, sinF)):
                        for tt in range(NT):
                            t = p.mm(bank[:, ri * 256:(ri + 1) * 256], mat[:, tt, ft * P:(ft + 1) * P], v_tok[:, tt, :],
                                     tt == 0, tt == NT - 1, after=t_in + sched["dft"] + free,
                                     signal=ri == 1 and tt == 1)
                    yield
                    u2 = bank[:, :].rearrange("p (r c) -> p r c", r=2)
                    oc = slice(256 * o, 256 * o + 256)
                    a, b = prod[:, 0], prod[:, 1]
                    t1 = p.tt(a, u2, bcast(KF[:, ft, 0, oc], 1, 2), ALU.mult, after=[t] + t_pr + sched["filters_done"])
                    t2 = p.tt(b, u2, bcast(KF[:, ft, 1, oc], 1, 2), ALU.mult, after=[t])
                    banks.give(bank, t1, t2)
                    t1 = p.tt(Yf[:, ft, 0], a[:, 0], b[:, 1], ALU.subtract, after=[t1, t2] + t_in)
                    t2 = p.tt(Yf[:, ft, 1], a[:, 1], b[:, 0], ALU.add, after=[t2])
                    t_pr = [t1, t2]
                    t_y += t_pr
                if o == 0:
                    bank, free = banks.take()
                    for tt in range(NT):
                        for n in range(4):
                            ft, ri = divmod(n, 2)
                            t = p.mm(bank[:, tt * 256:(tt + 1) * 256], (icos, isin)[ri][:, ft, tt * P:(tt + 1) * P],
                                     Yf[:, ft, ri, :], n == 0, n == 3, after=t_y + free, signal=tt == 1 and n == 3)
                    yield
                    t = p.tt(v_tok, x1_tok, bank[:, :].rearrange("p (t c) -> p t c", t=NT), ALU.mult,
                             after=[t, sched["tok", 1]])
                    banks.give(bank, t)
                    t_in = [t]
                else:
                    bank, free = banks.take()
                    for j in range(2):
                        for n in range(4):
                            ft, ri = divmod(n, 2)
                            t = p.mm(bank[:, j * S:(j + 1) * S], Yf[:, ft, ri, j * P:(j + 1) * P],
                                     (icos, isin)[ri][:, ft, :], n == 0, n == 3, after=t_y + free,
                                     signal=j == 1 and n == 3)
                    yield
                    y = u_hy[:, 4:6, :]
                    t = p.tt(y, y, bank[:, :].rearrange("p (j s) -> p j s", j=2), ALU.mult,
                             after=[t, sched["u_hy", 4], sched["u_hy", 5]])
                    banks.give(bank, t)
                    yield
                    sched["cat_hy"] = channel_norm(y, 2, cat[:, 0:2, :], "hy_norm_g", u_hy[:, 0:2, :],
                                                   (u_hy[:, 2, :], u_hy[:, 3, :], prod[:, 0, 0]), [t])

        def fourier():
            def evac(pair, bank, t):
                t = p.act(z_fn, bank[:, :].rearrange("p (a s) -> p a s", a=2), ACT.Copy, after=[t] + start2)
                sched["z_fn"] = t
                return [t]
            yield from channel_block(hT, FN, evac, src=w_in2, n_tiles=2)
            t_f1 = []
            for tt in range(NT):
                bank, free = banks.take()
                o = bank[:, :].rearrange("p (c j n) -> p c j n", c=2, j=2)
                for j in range(2):
                    t = p.mm(o[:, :, j, :], z_fn[:, j, tt * P:(tt + 1) * P], csC, True, True,
                             after=[sched["z_fn"]] + sched["dftL"] + free, signal=j == 1)
                yield
                t = p.act(f1[:, tt], bank[:, :].rearrange("p (c n) -> p c n", c=2), ACT.Copy, after=[t] + start2)
                banks.give(bank, t)
                t_f1.append(t)
            bank, free = banks.take()
            for j in range(2):
                for n in range(4):
                    tt, cs = divmod(n, 2)
                    t = p.mm(bank[:, j * S:(j + 1) * S], f1[:, tt, cs, j * P:(j + 1) * P], (cosL, sinL)[cs][:, tt, :],
                             n == 0, n == 3, after=t_f1 + free, signal=j == 1 and n == 3)
            yield
            t = p.act(y_fn, bank[:, :].rearrange("p (j s) -> p j s", j=2), ACT.Copy, after=[t] + start2)
            banks.give(bank, t)
            bank, free = banks.take()
            for j in range(2):
                t1 = p.mm(bank[:, j * S:(j + 1) * S], fn_w[:, j, :], y_fn[:, j, :], True, True,
                          after=[t] + sched["fn_w"] + free, signal=j == 1)
            yield
            t = [p.act(z_fn[:, j, :], bank[:, j * S:(j + 1) * S], ACT.Identity, after=[t1], bias=par_of("fn_b", j))
                 for j in range(2)]
            banks.give(bank, *t)
            yield
            sched["cat_fn"] = channel_norm(z_fn, 2, cat[:, 6:8, :], "fn_norm_g", y_fn,
                                           (f1[:, 0, 0], f1[:, 0, 1], f1[:, 1, 0]), t)

        def hgrn_z():
            wide = qk_set1.rearrange("p a h s -> p (a h s)")[:, 0:8 * P].rearrange("p (l t) -> p l t", l=8)
            t = p.load("act", wide, d["masks"], "masks_in", start2)
            sched["masks"] = p.copy(masks, wide, after=[t], eng="pool")
            base_q, base_f, base_v, base_g = HG, HG + 512, HG + 1536, HG + 2048

            def evac_to(dst, func, key):
                def evac(pair, bank, t):
                    t = p.act(dst[:, 2 * pair:2 * pair + 2, :], bank[:, :].rearrange("p (a s) -> p a s", a=2), func,
                              after=[t] + start2)
                    sched[key, pair] = t
                    return [t]
                return evac
            for i in range(2):
                yield from channel_block(hT, base_f + 512 * i, evac_to(pq[i], ACT.Sigmoid, ("f", i)), src=w_in2)
            yield from channel_block(hT, base_q, evac_to(q_hg, ACT.Silu, "q"), src=w_in2)
            for i in range(2):
                sched["k", i] = p.ts(k_hg[i], pq[i], -1.0, 1.0, ALU.mult, ALU.add,
                                     after=[sched[("f", i), 0], sched[("f", i), 1]])
                sched["pk", i] = p.op("pool", lambda e, i=i: e.memset(pk[i], 1.0), after=start2)
            sched["q_hg"] = p.ts(q_hg, q_hg, P ** -0.5, None, ALU.mult, after=[sched["q", 0], sched["q", 1]])

        def hgrn_vg():
            def evac_v(tt, bank, t):
                sched["v_hg", tt] = p.act(v_hg[:, tt, :], bank[:, :], ACT.Copy, after=[t] + start2)
                return [sched["v_hg", tt]]

            def evac_g(pair, bank, t):
                t = p.act(cat[:, 2 + 2 * pair:4 + 2 * pair, :], bank[:, :].rearrange("p (a s) -> p a s", a=2),
                          ACT.Silu, after=[t] + start2)
                sched["g_hg", pair] = t
                return [t]
            yield from token_block(hT, HG + 1536, evac_v, src=w_in2)
            yield from channel_block(hT, HG + 2048, evac_g, src=w_in2)

        def hgrn_scores():
            sets = [[qk_set0, []], [qk_set1, [sched["masks"]]]]
            step = 0

            def products(qv, kv, level_mask, tiles, after):
                for c, s_tile, t_tile in tiles:
                    bank, free = banks.take()
                    for h in range(HG_HEADS):
                        t = p.mm(bank[:, h * P:(h + 1) * P], kv[:, h, s_tile * P:(s_tile + 1) * P],
                                 qv[:, h, t_tile * P:(t_tile + 1) * P], True, True, after=after + free, signal=h == 3)
                    src = bank[:, :].rearrange("p (h t) -> p h t", h=HG_HEADS)
                    dst = sc[:, c]
                    if level_mask is None:
                        t1 = p.act(dst, src, ACT.Copy, after=[t] + start2)
                    else:
                        mask = bcast(masks[:, level_mask, :], 1, HG_HEADS)
                        t1 = p.op("dve", lambda e, dst=dst, mask=mask, src=src: e.copy_predicated(dst, mask, src),
                                  after=[t, sched["masks"], sched["sc", c]])
                    sched["sc", c] = t1
                    banks.give(bank, t1)
                return t

            set_, used = sets[0]
            t = p.tt(set_[:, 1], k_hg[0], k_hg[1], ALU.add, after=[sched["k", 0], sched["k", 1]] + start2)
            t = products(q_hg, set_[:, 1], None, ((0, 0, 0), (1, 1, 1)), [t, sched["q_hg"]])
            sets[0][1] = [t]
            yield
            state = [[sched["k", i], sched["pk", i], sched["q_hg"]] for i in range(2)]
            for level in range(LEVELS + 1):
                m = 2 ** level
                n_blocks = HG_HEADS * S // (2 * m)
                set_, used = sets[(level + 1) % 2]
                t_set = []
                for i in range(2):
                    hi, lo = (1, 0) if i == 0 else (0, 1)
                    edge = m - 1 if i == 0 else 0
                    eng = "dve" if i == 0 else "pool"

                    def halves(v):
                        return v.rearrange("p h s -> p (h s)").rearrange("p (b u m) -> p b u m", u=2, m=m)
                    t_q = p.tt(halves(set_[:, 0])[:, :, hi, :], halves(q_hg)[:, :, hi, :], halves(pq[i])[:, :, hi, :],
                               ALU.mult, after=state[i] + used + start2)
                    t_k = p.tt(halves(set_[:, 1])[:, :, lo, :], halves(k_hg[i])[:, :, lo, :],
                               halves(pk[i])[:, :, lo, :], ALU.mult, after=state[i] + used)
                    t_set += [t_q, t_k]
                    a, b = halves(pq[i]), halves(pk[i])
                    e_hi = a[:, :, hi, edge:edge + 1].to_broadcast([P, n_blocks, m])
                    e_lo = a[:, :, lo, edge:edge + 1].to_broadcast([P, n_blocks, m])
                    t_b = p.tt(b[:, :, lo, :], b[:, :, lo, :], e_hi, ALU.mult, after=[t_q, t_k], eng=eng)
                    t_a = p.tt(a[:, :, hi, :], a[:, :, hi, :], e_lo, ALU.mult, after=[t_q, t_k, t_b], eng=eng)
                    state[i] = [t_a, t_b]
                if level < LEVELS:
                    t = products(set_[:, 0], set_[:, 1], 1 + level, ((0, 0, 0), (1, 1, 1)), t_set)
                else:
                    t = products(set_[:, 0], set_[:, 1], None, ((2, 0, 1), (3, 1, 0)), t_set)
                sets[(level + 1) % 2][1] = [t]
                yield
            yield from until(("v_hg", 1), ("g_hg", 1))
            t_s = []
            for i in range(2):
                set_, used = sets[i]
                t_s.append(p.tt(set_[:, 0], q_hg, pq[i], ALU.mult, after=state[i] + used))
            yield
            out_banks = []
            for pair in range(2):
                bank, free = banks.take()
                for u in range(2):
                    h = 2 * pair + u
                    o = bank[:, u * S:(u + 1) * S]
                    for i in range(2):
                        p.mm(o, s_ctx[:, i, h, :], sets[i][0][:, 0, h, :], i == 0, False, loose=True,
                             after=t_s + free + [sched["s_ctx", 0], sched["s_ctx", 1]])
                    for n, (c, s_tile, t_tile) in enumerate(((0, 0, 0), (3, 1, 0), (2, 0, 1), (1, 1, 1))):
                        t = p.mm(o[:, t_tile * P:(t_tile + 1) * P], v_hg[:, s_tile, h * P:(h + 1) * P], sc[:, c, h, :],
                                 False, n == 3, loose=True, signal=u == 1 and n == 3,
                                 after=[sched["sc", k] for k in range(4)] + [sched["v_hg", k] for k in range(NT)])
                out_banks.append((bank, t))
            yield
            sq_, (v3, r3) = k_hg[0], (k_hg[1], pk[0])
            t_v = []
            for pair, (bank, t) in enumerate(out_banks):
                t = p.act(sq_[:, 2 * pair:2 * pair + 2, :], bank[:, :].rearrange("p (a s) -> p a s", a=2), ACT.Square,
                          after=[t])
                b2, free = banks.take()
                for u in range(2):
                    t1 = p.mm(b2[:, u * S:(u + 1) * S], ones[:, :], sq_[:, 2 * pair + u, :], True, True,
                              after=[t] + free, signal=u == 1)
                t1 = p.ts(v3[:, 2 * pair:2 * pair + 2, :], b2[:, :].rearrange("p (a s) -> p a s", a=2), 1.0 / P, EPS,
                          ALU.mult, ALU.add, after=[t1])
                banks.give(b2, t1)
                t_v.append(t1)
            yield
            t = rsqrt(v3, r3, pk[1], t_v)
            sched["cat_hg"] = []
            for h in range(HG_HEADS):
                bank, _ = out_banks[h // 2]
                t1 = p.stt(r3[:, h, :], bank[:, (h % 2) * S:(h % 2 + 1) * S], par_of("hg_norm_g", h), r3[:, h, :],
                           ALU.mult, ALU.mult, after=[t])
                if h % 2:
                    banks.give(bank, t1)
                sched["cat_hg"].append(p.tt(cat[:, 2 + h, :], cat[:, 2 + h, :], r3[:, h, :], ALU.mult,
                                            after=[t1, sched["g_hg", h // 2]]))

        run_together(hgrn_z())
        run_together(hgrn_scores(), chain(hgrn_vg(), hyena_z(), fourier()), chain(until(("u_hy", 5)), hyena()))
        show("cat", cat, sched["cat_hy"] + sched["cat_hg"] + sched["cat_fn"])

        t_res2 = []
        w_out2 = d["w_out_2"].rearrange("(k p) n -> p k n", p=P)
        for half in range(2):
            w, t_w, slot = ring.load(w_out2[:, :, half * 512:(half + 1) * 512])
            for i in range(4):
                dt = 4 * half + i
                bank, free = banks.take()
                t = proj_channels(cat, w, i * P, bank, 0, [t_w] + free + sched["cat_hy"] + sched["cat_hg"] + sched["cat_fn"])
                t1 = p.stt(xT[:, dt, :], bank[:, 0:S], mods[:, 16 + dt, 0:1], xT[:, dt, :], ALU.mult, ALU.add, after=[t])
                banks.give(bank, t1)
                t_res2.append(t1)
            ring.release(slot, t)
        show("x2", xT[:, :, :], t_res2)

        t_h2 = modulated_norm(xT[:, :, :], hT, 0, "norm2_g", 3, scratch8, t_res2)
        start3 = p.now()
        M = Arena(arena, ARENA)
        r_w = M.take(KT, 16)
        weigh = M.take(20)
        r_b = M.take(16)
        logit, prob, pick, tmp16, oh1, oh2 = (M.take(NT, 16) for _ in range(6))
        pairs6, grp, grp2, grp3 = M.take(8, 6), M.take(8), M.take(8), M.take(8)
        one2 = M.take(4, 2)
        combT = M.take(S)
        M.take(4)
        h_moe, s_moe = M.take(4, S), M.take(4, S)
        combine = M.take(N_EXPERTS, S)
        zeros = M.take(640)
        extra = [M.take(4096) for _ in range(3)]
        t_rw = p.load("act", r_w, d["router_w"].rearrange("(k p) e -> p k e", p=P), "router_w_in", start3)
        t_rb = p.load("act", r_b, d["router_b"].to_broadcast([P, 16]), "router_b_in", start3)
        t_wei = p.load("act", weigh, d["weigh"].to_broadcast([P, 20]), "weigh_in", start3)
        t_zm = p.op("pool", lambda e: e.memset(zeros, 0.0), after=start3)

        bank, free = banks.take()
        for tt in range(NT):
            for k in range(KT):
                t = p.mm(bank[:, tt * 16:(tt + 1) * 16], hT[:, k, tt * P:(tt + 1) * P], r_w[:, k, :], k == 0, k == KT - 1,
                         after=[t_rw] + t_h2 + free, signal=tt == 1 and k == KT - 1)
        lg = bank[:, 0:32].rearrange("p (t e) -> p t e", t=NT)
        neg_max, total = one2[:, 0], one2[:, 1]
        t1 = p.reduce(neg_max, lg, ALU.max, after=[t] + start3, negate=True)
        t = p.tt(logit, lg, bcast(neg_max, 2, 16), ALU.add, after=[t1])
        banks.give(bank, t)
        t = p.act(prob, logit, ACT.Exp, after=[t])
        t = p.reduce(total, prob, ALU.add, after=[t])
        t = p.recip(total, total, after=[t])
        t = p.tt(prob, prob, bcast(total, 2, 16), ALU.mult, after=[t])
        t = p.tt(pick, prob, bcast(r_b, 1, NT), ALU.add, after=[t, t_rb])
        g4 = pick.rearrange("p t e -> p (t e)").rearrange("p (g e) -> p g e", e=4)
        t1 = p.tt(pairs6[:, :, 0:3], g4[:, :, 0:3], g4[:, :, 1:4], ALU.add, after=[t])
        t2 = p.tt(pairs6[:, :, 3:5], g4[:, :, 0:2], g4[:, :, 2:4], ALU.add, after=[t])
        t3 = p.tt(pairs6[:, :, 5:6], g4[:, :, 0:1], g4[:, :, 3:4], ALU.add, after=[t])
        t = p.reduce(grp, pairs6, ALU.max, after=[t1, t2, t3])

        def first_max(dst, src, n, weights, best, after):
            t = p.reduce(best, src, ALU.max, after=after)
            t = p.tt(dst, src, bcast(best, 2, n), ALU.is_equal, after=[t])
            t = p.tt(dst, dst, bcast(weights, 1, NT), ALU.mult, after=[t, t_wei])
            t = p.reduce(best, dst, ALU.max, after=[t])
            return p.tt(dst, dst, bcast(best, 2, n), ALU.is_equal, after=[t])

        t = first_max(grp2.rearrange("p (t g) -> p t g", t=NT), grp.rearrange("p (t g) -> p t g", t=NT), 4,
                      weigh[:, 16:20], one2[:, 2], [t])
        t1 = p.ts(grp3, grp2, 1.0, 1e30, ALU.subtract, ALU.mult, after=[t])
        t = p.tt(g4, g4, bcast(grp2, 2, 4), ALU.mult, after=[t])
        t = p.tt(g4, g4, bcast(grp3, 2, 4), ALU.add, after=[t, t1])
        t1 = first_max(oh1, pick, 16, weigh[:, 0:16], one2[:, 2], [t])
        t = p.stt(tmp16, oh1, -2e30, pick, ALU.mult, ALU.add, after=[t1])
        t = first_max(oh2, tmp16, 16, weigh[:, 0:16], one2[:, 3], [t])
        t = p.tt(oh1, oh1, oh2, ALU.add, after=[t])
        t = p.tt(oh1, oh1, prob, ALU.mult, after=[t])
        t = p.reduce(total, oh1, ALU.add, after=[t])
        t = p.recip(total, total, after=[t])
        t = p.tt(oh1, oh1, bcast(total, 2, 16), ALU.mult, after=[t])
        show("comb", oh1, [t])
        bank, free = banks.take()
        for tt in range(NT):
            t1 = p.transpose(bank[0:16, tt * P:(tt + 1) * P], oh1[:, tt, :], ident[:, :], after=[t] + free,
                             signal=tt == 1)
        t = p.copy(combT[0:16], bank[0:16, 0:S], after=[t1])
        banks.give(bank, t)
        t_comb = []
        for pair in range(N_EXPERTS // 2):
            bank, free = banks.take()
            for u in range(2):
                e = 2 * pair + u
                t1 = p.mm(bank[:, u * S:(u + 1) * S], ident[0:16, e:e + 1].to_broadcast([16, P]), combT[0:16], True, True,
                          after=[t] + free, signal=u == 1)
            t2 = p.act(combine[:, 2 * pair:2 * pair + 2, :], bank[:, :].rearrange("p (a s) -> p a s", a=2), ACT.Copy,
                       after=[t1])
            banks.give(bank, t2)
            t_comb.append(t2)

        before = p.now()
        all_banks = [banks.take()[0] for _ in range(8)]
        acc_banks, gu_banks = all_banks[0:4], all_banks[4:8]
        moe_slots = [s[:, :] for s in ring.slots[0:3]] + extra
        moe_loaded = [p.semaphore(f"moe_weights_in_slot{s}") for s in range(6)]
        moe_gu, moe_silu, moe_prod, moe_hidden, moe_down = (
            p.semaphore("moe_" + n) for n in ("gate_up_done", "silu_done", "product_done", "hidden_done", "down_done"))
        rounds = N_EXPERTS // 2
        wg = d["moe_w_gate"].rearrange("e (k p) n -> p (e k) n", p=P)
        wu = d["moe_w_up"].rearrange("e (k p) n -> p (e k) n", p=P)
        wd = d["moe_w_down"].rearrange("e (k p) n -> p (e k) n", p=P)
        loads = [(wg, 8), (wu, 8), (wd, 4)]
        views = [[moe_slots[3 * u + i].rearrange("p (k n) -> p k n", k=loads[i][1]) for i in range(3)] for u in range(2)]
        p.wait("pe", before + t_h2)
        p.wait("act", before)
        p.wait("dve", before + t_comb)
        slot_readers = dict(ring.free)
        for u in range(2):
            for i, (src, tiles) in enumerate(loads):
                p.dma("sp", views[u][i], src[:, u * tiles:(u + 1) * tiles], moe_loaded[3 * u + i], 1,
                      start3 if 3 * u + i >= 3 else slot_readers[3 * u + i])

        def sp_loop(e):
            with e.Fori(0, rounds - 1) as r:
                for u in range(2):
                    for i, (src, tiles) in enumerate(loads):
                        if i == 0:
                            e.wait_ge(moe_gu, 8 * r + (4 * u + 4))
                        if i == 2:
                            e.wait_ge(moe_down, 2 * r + (u + 1))
                        e.dma_start(views[u][i], src[:, bass.ds(2 * tiles * r + (2 + u) * tiles, tiles)])\
                            .then_inc(moe_loaded[3 * u + i], 16)

        def pe_loop(e):
            for b in acc_banks:
                e.matmul(b[:, :], zeros[:, 0:P], zeros[:, P:P + 512], start=True, stop=False, skip_group_check=True)
            with e.Fori(0, rounds) as r:
                for u in range(2):
                    w_g, w_u, w_d = views[u]
                    e.wait_ge(moe_loaded[3 * u], 16 * r + 16)
                    e.wait_ge(moe_loaded[3 * u + 1], 16 * r + 16)
                    for ft in range(4):
                        e.wait_ge(moe_hidden, 8 * r + (4 * u + ft + 1))
                        for half, w in enumerate((w_g, w_u)):
                            for k in range(KT):
                                mm = e.matmul(gu_banks[ft][:, half * S:(half + 1) * S], w[:, k, ft * P:(ft + 1) * P],
                                              hT[:, k, :], start=k == 0, stop=k == KT - 1)
                        mm.then_inc(moe_gu, 1)
                    e.wait_ge(moe_loaded[3 * u + 2], 16 * r + 16)
                    for ft in range(4):
                        e.wait_ge(moe_hidden, 8 * r + (4 * u + ft + 5))
                        for dt in range(KT):
                            mm = e.matmul(acc_banks[dt // 2][:, dt % 2 * S:(dt % 2 + 1) * S],
                                          w_d[:, ft, dt * P:(dt + 1) * P], h_moe[:, ft, :], start=False, stop=False,
                                          skip_group_check=True)
                    mm.then_inc(moe_down, 1)
            for b in acc_banks:
                e.matmul(b[:, :], zeros[:, 0:P], zeros[:, P:P + 512], start=False, stop=True, skip_group_check=True)\
                    .then_inc(moe_down, 1)

        def act_loop(e):
            with e.Fori(0, rounds) as r:
                for u in range(2):
                    for ft in range(4):
                        e.wait_ge(moe_gu, 8 * r + (4 * u + ft + 1))
                        e.wait_ge(moe_hidden, 8 * r + (4 * u + ft + 1))
                        e.activation(s_moe[:, ft, :], gu_banks[ft][:, 0:S], ACT.Silu).then_inc(moe_silu, 1)

        def dve_loop(e):
            with e.Fori(0, rounds) as r:
                for u in range(2):
                    for ft in range(4):
                        e.wait_ge(moe_silu, 8 * r + (4 * u + ft + 1))
                        e.tensor_tensor(s_moe[:, ft, :], s_moe[:, ft, :], gu_banks[ft][:, S:2 * S], ALU.mult)\
                            .then_inc(moe_prod, 1)
                        e.wait_ge(moe_prod, 8 * r + (4 * u + ft + 1))
                        e.tensor_tensor(h_moe[:, ft, :].unsqueeze(1), s_moe[:, ft, :].unsqueeze(1),
                                        combine[:, bass.ds(2 * r + u, 1), :], ALU.mult).then_inc(moe_hidden, 1)

        p.queues["dve"].append(lambda e: e.memset(s_moe[:, 0, 0:1], 0.0).then_inc(moe_hidden, 4))
        for name, loop in (("sp", sp_loop), ("pe", pe_loop), ("act", act_loop), ("dve", dve_loop)):
            p.queues[name].append(loop)
        t_moe = [(moe_down, N_EXPERTS + 4)]

        t_res3 = [p.stt(xT[:, dt, :], acc_banks[dt // 2][:, dt % 2 * S:(dt % 2 + 1) * S], mods[:, 40 + dt, 0:1],
                        xT[:, dt, :], ALU.mult, ALU.add, after=t_moe) for dt in range(KT)]
        for b in all_banks:
            banks.give(b, t_res3[-1])
        t_r = channel_stats(xT[:, :, :], KT, combine[:, 0:8, :], t_res3)
        s_out = p.semaphore("out_written")
        out_v = out.rearrange("(k p) s -> p k s", p=P)
        for k in range(KT):
            t = p.stt(xT[:, k, :], xT[:, k, :], par_of("final_g", k), rms[:, 1, :], ALU.mult, ALU.mult, after=[t_r])
            if k % 2:
                t_o = p.dma("sp", out_v[:, k - 1:k + 1, :], xT[:, k - 1:k + 1, :], s_out, (k + 1) // 2, [t])
        p.wait("sp", [t_o] + dumps)

        block = ctx.enter_context(nc.Block())
        for name, where in (("sp", block.sync), ("pe", block.tensor), ("act", block.scalar), ("dve", block.vector),
                            ("pool", block.gpsimd)):
            def play(e, name=name):
                for instruction in p.queues[name]:
                    instruction(e)
            where(play)


def shape_constants():
    f = np.float32
    q = np.arange(P)
    c = {"ident": np.eye(P, dtype=f)}
    upper = np.where(q[None, :] > q[:, None], NEG, 0.0)
    c["causal_add"] = np.concatenate([np.zeros((P, P)), upper], axis=1).astype(f)
    c["causal_T"] = (q[:, None] <= q[None, :]).astype(f)
    t = np.arange(S).reshape(NT, P).T[:, :, None]
    b = np.arange(32)[None, None, :]
    ok = (b < 15) & (16 * b + 31 <= t)
    c["cmp_add"] = np.where(ok, 0.0, NEG).astype(f)
    c["cmp_keep"] = ok.astype(f)
    c["sel"] = (q[:, None] % 32 == np.arange(NH)[None, :]).astype(f)
    c["copy_of"] = (q[:, None] // 32 == np.arange(4)[None, :]).astype(f)
    d4 = D // 4
    omega = 1.0 / (10000.0 ** (np.arange(d4) / d4))
    ar, ac = (np.arange(S) // 64)[:, None] * omega, (np.arange(S) % 64)[:, None] * omega
    c["posT"] = np.concatenate([np.sin(ar), np.cos(ar), np.sin(ac), np.cos(ac)], axis=1).T.astype(f)
    tf = 2 * np.pi / (2 * S) * np.outer(np.arange(S), np.arange(256) + 0.5)

    def by_tiles(m):
        return np.ascontiguousarray(m.reshape(-1, P, m.shape[1]).transpose(1, 0, 2)).astype(f)
    c["cosF"], c["sinF"] = by_tiles(np.cos(tf)), by_tiles(-np.sin(tf))
    c["icos"], c["isin"] = by_tiles(np.cos(tf).T / 256), by_tiles(-np.sin(tf).T / 256)
    tk = 2 * np.pi / S * np.outer(np.arange(S), np.arange(S))
    c["cosL"], c["sinL"] = by_tiles(np.cos(tk) / 128), by_tiles(-np.sin(tk) / 128)
    cd = 2 * np.pi / HD * np.outer(np.arange(HD), np.arange(HD))
    c["csC"] = np.stack([np.kron(np.eye(2), np.cos(cd)), np.kron(np.eye(2), np.sin(cd))], axis=1).astype(f)
    pos = np.linspace(0.0, 1.0, S)[:, None]
    w = 2 * np.pi * np.arange(S)[:, None] / S
    bands = np.linspace(1e-4, 15, 16)[None, :]
    c["embT"] = np.concatenate([pos, np.cos(bands * w), -np.sin(bands * w)], axis=1).T.astype(f)
    deltas = np.linspace(math.log(1e-2) / 1.5, math.log(1e-2) / 0.3, 256)
    c["decay"] = by_tiles(np.exp(-pos * np.abs(deltas)[None, :]))
    masks = [np.eye(P, dtype=bool)]
    s_, t_ = q[:, None], q[None, :]
    for level in range(LEVELS):
        m = 2 ** level
        masks.append((s_ // (2 * m) == t_ // (2 * m)) & (s_ // m % 2 != t_ // m % 2))
    c["masks"] = np.stack(masks, axis=1).astype(f)
    c["weigh"] = np.concatenate([16.0 - np.arange(16), 4.0 - np.arange(4)])[None].astype(f)
    return c


def pack_params(i):
    out = np.zeros((P, N_PARAM), np.float32)

    def put(name, cols, rows=slice(0, P)):
        a, b = PARAM_AT[name]
        out[rows, a:b] = cols

    def tiles(v):
        return np.reshape(v, (-1, P)).T
    lo, hi = slice(0, HD), slice(HD, P)
    for name in ("norm_g", "conv_b", "b_rg_a", "b_rg_x"):
        put(name, tiles(i[name]))
    put("lam", tiles(i["lru_lambda"]))
    for name in ("qn_a", "kn_a", "qn_c", "kn_c"):
        for rows in (lo, hi):
            put(name, np.reshape(i[name], (HD, 1)), rows)
    put("conv_w", tiles(i["conv_w"]))
    for half, rows in enumerate((lo, hi)):
        put("cmp_pos", i["cmp_pos"][0][half::2].T, rows)
    for r in range(0, P, 32):
        put("b_forget", np.reshape(i["b_forget"], (NH, 1)), slice(r, r + NH))
    put("cond", np.stack([tiles(i["c_2"]), tiles(i["c_ctx_2"])], axis=2).reshape(P, 16))
    for name, src in (("ada_b", "ada_b_2"), ("norm1_g", "norm1_g_2"), ("norm2_g", "norm2_g_2"),
                      ("hy_conv_w", "hy_conv_w_2"), ("hy_conv_b", "hy_conv_b_2"), ("hy_norm_g", "hy_norm_g_2"),
                      ("hg_norm_g", "hg_norm_g_2"), ("fn_b", "fn_b_2"), ("fn_norm_g", "fn_norm_g_2"),
                      ("final_g", "final_norm_g_2")):
        put(name, tiles(i[src]))
    for name, src in (("filt_b1", "hy_filt_b1_2"), ("filt_b2", "hy_filt_b2_2"), ("filt_fr", "hy_filt_freq_2")):
        put(name, np.reshape(i[src], (HD, 1)), lo)
    put("filt_w1", i["hy_filt_w1_2"][0], slice(0, 33))
    put("filt_w2", i["hy_filt_w2_2"][0], lo)
    return out


DEBUG = False


def kernel(**inputs):
    import concourse.bacc as bacc
    from concourse.bass_utils import run_bass_kernel_spmd

    i = {k: np.asarray(v) for k, v in inputs.items()}
    arrays = dict(shape_constants())
    arrays["params"] = pack_params(i)
    arrays["xT"] = np.ascontiguousarray(i["x"][0].T)
    for name in ("w_in", "w_branch", "w_out", "w_rg_a", "w_rg_x", "cmp_k_w1", "cmp_k_w2", "cmp_v_w1", "cmp_v_w2", "b_spatial"):
        arrays[name] = i[name][0]
    arrays["ln_v_g"] = i["ln_v_g"]
    arrays["ctxT"] = np.ascontiguousarray(i["ctx_2"][0].T)
    for name, src in (("ada_w", "ada_w_2"), ("w_in_2", "w_in_2"), ("w_out_2", "w_out_2"), ("filt_w3", "hy_filt_w3_2"),
                      ("fn_w", "fn_w_2"), ("moe_w_gate", "moe_w_gate_2"), ("moe_w_up", "moe_w_up_2"),
                      ("moe_w_down", "moe_w_down_2")):
        arrays[name] = i[src][0]
    arrays["hy_bias"] = i["hy_bias_2"].reshape(1, 512)
    arrays["router_w"], arrays["router_b"] = i["router_w_2"], i["router_b_2"][None]
    arrays["w_spatial_T"] = np.ascontiguousarray(i["w_spatial"][0].transpose(2, 0, 1))
    nc = bacc.Bacc("TRN2", target_bir_lowering=False, num_devices=1)
    d = {n: nc.dram_tensor("in_" + n, a.shape, mybir.dt.from_np(a.dtype), kind="ExternalInput").ap()
         for n, a in arrays.items()}
    out = nc.dram_tensor("out", (D, S), F32, kind="ExternalOutput").ap()
    dump = [] if DEBUG else None
    build(nc, d, out, dump)
    r = run_bass_kernel_spmd(nc, [{"in_" + n: a for n, a in arrays.items()}], core_ids=[0]).results[0]
    y = np.ascontiguousarray(r["out"].T)[None]
    if DEBUG:
        return (y,) + tuple(r[n] for n, _ in dump)
    return y
```

```python
import math
from collections import deque
from contextlib import ExitStack

import numpy as np
import concourse.bass as bass
from concourse import mybir

F32 = mybir.dt.float32
F32R = mybir.dt.float32r
U8 = mybir.dt.uint8
ALU = mybir.AluOpType
ACT = mybir.ActivationFunctionType
AX_X = mybir.AxisListType.X

P = 128
S = 256
NT = S // P
D = 1024
KT = D // P
W = 512
WT = W // P
HD = 64
NH = W // HD
EPS = 1e-6
NEG = -1e30
N_EXPERTS = 16
D_EXPERT = 512
HG_HEADS = 4
LEVELS = 7
MAGIC = 1.5 * 2.0 ** 23

_SPLITS = (W, W, W, NH, W, W, W, W, 128, 128, 128, 128, 128, 128, 3 * NH, W, W, W, W, 4 * D)
_NAMES = "qa ka va fa ga xb gb qc kcc vcc ksc vsc kwc vwc gate gc ud vd gd mg".split()
COL = dict(zip(_NAMES, np.cumsum((0,) + _SPLITS[:-1]).tolist()))
W_IN_COLS = sum(_SPLITS)

_PARAMS = [("norm_g", 8), ("qn_a", 1), ("kn_a", 1), ("qn_c", 1), ("kn_c", 1), ("conv_w", 16), ("conv_b", 4),
           ("b_rg_a", 4), ("b_rg_x", 4), ("lam", 4), ("cmp_pos", 16), ("b_forget", 1), ("cond", 16),
           ("ada_b", 48), ("norm1_g", 8), ("norm2_g", 8), ("hy_conv_w", 18), ("hy_conv_b", 6),
           ("hy_norm_g", 2), ("hg_norm_g", 4), ("fn_b", 2), ("fn_norm_g", 2), ("final_g", 8),
           ("filt_b1", 1), ("filt_b2", 1), ("filt_fr", 1), ("filt_w1", 64), ("filt_w2", 64)]
PARAM_AT = {}
_o = 0
for _n, _c in _PARAMS:
    PARAM_AT[_n] = (_o, _o + _c)
    _o += _c
N_PARAM = _o


class Program:

    def __init__(self, nc, ctx):
        self.nc, self.ctx = nc, ctx
        self.queues = {n: [] for n in ("pe", "act", "dve", "pool", "sp")}
        self.done = {n: ctx.enter_context(nc.semaphore(f"done_{n}")) for n in self.queues}
        self.count = dict.fromkeys(self.queues, 0)
        self.waited = {n: {} for n in self.queues}
        self.n_sems = 0

    def semaphore(self, name):
        return self.ctx.enter_context(self.nc.semaphore(name))

    def wait(self, eng, after):
        seen = self.waited[eng]
        need = {}
        for sem, value in after:
            if seen.get(id(sem), 0) < value:
                need[id(sem)] = (sem, max(value, need.get(id(sem), (sem, 0))[1]))
        for key, (sem, value) in need.items():
            seen[key] = value
            self.queues[eng].append(lambda e, sem=sem, value=value: e.wait_ge(sem, value))

    def op(self, eng, instruction, after=(), signal=True):
        self.wait(eng, after)
        if not signal:
            self.queues[eng].append(instruction)
            return None
        self.count[eng] += 1
        self.queues[eng].append(lambda e: instruction(e).then_inc(self.done[eng], 1))
        return (self.done[eng], self.count[eng])

    def dma(self, eng, out, in_, sem, count, after=()):
        self.wait(eng, after)
        self.queues[eng].append(lambda e: e.dma_start(out, in_).then_inc(sem, 16))
        return (sem, 16 * count)

    def now(self):
        return [(self.done[n], c) for n, c in self.count.items() if c]

    def load(self, eng, out, in_, name, after=()):
        return self.dma(eng, out, in_, self.semaphore(name), 1, after)

    def mm(self, out, lhsT, rhs, start, stop, after=(), signal=False, loose=False):
        return self.op("pe", lambda e: e.matmul(out, lhsT, rhs, start=start, stop=stop,
                                                skip_group_check=loose), after, signal)

    def transpose(self, out, in_, ident, after=(), signal=False):
        return self.op("pe", lambda e: e.transpose(out, in_, ident), after, signal)

    def act(self, out, in_, func, after=(), **kw):
        return self.op("act", lambda e: e.activation(out, in_, func, **kw), after)

    def tt(self, out, a, b, op, after=(), eng="dve"):
        return self.op(eng, lambda e: e.tensor_tensor(out, a, b, op), after)

    def ts(self, out, a, s1, s2, op0, op1=None, after=(), eng="dve"):
        if op1 is None:
            return self.op(eng, lambda e: e.tensor_scalar(out, a, s1, None, op0), after)
        return self.op(eng, lambda e: e.tensor_scalar(out, a, s1, s2, op0, op1), after)

    def stt(self, out, a, s, b, op0, op1, after=()):
        return self.op("dve", lambda e: e.scalar_tensor_tensor(out=out, in0=a, scalar=s, in1=b, op0=op0, op1=op1),
                       after)

    def copy(self, out, in_, after=(), eng="dve"):
        return self.op(eng, lambda e: e.tensor_copy(out, in_), after)

    def reduce(self, out, in_, op, after=(), negate=False):
        return self.op("dve", lambda e: e.tensor_reduce(out, in_, AX_X, op, negate=negate), after)

    def recip(self, out, in_, after=()):
        return self.op("dve", lambda e: e.reciprocal(out, in_), after)


def bcast(ap, dim, n):
    shape = list(ap.shape)
    shape.insert(dim, n)
    return ap.unsqueeze(dim).to_broadcast(shape)


def run_together(*streams, filler=None):
    streams = deque(streams)
    turn, every = 0, len(streams)
    while streams:
        stream = streams.popleft()
        if filler is not None and turn % every == 0:
            next(filler, None)
        turn += 1
        try:
            next(stream)
            streams.append(stream)
        except StopIteration:
            pass


class WeightRing:

    def __init__(self, p, slots):
        self.p, self.slots, self.sems, self.uses = p, [], [], []
        self.free = deque()
        for s in slots:
            self.add(s, [])

    def add(self, slot, after):
        self.free.append((len(self.slots), after))
        self.sems.append(self.p.semaphore(f"weights_in_slot{len(self.slots)}"))
        self.slots.append(slot)
        self.uses.append(0)

    def drop(self, i):
        self.free = deque(x for x in self.free if x[0] != i)

    def load(self, src):
        i, readers = self.free.popleft()
        self.uses[i] += 1
        _, a, b = src.shape
        view = self.slots[i][:, 0:a * b].rearrange("p (a b) -> p a b", a=a)
        return view, self.p.dma("sp", view, src, self.sems[i], self.uses[i], readers), i

    def release(self, i, tok):
        self.free.append((i, [tok]))


class Banks:

    def __init__(self, tensors):
        self.free = deque((t, []) for t in tensors)

    def take(self):
        return self.free.popleft()

    def give(self, bank, *readers):
        self.free.append((bank, list(readers)))


class Arena:

    def __init__(self, tensor, size):
        self.t, self.size, self.at = tensor, size, 0

    def take(self, *dims):
        n = int(np.prod(dims))
        assert self.at + n <= self.size, (self.at + n, self.size)
        v = self.t[:, self.at:self.at + n]
        self.at += n
        if len(dims) == 2:
            v = v.rearrange("p (a b) -> p a b", a=dims[0])
        elif len(dims) == 3:
            v = v.rearrange("p (a b c) -> p a b c", a=dims[0], b=dims[1])
        elif len(dims) == 4:
            v = v.rearrange("p (a b c d) -> p a b c d", a=dims[0], b=dims[1], c=dims[2])
        return v


N_SLOTS = 3
ARENA = 35200
KEPT = ARENA - 2 * S


def build(nc, d, out, dump):
    with ExitStack() as ctx:
        p = Program(nc, ctx)

        def sb(name, shape, dt=F32):
            return ctx.enter_context(nc.sbuf_tensor(name, shape, dt))

        ring = WeightRing(p, [sb(f"slot{i}", [P, 4096]) for i in range(N_SLOTS)])
        banks = Banks([ctx.enter_context(nc.psum_tensor(f"bank{i}", [P, 512], F32)) for i in range(8)])

        par = sb("par", [P, N_PARAM])
        ident = sb("ident", [P, P])
        ones = sb("ones", [P, P])
        xT = sb("xT", [P, KT, S])
        hT = sb("hT", [P, KT, S])
        rms = sb("rms", [P, 3, S])
        mods = sb("mods", [P, 48, 2])
        arena_lifetime = ctx.enter_context(ExitStack())
        arena = arena_lifetime.enter_context(nc.sbuf_tensor("arena", [P, ARENA], F32))

        def par_of(name, i=0, n=1, rows=P):
            a = PARAM_AT[name][0] + i
            return par[0:rows, a:a + n]

        t_par = p.load("sp", par[:, :], d["params"], "params_in")
        t_x = p.load("sp", xT[:, :, :], d["xT"].rearrange("(k p) s -> p k s", p=P), "x_in")
        t_ident = p.load("act", ident[:, :], d["ident"], "ident_in")
        t_ones = p.op("dve", lambda e: e.memset(ones[:, :], 1.0))

        dumps = []

        def show(name, ap, after):
            if dump is None:
                return
            t = nc.dram_tensor("dump_" + name, tuple(ap.shape), F32, kind="ExternalOutput").ap()
            dump.append(("dump_" + name, tuple(ap.shape)))
            dumps.append(p.load("sp", t, ap, "s_" + name, after))

        def rsqrt(v, r, scratch, after):
            t1 = p.act(r, v, ACT.Ln, after=after)
            t2 = p.act(r, r, ACT.Exp, after=[t1], scale=-0.5)
            t3 = p.tt(scratch, v, r, ALU.mult, after=[t2])
            t4 = p.stt(scratch, scratch, -0.5, r, ALU.mult, ALU.mult, after=[t3])
            return p.stt(r, scratch, 1.5, r, ALU.add, ALU.mult, after=[t4])

        def channel_stats(src, n, sq, after, width=None):
            bank, free = banks.take()
            if len(after) == n:
                t_sq = [[p.act(sq[:, k, :], src[:, k, :], ACT.Square, after=[after[k]])] for k in range(n)]
            else:
                t_sq = [[p.act(sq, src, ACT.Square, after=after)]] * n
            for k in range(n):
                t_s = p.mm(bank[:, 0:S], ones[:, :], sq[:, k, :], k == 0, k == n - 1,
                           after=t_sq[k] + [t_ones] + free, signal=k == n - 1)
            t1 = p.ts(rms[:, 0, :], bank[:, 0:S], 1.0 / (width or n * P), EPS, ALU.mult, ALU.add, after=[t_s])
            banks.give(bank, t1)
            return p_rms(t1)

        def p_rms(t1):
            return rsqrt(rms[:, 0, :], rms[:, 1, :], rms[:, 2, :], [t1])

        def head_norm(src, heads, dst_list, sq, ss, after, gains=None):
            a = src.shape[1]
            t1 = p.tt(sq, src, src, ALU.mult, after=after)
            n = a * heads
            v, r, scratch = ss[:, 0, 0:n], ss[:, 1, 0:n], ss[:, 2, 0:n]
            t2 = p.reduce(v, sq.rearrange("p a h d -> p (a h) d"), ALU.add, after=[t1])
            t3 = p.ts(v, v, 1.0 / HD, EPS, ALU.mult, ALU.add, after=[t2])
            t4 = rsqrt(v, r, scratch, [t3])
            rb = bcast(r.rearrange("p (a h) -> p a h", a=a), 3, HD)
            return [p.tt(dst, src, rb, ALU.mult, after=[t4]) for dst in dst_list][-1]

        def proj_tokens(h, w, c0, n, tt, after):
            bank, free = banks.take()
            k_n = w.shape[1]
            for k in range(k_n):
                t = p.mm(bank[:, 0:n], h[:, k, tt * P:(tt + 1) * P], w[:, k, c0:c0 + n], k == 0, k == k_n - 1,
                         after=after + free, signal=k == k_n - 1)
            return bank, t

        def proj_channels(h, w, c0, bank, at, after, m=P):
            k_n = w.shape[1]
            for k in range(k_n):
                t = p.mm(bank[0:m, at:at + S], w[:, k, c0:c0 + m], h[:, k, :], k == 0, k == k_n - 1,
                         after=after, signal=k == k_n - 1)
            return t

        w_in = d["w_in"].rearrange("(k p) n -> p k n", p=P)

        def token_block(h, col, evac, src=w_in, n=512):
            w, t_w, slot = ring.load(src[:, :, col:col + n])
            for tt in range(NT):
                bank, t = proj_tokens(h, w, 0, n, tt, [t_w] + t_h_of[id(h)])
                banks.give(bank, *evac(tt, bank, t))
                yield
            ring.release(slot, t)

        def channel_block(h, col, evac, src=w_in, n_tiles=4):
            w, t_w, slot = ring.load(src[:, :, col:col + n_tiles * P])
            for pair in range(n_tiles // 2):
                bank, free = banks.take()
                for u in range(2):
                    t = proj_channels(h, w, (2 * pair + u) * P, bank, u * S, [t_w] + t_h_of[id(h)] + free)
                    if u == 0:
                        yield
                banks.give(bank, *evac(pair, bank, t))
                yield
            ring.release(slot, t)

        A = Arena(arena, KEPT)
        ysT = A.take(4, WT, S)
        merged = A.take(KT, S)
        t_rstd = channel_stats(xT[:, :, :], KT, merged, [t_x])
        for k in range(KT):
            t = p.stt(hT[:, k, :], xT[:, k, :], par_of("norm_g", k), rms[:, 1, :], ALU.mult, ALU.mult,
                      after=[t_rstd, t_par])
        t_h = [t]
        t_h_of = {id(hT): t_h}

        t_pos = p.load("act", merged, d["posT"].rearrange("(k p) s -> p k s", p=P), "position_in", [t])
        t_pos = p.tt(xT[:, :, :], xT[:, :, :], merged, ALU.add, after=[t_pos])

        causal_add = A.take(2 * P)
        causal_T = A.take(P)
        cmp_add = A.take(NT, 32)
        cmp_keep = A.take(NT, 32)
        sel, copy_of = A.take(8), A.take(4)
        lnv_row = A.take(512)
        b_sp = A.take(4, P)
        wsT = A.take(8, P)
        w_rg = A.take(2, 4, P)
        w_cmp2 = A.take(2, HD)
        w_f = A.take(KT, P)
        w_gate = A.take(KT, 3 * NH)
        t_c = []
        for view, src in ((causal_add, d["causal_add"]), (causal_T, d["causal_T"]),
                          (cmp_add, d["cmp_add"]), (cmp_keep, d["cmp_keep"]), (sel, d["sel"]), (copy_of, d["copy_of"])):
            t_c.append(p.load("act", view, src, f"const{len(t_c)}_in"))
        t_lnv = p.load("act", lnv_row, d["ln_v_g"].to_broadcast([P, 512]), "ln_v_g_in")
        t_bsp = []
        for u in range(2):
            src = d["b_spatial"][u::2, :].unsqueeze(0).to_broadcast([HD, 4, P])
            t_bsp.append(p.load("act", b_sp[u * HD:(u + 1) * HD], src, f"b_spatial{u}_in"))
        t_ws = p.load("act", wsT, d["w_spatial_T"], "w_spatial_in")
        t_rgw = []
        t_rgz = p.op("pool", lambda e: e.memset(w_rg, 0.0))
        for u in range(2):
            for i, name in enumerate(("w_rg_a", "w_rg_x")):
                t_rgw.append(p.load("act", w_rg[u * HD:(u + 1) * HD, i, :, u * HD:(u + 1) * HD],
                                    d[name].rearrange("(j u) k n -> u k j n", u=2)[u], f"{name}{u}_in", [t_rgz]))
        t_cw2 = [p.load("act", w_cmp2[:, i], d[n], n + "_in") for i, n in enumerate(("cmp_k_w2", "cmp_v_w2"))]
        t_z = p.op("dve", lambda e: e.memset(w_f, 0.0))
        t_wf = [p.load("act", w_f[:, :, c:c + NH], w_in[:, :, COL["fa"]:COL["fa"] + NH], f"w_fa{c}_in", [t_z])
                for c in (0, 32, 64, 96)]
        t_wg = p.load("act", w_gate, w_in[:, :, COL["gate"]:COL["gate"] + 3 * NH], "w_gate_in")

        q_tm, k_tm, v_tm = A.take(NT, NH, HD), A.take(NT, NH, HD), A.take(NT, W)
        qaT, kaT = A.take(WT, 2, S), A.take(WT, 2, S)
        sq = A.take(NT, NH, HD)
        head_ss = A.take(3, 16)
        sched = {}

        t_zero = {id(qaT): t_ones, id(kaT): t_ones}

        def heads_to_channels(src_tm, dst, gain, after):
            for pair in range(2):
                bank, free = banks.take()
                for u in range(2):
                    for tt in range(NT):
                        i = 2 * u + tt
                        hp = 2 * pair + u
                        t = p.transpose(bank[:, i * P:(i + 1) * P], src_tm[:, tt, 2 * hp:2 * hp + 2, :].rearrange("p h d -> p (h d)"),
                                        ident[:, :], after=[after, t_ident] + free, signal=i == 3)
                src = bank[:, :].rearrange("p (a s) -> p a s", a=2)
                pairs = slice(2 * pair, 2 * pair + 2)
                if len(dst.shape) == 3:
                    t = p.ts(dst[:, pairs, :], src, gain, None, ALU.mult, after=[t, t_par])
                    banks.give(bank, t)
                else:
                    ts_ = [p.ts(dst[r, pairs, j, :], src[r], gain[r], None, ALU.mult, after=[t, t_par, t_zero[id(dst)]])
                           for j, r in enumerate((slice(0, HD), slice(HD, P)))]
                    banks.give(bank, *ts_)
                    t = ts_[1]
                yield
            sched[id(dst)] = t

        def to_tokens(dst, n=512):
            def evac(tt, bank, t):
                sched[id(dst), tt] = p.act(dst[:, tt, 0:n], bank[:, 0:n], ACT.Copy, after=[t])
                return [sched[id(dst), tt]]
            return evac

        def flat(v):
            return v.rearrange("p a h d -> p a (h d)")

        def gate_block(n, name):
            def evac(pair, bank, t):
                t = p.act(ysT[:, n, 2 * pair:2 * pair + 2, :], bank[:, :].rearrange("p (a s) -> p a s", a=2),
                          ACT.Silu, after=[t])
                sched["gate", n, pair] = t
                return [t]
            return channel_block(hT, COL[name], evac)

        class Lane:

            def __init__(self, space, free=()):
                self.s = space[:, 0:2 * S].rearrange("p (j k) -> p j k", j=2)
                self.pT = space[:, 2 * S:4 * S].rearrange("p (a b) -> p a b", b=P)
                self.stat = A.take(4, 2)
                self.s_free, self.pT_free = list(free), list(free)

        def spare_banks(n):
            while len(banks.free) < n:
                yield

        def attend(lane, hp, qt, q_T, k_of, v_of, acc, after, first, last, gate=None):
            n_k = (qt + 1) * P
            cols = slice(qt * P, (qt + 1) * P)
            yield from spare_banks(3)
            bank, free = banks.take()
            for j in range(2):
                o = bank[:, j * S:j * S + n_k]
                t = p.mm(o, q_T[:, hp, j, cols], k_of(j)[:, 0:n_k], True, True, after=after + free, signal=j == 1)
            yield
            s = lane.s[:, :, 0:n_k]
            neg_max, total, inv = lane.stat[:, 0], lane.stat[:, 1], lane.stat[:, 2]
            mask = bcast(causal_add[:, 2 * P - n_k:2 * P], 1, 2)
            t = p.stt(s, bank[:, :].rearrange("p (j k) -> p j k", j=2)[:, :, 0:n_k], HD ** -0.5, mask,
                      ALU.mult, ALU.add, after=[t, t_c[0]] + lane.s_free)
            banks.give(bank, t)
            t = p.reduce(neg_max, s, ALU.max, after=[t], negate=True)
            t_e = [p.act(s[:, j, :], s[:, j, :], ACT.Exp, after=[t], bias=neg_max[:, j:j + 1],
                         accum_out=total[:, j:j + 1]) for j in range(2)]
            t = p.recip(inv, total, after=t_e)
            if gate is not None:
                t = p.tt(inv, inv, gate, ALU.mult, after=[t])
            t = p.tt(s, s, bcast(inv, 2, n_k), ALU.mult, after=[t])
            yield
            yield from spare_banks(3)
            bank, free = banks.take()
            n_kt = qt + 1
            for i in range(2 * n_kt):
                j, kt = divmod(i, n_kt)
                t1 = p.transpose(bank[:, i * P:(i + 1) * P], s[:, j, kt * P:(kt + 1) * P], ident[:, :],
                                 after=[t] + free, signal=i == 2 * n_kt - 1)
            lane.s_free = [t1]
            pT = lane.pT[:, 0:2 * n_kt, :]
            t = p.act(pT, bank[:, 0:2 * n_kt * P].rearrange("p (a b) -> p a b", b=P), ACT.Copy,
                      after=[t1] + lane.pT_free)
            banks.give(bank, t)
            yield
            for i in range(2 * n_kt):
                j, kt = divmod(i, n_kt)
                t1 = p.mm(acc[0][j * HD:(j + 1) * HD, cols], v_of(kt, j), pT[:, i, :],
                          first and kt == 0 and qt == 0, last and kt == n_kt - 1, after=[t] + after + acc[1],
                          signal=i == 2 * n_kt - 1, loose=True)
            lane.pT_free = [t1]
            lane.last = t1

        def finish_head_pair(n, hp, acc, t):
            t = p.tt(ysT[:, n, hp, :], ysT[:, n, hp, :], acc[0][:, 0:S], ALU.mult,
                     after=[t, sched["gate", n, hp // 2]])
            banks.give(acc[0], t)
            sched["ys", n, hp] = t

        def fox_decay():
            bank, free = banks.take()
            t = proj_channels(hT, w_f, 0, bank, 0, t_wf + t_h + free)
            yield
            f, u, c = fox_f[:, 0], fox_f[:, 1], fox_f[:, 2]
            t1 = p.ts(f, bank[:, 0:S], par_of("b_forget"), None, ALU.add, after=[t, t_par])
            banks.give(bank, t1)
            t = p.stt(u, f, -1.0, f, ALU.mult, ALU.max, after=[t1])
            t = p.act(u, u, ACT.Exp, after=[t], scale=-1.0)
            t = p.act(u, u, ACT.Ln, after=[t], bias=1.0)
            t = p.stt(u, f, 0.0, u, ALU.min, ALU.subtract, after=[t])
            t = p.op("dve", lambda e: e.tensor_tensor_scan(c, ones_row, u, 0.0, ALU.mult, ALU.add),
                     after=[t, t_ones_row])
            tq = [p.op("dve", lambda e: e.memset(f, 1.0), after=[t])]
            tk = [p.op("dve", lambda e: e.memset(u, 1.0), after=[t])]
            for r in (0, HD):
                tq.append(p.ts(f[r + 32:r + HD], c[r + 32:r + HD], 8.0, None, ALU.mult, after=[t, tq[0]]))
                tk.append(p.ts(u[r:r + 32], c[r:r + 32], -8.0, None, ALU.mult, after=[t, tk[0]]))
            t_a = []
            for j, rows in enumerate((slice(HD, P), slice(0, HD))):
                own = sel[rows].rearrange("p (h j) -> p h j", j=2)[:, :, j]
                t_a.append(p.tt(qaT[rows, :, j, :], bcast(own, 2, S), bcast(f[rows], 1, WT), ALU.mult,
                                after=tq + [t_c[4]]))
                t_a.append(p.copy(kaT[rows, :, j, :], bcast(u[rows], 1, WT), after=tk))
            sched["aug"] = t_a

        ones_row = A.take(S)
        t_ones_row = p.op("dve", lambda e: e.memset(ones_row, 1.0))
        fox_f = A.take(3, S)
        lanes = [Lane(A.take(4 * S)) for _ in range(3)]

        def until(*keys):
            while not all(k in sched for k in keys):
                yield

        def fox(lane, hp):
            acc = banks.take()
            for qt in range(NT):
                yield from attend(lane, hp, qt, qaT, lambda j: kaT[:, hp, j, :],
                                  lambda kt, j: v_tm[:, kt, (2 * hp + j) * HD:(2 * hp + j + 1) * HD], acc,
                                  sched["aug"] + [sched[id(qaT)], sched[id(kaT)]]
                                  + [sched[id(v_tm), tt] for tt in range(NT)], True, True)
            finish_head_pair(0, hp, acc, lane.last)

        qc_tm, kv_tm = A.take(NT, NH, HD), A.take(NT, 4, 2, HD)
        k_dup = A.take(2, NT, 2, 2 * HD).rearrange("p a b c (d e) -> p a b c d e", d=2)
        qcT = A.take(WT, 2, S)
        t_zero[id(qcT)] = p.op("pool", lambda e: e.memset(qcT, 0.0))
        kT2 = A.take(2, 2, S)
        two_xb = A.take(WT * (3 + S))
        two = two_xb[:, 0:4 * S].rearrange("p (i g s) -> p i g s", i=2, g=2)
        blocks_cmp = A.take(2 * 16 * 30 + 2 * P)
        cmp_tm = blocks_cmp[:, 960:].rearrange("p (i n) -> p i n", i=2)
        blocks = blocks_cmp[:, 0:960].rearrange("p (i r g b) -> p i r g b", i=2, r=16, g=2)
        cmp_h = A.take(2, 2, 4, 32)
        vc, vcz = A.take(2, HD), A.take(2, 4, HD)
        kc = A.take(2, 2, HD)
        kc_n = A.take(2, 2, HD)
        kcT = A.take(2, 32)
        gates = A.take(NT, 3 * NH)
        p_c = A.take(NH, 32)
        p_cT = A.take(2, S)
        c_stat = A.take(3, NH)
        n_cmp = 15

        def gates_c():
            for tt in range(NT):
                bank, t = proj_tokens(hT, w_gate, 0, 3 * NH, tt, [t_wg] + t_h)
                t = p.act(gates[:, tt, :], bank[:, 0:3 * NH], ACT.Sigmoid, after=[t])
                sched["gates", tt] = t
                banks.give(bank, t)
                yield

        def compress():
            def evac(pair, bank, t):
                t_e = []
                for i in range(2):
                    for g in range(2):
                        src = bank[g * HD:(g + 1) * HD, i * S:(i + 1) * S]
                        t_e.append(p.act(two[0:HD, i, g, :], src, ACT.Copy, after=[t]))
                        t_e.append(p.act(two[HD:P, i, g, 0:S - 1], src[:, 1:S], ACT.Copy, after=[t]))
                sched["two"] = t_e
                return t_e
            yield from channel_block(hT, COL["kcc"], evac, n_tiles=2)
            t_b = []
            pos = bcast(par_of("cmp_pos", 0, 16), 2, n_cmp)
            for i in range(2):
                for g in range(2):
                    for first in range(2):
                        src = two[:, i, g, 16 * first:16 * first + 240].rearrange("p (b r u) -> p r b u", r=8, u=2)
                        r = slice(8 * first, 8 * first + 8)
                        t_b.append(p.tt(blocks[:, i, r, g, :], src[:, :, :, 0], pos[:, r, :], ALU.add,
                                        after=sched["two"] + [t_par]))
            sched["blocks"] = t_b
            t_z = p.op("dve", lambda e: e.memset(cmp_h, 0.0))
            for i, name in enumerate(("cmp_k_w1", "cmp_v_w1")):
                w1, t_w, slot = ring.load(d[name].rearrange("(r k) n -> k r n", k=P))
                bank, free = banks.take()
                for r in range(16):
                    t = p.mm(bank[0:30, 0:P], blocks[:, i, r, :, :].rearrange("p g b -> p (g b)"), w1[:, r, :], r == 0,
                             r == 15, after=[t_w] + t_b + free, signal=r == 15)
                ring.release(slot, t)
                yield
                t = p.act(cmp_tm[0:30, i], bank[0:30, 0:P], ACT.Silu, after=[t])
                banks.give(bank, t)
                bank, free = banks.take()
                t = p.transpose(bank[:, 0:30], cmp_tm[0:30, i], ident[0:30, 0:30], after=[t] + free, signal=True)
                yield
                t_s = [p.act(cmp_h[:, i, g, :, 0:n_cmp], bcast(bank[:, 15 * g:15 * g + 15], 1, 4), ACT.Copy,
                             after=[t, t_z]) for g in range(2)]
                banks.give(bank, *t_s)
                sched["cmp_h", i] = t_s
            bank, free = banks.take()
            for g in range(2):
                t = p.mm(bank[0:32, g * HD:(g + 1) * HD], cmp_h[:, 0, g, 0, :], w_cmp2[:, 0, :], True, True,
                         after=sched["cmp_h", 0] + sched["cmp_h", 1] + t_cw2 + free)
            for g in range(2):
                t = p.mm(bank[:, P + g * HD:P + (g + 1) * HD], cmp_h[:, 1, g, :, :].rearrange("p a b -> p (a b)"),
                         w_cmp2[:, 1, :], True, True, signal=g == 1)
            yield
            t1 = p.copy(kc[0:32, 0], bank[0:32, 0:P].rearrange("p (g d) -> p g d", g=2), after=[t])
            t2 = p.copy(vc, bank[:, P:2 * P].rearrange("p (g d) -> p g d", g=2), after=[t])
            banks.give(bank, t1, t2)
            sched["vc"] = [p.tt(vcz[:, g], bcast(vc[:, g], 1, 4), bcast(copy_of, 2, HD), ALU.mult, after=[t2, t_c[5]])
                           for g in range(2)]
            t = head_norm(kc[0:32, 0:1], 2, [kc_n[0:32, :, c, :].unsqueeze(1) for c in range(2)],
                          kc[0:32, 1:2], c40[0:32], [t1])
            bank, free = banks.take()
            for g in range(2):
                t1 = p.transpose(bank[:, g * 32:(g + 1) * 32], kc_n[0:32, g].rearrange("p c d -> p (c d)"),
                                 ident[0:32, 0:32], after=[t] + free, signal=g == 1)
            yield
            t = p.ts(kcT, bank[:, 0:64].rearrange("p (g b) -> p g b", g=2), par_of("kn_c"), None, ALU.mult, after=[t1])
            banks.give(bank, t)
            sched["kcT"] = t

        c40 = A.take(3, 16)

        def keys_to_channels():
            for kind in range(2):
                src = kv_tm[:, :, 2 * kind, :, :]
                t = head_norm(src, 2, [k_dup[:, kind, :, :, c, :] for c in range(2)],
                              flat(sq)[:, 0, 0:2 * P].rearrange("p (a h d) -> p a h d", a=2, h=2), head_ss,
                              [sched[id(kv_tm), tt] for tt in range(NT)])
                bank, free = banks.take()
                for g in range(2):
                    for tt in range(NT):
                        i = 2 * g + tt
                        t1 = p.transpose(bank[:, i * P:(i + 1) * P], k_dup[:, kind, tt, g].rearrange("p c d -> p (c d)"),
                                         ident[:, :], after=[t] + free, signal=i == 3)
                yield
                t = p.ts(kT2[:, kind], bank[:, :].rearrange("p (g s) -> p g s", g=2), par_of("kn_c"), None,
                         ALU.mult, after=[t1, t_par])
                banks.give(bank, t)
                sched["kT2", kind] = t

        def nsa_compressed_weights():
            t_p = p.op("dve", lambda e: e.memset(p_c, 0.0))
            t_done = [t_p]
            for tt in range(NT):
                bank, free = banks.take()
                for h in range(NH):
                    t = p.mm(bank[:, h * 32:(h + 1) * 32], qcT[:, h // 2, h % 2, tt * P:(tt + 1) * P],
                             kcT[:, h // 4, :], True, True, after=[sched[id(qcT)], sched["kcT"]] + free,
                             signal=h == NH - 1)
                yield
                s3 = bank[:, 0:S].rearrange("p (h b) -> p h b", b=32)
                t = p.stt(p_c, s3, HD ** -0.5, bcast(cmp_add[:, tt], 1, NH), ALU.mult, ALU.add,
                          after=[t] + t_c + t_done)
                banks.give(bank, t)
                t = p.reduce(c_stat[:, 0], p_c, ALU.max, after=[t], negate=True)
                t = p.tt(p_c, p_c, bcast(c_stat[:, 0], 2, 32), ALU.add, after=[t])
                t = p.act(p_c, p_c, ACT.Exp, after=[t])
                t = p.reduce(c_stat[:, 1], p_c, ALU.add, after=[t])
                t = p.recip(c_stat[:, 2], c_stat[:, 1], after=[t])
                t = p.tt(c_stat[:, 2], c_stat[:, 2], gates[:, tt, 0:NH], ALU.mult, after=[t, sched["gates", tt]])
                t = p.tt(p_c, p_c, bcast(c_stat[:, 2], 2, 32), ALU.mult, after=[t])
                t = p.tt(p_c, p_c, bcast(cmp_keep[:, tt], 1, NH), ALU.mult, after=[t])
                bank, free = banks.take()
                for g in range(2):
                    t1 = p.transpose(bank[:, g * P:(g + 1) * P], p_c[:, 4 * g:4 * g + 4].rearrange("p h b -> p (h b)"),
                                     ident[:, :], after=[t] + free, signal=g == 1)
                t_done = [t1]
                yield
                t = p.copy(p_cT[:, :, tt * P:(tt + 1) * P], bank[:, 0:2 * P].rearrange("p (g q) -> p g q", g=2),
                           after=[t1])
                banks.give(bank, t)
                sched["p_cT", tt] = t

        def nsa(lane, hp):
            yield from until(("p_cT", 1), ("kT2", 1), ("gate", 2, 1))
            g = hp // 2
            acc = banks.take()
            for j in range(2):
                p.mm(acc[0][j * HD:(j + 1) * HD, 0:S], vcz[:, g, (2 * hp + j) % 4, :], p_cT[:, g, :], True, False,
                     after=acc[1] + sched["vc"] + [sched["p_cT", 0], sched["p_cT", 1]], loose=True)
            for kind in range(2):
                for qt in range(NT):
                    yield from attend(lane, hp, qt, qcT, lambda j: kT2[:, kind, g, :],
                                      lambda kt, j: kv_tm[:, kt, 2 * kind + 1, g, :], acc,
                                      [sched[id(qcT)], sched["kT2", kind]]
                                      + [sched[id(kv_tm), tt] for tt in range(NT)],
                                      False, kind == 1,
                                      gate=gates[:, qt, (1 + kind) * NH + 2 * hp:(1 + kind) * NH + 2 * hp + 2])
            finish_head_pair(2, hp, acc, lane.last)

        xb = two_xb.rearrange("p (a s) -> p a s", a=WT)
        def as_tiles(v):
            return v.rearrange("p a h d -> p (a h d)").rearrange("p (a s) -> p a s", a=WT)
        xc, la, lr, li = as_tiles(q_tm), as_tiles(k_tm), merged[:, 0:4, :], merged[:, 4:8, :]
        sp4 = A.take(3, 4)

        def lru_softplus():
            u, s, acc_ = sp4[:, 0], sp4[:, 1], sp4[:, 2]
            lam = par_of("lam", 0, 4)
            t = p.stt(s, lam, -1.0, lam, ALU.mult, ALU.max, after=[t_par])
            t = p.act(u, s, ACT.Exp, after=[t], scale=-1.0)
            t = p.ts(s, u, 2.0, None, ALU.add, after=[t])
            t = p.recip(s, s, after=[t])
            t = p.tt(u, u, s, ALU.mult, after=[t])
            t = p.tt(s, u, u, ALU.mult, after=[t])
            t = p.ts(acc_, s, 1 / 15, 1 / 13, ALU.mult, ALU.add, after=[t])
            for c in (1 / 11, 1 / 9, 1 / 7, 1 / 5, 1 / 3, 1.0):
                t = p.tt(acc_, acc_, s, ALU.mult, after=[t])
                t = p.ts(acc_, acc_, c, None, ALU.add, after=[t])
            t = p.stt(acc_, acc_, 8.0, u, ALU.mult, ALU.mult, after=[t])
            t = p.ts(s, lam, -1.0, 0.0, ALU.mult, ALU.max, after=[t])
            t = p.stt(u, s, 4.0, acc_, ALU.mult, ALU.add, after=[t])
            sched["sp4"] = t

        def lru():
            t_z = p.op("dve", lambda e: e.memset(xb[:, :, 0:3], 0.0), after=sched["blocks"])

            def evac(pair, bank, t):
                t = p.act(xb[:, 2 * pair:2 * pair + 2, 3:3 + S], bank[:, :].rearrange("p (a s) -> p a s", a=2),
                          ACT.Copy, after=[t] + sched["blocks"])
                sched["xb", pair] = t
                return [t]
            yield from channel_block(hT, COL["xb"], evac)
            t_x = [t_z, sched["xb", 0], sched["xb", 1], t_par]
            t_c4 = []
            for j in range(WT):
                t = p.ts(xc[:, j, :], xb[:, j, 0:S], par_of("conv_w", j), par_of("conv_b", j), ALU.mult, ALU.add,
                         after=t_x + [sched[id(qaT)]])
                for tap in range(1, 4):
                    t = p.stt(xc[:, j, :], xb[:, j, tap:tap + S], par_of("conv_w", 4 * tap + j), xc[:, j, :],
                              ALU.mult, ALU.add, after=[t])
                t_c4.append(t)
            t_g = []
            for i, (dst, b) in enumerate(((lr, "b_rg_a"), (li, "b_rg_x"))):
                for j in range(WT):
                    bank, free = banks.take()
                    t = p.mm(bank[:, 0:S], w_rg[:, i, j, :], xc[:, j, :], True, True,
                             after=t_rgw + [t_c4[j]] + free, signal=True)
                    yield
                    t = p.act(dst[:, j, :], bank[:, 0:S], ACT.Sigmoid, after=[t], bias=par_of(b, j))
                    banks.give(bank, t)
                    t_g.append(t)
            t_t = [p.act(lr[:, j, :], lr[:, j, :], ACT.Tanh, after=t_g + [sched["sp4"]], scale=sp4[:, 0, j:j + 1])
                   for j in range(WT)]
            yield
            t1 = p.ts(la, lr, 1.0, None, ALU.add, after=t_t + [sched[id(kaT)]])
            t1 = p.recip(la, la, after=[t1])
            yield
            t2 = p.act(lr, lr, ACT.Sqrt, after=t_t + [t1])
            t = p.tt(li, li, xc, ALU.mult, after=t_g)
            t = p.tt(li, li, la, ALU.mult, after=[t, t1])
            yield
            t = p.stt(li, lr, 2.0, li, ALU.mult, ALU.mult, after=[t, t2])
            t1 = p.ts(la, la, 2.0, -1.0, ALU.mult, ALU.add, after=[t])
            yield
            for j in range(WT):
                t = p.op("dve", lambda e, j=j: e.tensor_tensor_scan(xc[:, j, :], la[:, j, :], li[:, j, :], 0.0,
                                                                   ALU.mult, ALU.add), after=[t1, t])
            t = p.tt(ysT[:, 1], ysT[:, 1], xc, ALU.mult, after=[t, sched["gate", 1, 0], sched["gate", 1, 1]])
            for j in range(WT):
                sched["ys", 1, j] = t

        uT = k_dup.rearrange("p a b c d e -> p (a b c d e)").rearrange("p (a s) -> p a s", a=WT)
        vd = flat(qc_tm)
        bn = A.take(NT, 12)

        def spatial():
            t_m = p.tt(wsT, wsT, bcast(causal_T, 1, 8), ALU.mult, after=[t_ws, t_c[1]])

            def evac_u(pair, bank, t):
                sched["u", pair] = p.act(uT[:, 2 * pair:2 * pair + 2, :], bank[:, :].rearrange("p (a s) -> p a s", a=2),
                                         ACT.Gelu, after=[t, sched["kT2", 0], sched["kT2", 1]])
                return [sched["u", pair]]

            def evac_v(tt, bank, t):
                sched["v", tt] = p.act(vd[:, tt, :], bank[:, :], ACT.Gelu, after=[t, sched[id(qcT)]])
                return [sched["v", tt]]
            yield from channel_block(hT, COL["ud"], evac_u)
            yield from token_block(hT, COL["vd"], evac_v)
            t_n = []
            for tt in range(NT):
                st, mv = bn[:, tt, 0:6], bn[:, tt, 6:8]
                t = p.op("dve", lambda e, tt=tt, st=st: e.bn_stats(st, vd[:, tt, :]), after=[sched["v", tt]])
                t = p.op("dve", lambda e, st=st, mv=mv: e.bn_aggr(mv, st), after=[t])
                t = p.ts(bn[:, tt, 8:9], bn[:, tt, 7:8], EPS, None, ALU.add, after=[t])
                t = rsqrt(bn[:, tt, 8:9], bn[:, tt, 9:10], bn[:, tt, 10:11], [t])
                t = p.ts(vd[:, tt, :], vd[:, tt, :], bn[:, tt, 6:7], bn[:, tt, 9:10], ALU.subtract, ALU.mult, after=[t])
                t_n.append(p.tt(vd[:, tt, :], vd[:, tt, :], lnv_row, ALU.mult, after=[t, t_lnv]))
            yield
            for j in range(WT):
                bank, free = banks.take()
                for tt in range(NT):
                    for u in range(2):
                        g = 2 * j + u
                        t = p.mm(bank[u * HD:(u + 1) * HD, tt * P:(tt + 1) * P], vd[:, tt, g * HD:(g + 1) * HD],
                                 wsT[:, g, :], True, True, after=[t_m] + t_n + free,
                                 signal=tt == NT - 1 and u == 1)
                yield
                t1 = p.tt(uT[:, j, :], uT[:, j, :], ysT[:, 3, j, :], ALU.mult,
                          after=[sched["u", j // 2], sched["gate", 3, j // 2]])
                t = p.tt(ysT[:, 3, j, :].rearrange("p (a t) -> p a t", a=NT),
                         bank[:, 0:S].rearrange("p (a t) -> p a t", a=NT), bcast(b_sp[:, j], 1, NT), ALU.add,
                         after=[t, t1] + t_bsp)
                banks.give(bank, t)
                sched["ys", 3, j] = p.tt(ysT[:, 3, j, :], ysT[:, 3, j, :], uT[:, j, :], ALU.mult, after=[t])

        ada_row = w_f.rearrange("p k n -> p (k n)").rearrange("p (a n) -> p a n", a=2)

        def ada():
            cond = par_of("cond", 0, 16).rearrange("p (k c) -> p k c", c=2)
            t_s = p.act(cond, cond, ACT.Silu, after=[t_par])
            t_row = [[], []]
            ada_w = d["ada_w"].rearrange("(k p) n -> p k n", p=P)
            for c in range(12):
                w, t_w, slot = ring.load(ada_w[:, :, c * 512:(c + 1) * 512])
                bank, free = banks.take()
                for k in range(KT):
                    t = p.mm(bank[0:2, :], cond[:, k, :], w[:, k, :], k == 0, k == KT - 1, after=[t_w, t_s] + free,
                             signal=k == KT - 1)
                ring.release(slot, t)
                yield
                row = ada_row[0:2, c % 2]
                t = p.copy(row, bank[0:2, :], after=[t] + t_row[c % 2])
                banks.give(bank, t)
                bank, free = banks.take()
                for i in range(4):
                    t1 = p.transpose(bank[:, 2 * i:2 * i + 2], row[:, i * P:(i + 1) * P], ident[0:2, 0:2],
                                     after=[t, t_ident] + free, signal=i == 3)
                t_row[c % 2] = [t1]
                t = p.tt(mods[:, 4 * c:4 * c + 4, :], bank[:, 0:8].rearrange("p (a c) -> p a c", c=2),
                         bcast(par_of("ada_b", 4 * c, 4), 2, 2), ALU.add, after=[t1])
                banks.give(bank, t)
                sched["mods", c] = t
                yield

        m_tmp = arena[:, KEPT:ARENA].rearrange("p (a s) -> p a s", a=2)
        m_tmp_free = [[], []]

        def merge():
            t_m = {}
            step = 0
            for n in (1, 3, 0, 2):
                yield from until(*[("ys", n, j) for j in range(WT)])
                t_y = [sched["ys", n, j] for j in range(WT)]
                wb, t_wb, slot_b = ring.load(d["w_branch"][n].rearrange("(k p) n -> p k n", p=P))
                for half in range(2):
                    col = COL["mg"] + n * D + half * 512
                    wm, t_wm, slot_m = ring.load(w_in[:, :, col:col + 512])
                    for i in range(4):
                        dt = 4 * half + i
                        bank, free = banks.take()
                        proj_channels(hT, wm, i * P, bank, 0, [t_wm] + free)
                        for k in range(WT):
                            t = p.mm(bank[:, S:2 * S], wb[:, k, dt * P:(dt + 1) * P], ysT[:, n, k, :], k == 0,
                                     k == WT - 1, after=[t_wb] + t_y, signal=k == WT - 1)
                        tmp = m_tmp[:, step % 2]
                        t1 = p.act(tmp, bank[:, 0:S], ACT.Sigmoid, after=[t] + m_tmp_free[step % 2])
                        if not t_m.get(dt):
                            t2 = p.tt(merged[:, dt, :], tmp, bank[:, S:2 * S], ALU.mult, after=[t1])
                            banks.give(bank, t2)
                        else:
                            t2 = p.tt(tmp, tmp, bank[:, S:2 * S], ALU.mult, after=[t1])
                            banks.give(bank, t2)
                            t2 = p.tt(merged[:, dt, :], merged[:, dt, :], tmp, ALU.add, after=[t2, t_m[dt]])
                        m_tmp_free[step % 2] = [t2]
                        t_m[dt] = t2
                        step += 1
                        yield
                    ring.release(slot_m, t)
                ring.release(slot_b, t)
            sched["merged"] = list(t_m.values())
        def chain(*streams):
            for s_ in streams:
                yield from s_

        def qk_fox():
            for src, dst, g in ((q_tm, qaT, "qn_a"), (k_tm, kaT, "kn_a")):
                t = head_norm(src, NH, [src], sq, head_ss, [sched[id(src), tt] for tt in range(NT)])
                yield
                yield from heads_to_channels(src, dst, par_of(g), t)

        def q_nsa():
            t = head_norm(qc_tm, NH, [qc_tm], sq, head_ss, [sched[id(qc_tm), tt] for tt in range(NT)])
            yield
            yield from heads_to_channels(qc_tm, qcT, par_of("qn_c"), t)

        def tokens_of(dst, name, n=512):
            def evac(tt, bank, t):
                target = dst[:, tt]
                if len(target.shape) == 3:
                    target = target.rearrange("p a b -> p (a b)")
                elif len(target.shape) == 4:
                    target = target.rearrange("p a b c -> p (a b c)")
                sched[id(dst), tt] = p.act(target, bank[:, 0:n], ACT.Copy, after=[t])
                return [sched[id(dst), tt]]
            return token_block(hT, COL[name], evac)

        for _ in chain(tokens_of(q_tm, "qa"), tokens_of(k_tm, "ka")):
            pass
        lru_softplus()
        projections = chain(fox_decay(), tokens_of(v_tm, "va"), gate_block(0, "ga"), tokens_of(qc_tm, "qc"),
                            tokens_of(kv_tm, "ksc"), gates_c(), gate_block(1, "gb"), gate_block(2, "gc"),
                            gate_block(3, "gd"))
        keys_and_queries = chain(qk_fox(), until((id(qc_tm), 1)), q_nsa(), until((id(kv_tm), 1)), keys_to_channels())
        jobs = deque([(fox, 0), (fox, 1), (fox, 2)] + [(nsa, hp) for hp in range(WT)] + [(fox, 3)])

        def work(lane):
            yield from until("aug", id(qaT), id(kaT), (id(v_tm), 1))
            while jobs:
                job, hp = jobs.popleft()
                yield from job(lane, hp)

        filling = chain(until(("gate", 1, 1)), ada(), merge())

        def late_worker():
            yield from until(("kT2", 1))
            yield from work(Lane(sq.rearrange("p a h d -> p (a h d)"), p.now()))

        run_together(chain(projections, until(("cmp_h", 1)), lru(), spatial()),
                     chain(keys_and_queries, compress(), nsa_compressed_weights()),
                     *map(work, lanes), late_worker(), filler=filling)
        for n in range(4):
            show(f"ys{n}", ysT[:, n], [sched["ys", n, j] for j in range(WT)])

        B = Arena(arena, ARENA)
        cat, qk_set0 = B.take(KT, S), B.take(2, HG_HEADS, S)
        scratch8 = B.take(KT, S)
        KF = B.take(2, 2, 2 * 256)
        s_ctx = B.take(2, HG_HEADS, P)
        gs = B.take(KT, 2)
        zero = B.take(1)
        ones2 = B.take(S)
        x_region = B.at
        w_in2 = d["w_in_2"].rearrange("(k p) n -> p k n", p=P)
        HY, HG, FN = 0, 768, 3328
        t_zero1 = [None]

        gs_free = []

        def modulated_norm(src, dst, which, gain, part, sq, after):
            t = p.ts(gs[:, :, which], mods[:, 8 * (part + 1):8 * (part + 2), which], 1.0, None, ALU.add,
                     after=[sched["mods", c] for c in range(12)] + gs_free)
            t_gs = p.tt(gs[:, :, which], gs[:, :, which], par_of(gain, 0, KT), ALU.mult, after=[t])
            t_r = channel_stats(src, KT, sq, after)
            ts_ = []
            for k in range(KT):
                t1 = p.stt(dst[:, k, :], src[:, k, :], gs[:, k, which:which + 1], rms[:, 1, :], ALU.mult, ALU.mult,
                           after=[t_r, t_gs])
                ts_.append(p.act(dst[:, k, :], dst[:, k, :], ACT.Identity, after=[t1],
                                 bias=mods[:, 8 * part + k, which:which + 1]))
            gs_free[:] = [t1]
            return ts_

        def context():
            C = Arena(arena, ARENA)
            C.at = x_region
            ctxT, hc = C.take(KT, S), C.take(KT, S)
            f, e = C.take(2 * HG_HEADS, S), C.take(2 * HG_HEADS, S)
            v = C.take(NT, W)
            ke = ctxT.rearrange("p k s -> p (k s)").rearrange("p (t n) -> p t n", t=NT)
            start = p.now()
            t_ctx = p.load("act", ctxT, d["ctxT"].rearrange("(k p) s -> p k s", p=P), "ctx_in", start)
            yield
            for _ in range(8):
                yield
            yield from until(("mods", 11))
            t_hc = modulated_norm(ctxT, hc, 1, "norm1_g", 0, hc, [t_ctx])
            t_h_of[id(hc)] = t_hc
            yield

            def evac_f(direction):
                def evac(pair, bank, t):
                    a = 4 * direction + 2 * pair
                    t = p.act(f[:, a:a + 2, :], bank[:, :].rearrange("p (a s) -> p a s", a=2), ACT.Sigmoid, after=[t] + start)
                    sched["cf", direction, pair] = t
                    return [t]
                return evac

            def evac_v(tt, bank, t):
                sched["cv", tt] = p.act(v[:, tt, :], bank[:, :], ACT.Copy, after=[t] + start)
                return [sched["cv", tt]]
            t_e1 = p.op("dve", lambda e_: e_.memset(e[:, 0:4, S - 1:S], 1.0), after=start)
            t_e1 = p.op("dve", lambda e_: e_.memset(e[:, 4:8, 0:1], 1.0))
            for direction in range(2):
                yield from channel_block(hc, HG + 512 * (1 + direction), evac_f(direction), src=w_in2)
                for h in range(HG_HEADS):
                    a = 4 * direction + h
                    if direction == 0:
                        o, i_ = e[:, a, S - 2::-1], f[:, a, S - 1:0:-1]
                    else:
                        o, i_ = e[:, a, 1:S], f[:, a, 0:S - 1]
                    t = p.op("dve", lambda e_, o=o, i_=i_: e_.tensor_tensor_scan(
                        o, i_, zero.to_broadcast([P, S - 1]), 1.0, ALU.mult, ALU.add),
                        after=[sched["cf", direction, h // 2], t_e1, t_zero1[0]])
                a = slice(4 * direction, 4 * direction + 4)
                t = p.tt(f[:, a, :], f[:, a, :], e[:, a, :], ALU.mult, after=[t])
                t = p.tt(e[:, a, :], e[:, a, :], f[:, a, :], ALU.subtract, after=[t])
                yield
                for tt in range(NT):
                    bank, free = banks.take()
                    for h in range(HG_HEADS):
                        t1 = p.transpose(bank[:, h * P:(h + 1) * P], e[:, 4 * direction + h, tt * P:(tt + 1) * P],
                                         ident[:, :], after=[t] + free, signal=h == 3)
                    t2 = p.act(ke[:, tt, 512 * direction:512 * direction + 512], bank[:, :], ACT.Copy, after=[t1] + t_hc)
                    banks.give(bank, t2)
                    sched["ke", direction, tt] = t2
                    yield
            yield from token_block(hc, HG + 512 * 3, evac_v, src=w_in2)
            for direction in range(2):
                bank, free = banks.take()
                for h in range(HG_HEADS):
                    for tt in range(NT):
                        n = 512 * direction + h * P
                        t = p.mm(bank[:, h * P:(h + 1) * P], ke[:, tt, n:n + P], v[:, tt, h * P:(h + 1) * P],
                                 tt == 0, tt == NT - 1,
                                 after=free + [sched["ke", direction, tt], sched["cv", tt]],
                                 signal=h == 3 and tt == NT - 1)
                yield
                t = p.act(s_ctx[:, direction], bank[:, :].rearrange("p (h v) -> p h v", h=HG_HEADS), ACT.Copy,
                          after=[t])
                banks.give(bank, t)
                sched["s_ctx", direction] = t
            sched["ctx_done"] = [t]

        X = Arena(arena, ARENA)
        X.at = x_region
        cosF, sinF = X.take(NT, 256), X.take(NT, 256)
        icos, isin = X.take(2, S), X.take(2, S)
        cosL, sinL = X.take(NT, S), X.take(NT, S)
        csC = X.take(2, P)
        fn_w = X.take(2, P)
        xh_region = X.at
        decay = X.take(NT, 256)
        embT, h1, h2, red = X.take(S), X.take(S), X.take(S), X.take(S)
        w3 = X.take(1024)
        skip = X.take(512)
        hfb = X.take(2, 256)
        plus, minus = X.take(NT, 2, 256), X.take(NT, 2, 256)

        def filters():
            start = p.now()
            t_f = {n: p.load("act", v, src, n + "_in", start) for n, v, src in (
                ("cosF", cosF, d["cosF"]), ("sinF", sinF, d["sinF"]), ("icos", icos, d["icos"]),
                ("isin", isin, d["isin"]), ("cosL", cosL, d["cosL"]), ("sinL", sinL, d["sinL"]),
                ("csC", csC, d["csC"]), ("decay", decay, d["decay"]), ("embT", embT[0:33], d["embT"]),
                ("w3", w3[0:HD], d["filt_w3"]), ("skip", skip[0:1], d["hy_bias"]))}
            t_z = p.op("pool", lambda e: e.memset(fn_w, 0.0), after=start)
            sched["fn_w"] = [p.load("act", fn_w[u * HD:(u + 1) * HD, :, u * HD:(u + 1) * HD],
                                    d["fn_w"].rearrange("(j u) k n -> u k j n", u=2)[u], f"fn_w{u}_in", [t_z])
                             for u in range(2)]
            sched["dft"] = [t_f[n] for n in ("cosF", "sinF", "icos", "isin")]
            sched["dftL"] = [t_f[n] for n in ("cosL", "sinL", "csC")]
            yield
            t_in, rhs = [t_f["embT"]], embT[0:33]
            for layer, (w, b, out_) in enumerate((("filt_w1", "filt_b1", h1), ("filt_w2", "filt_b2", h2))):
                rows = 33 if layer == 0 else HD
                bank, free = banks.take()
                t = p.mm(bank[0:HD, 0:S], par_of(w, 0, HD, rows), rhs, True, True, after=t_in + [t_par] + free,
                         signal=True)
                yield
                o, r = out_[0:HD], red[0:HD]
                t = p.ts(o, bank[0:HD, 0:S], par_of(b, rows=HD), par_of("filt_fr", rows=HD), ALU.add, ALU.mult,
                         after=[t] + start)
                banks.give(bank, t)
                t = p.ts(r, o, 1 / (2 * math.pi), MAGIC, ALU.mult, ALU.add, after=[t])
                t = p.ts(r, r, MAGIC, None, ALU.subtract, after=[t])
                t = p.stt(o, r, -6.28125, o, ALU.mult, ALU.add, after=[t])
                t = p.stt(o, r, -(2 * math.pi - 6.28125), o, ALU.mult, ALU.add, after=[t])
                t = p.ts(o, o, 3.1415925, -3.1415925, ALU.min, ALU.max, after=[t])
                t = p.act(o, o, ACT.Sin, after=[t])
                t_in, rhs = [t], o
            t_pm = []
            t_used = list(start)
            for tt in range(NT):
                for o in range(2):
                    bank, free = banks.take()
                    t = p.mm(bank[:, :], h2[0:HD, tt * P:(tt + 1) * P], w3[0:HD, 512 * o:512 * o + 512], True, True,
                             after=t_in + [t_f["w3"]] + free, signal=True)
                    yield
                    t = p.tt(hfb, bank[:, :].rearrange("p (d c) -> p d c", d=2), bcast(decay[:, tt, :], 1, 2), ALU.mult,
                             after=[t, t_f["decay"]] + t_used)
                    banks.give(bank, t)
                    if tt == 0:
                        t1 = p.op("dve", lambda e: e.memset(hfb[0:1, 1, :], 0.0), after=[t])
                        t = p.tt(hfb[0:1, 0, :], hfb[0:1, 0, :], skip[0:1, 256 * o:256 * o + 256], ALU.add,
                                 after=[t, t1, t_f["skip"]])
                    t1 = p.tt(plus[:, tt, o, :], hfb[:, 0, :], hfb[:, 1, :], ALU.add, after=[t] + start)
                    t2 = p.tt(minus[:, tt, o, :], hfb[:, 0, :], hfb[:, 1, :], ALU.subtract, after=[t])
                    t_used = [t1, t2]
                    t_pm += t_used
            for ft in range(2):
                for ri, (mat, taps) in enumerate(((cosF, plus), (sinF, minus))):
                    bank, free = banks.take()
                    for tt in range(NT):
                        t = p.mm(bank[:, :], mat[:, tt, ft * P:(ft + 1) * P],
                                 taps[:, tt].rearrange("p o c -> p (o c)"), tt == 0, tt == NT - 1,
                                 after=t_pm + sched["dft"] + free, signal=tt == NT - 1)
                    yield
                    t = p.act(KF[:, ft, ri, :], bank[:, :], ACT.Copy, after=[t])
                    banks.give(bank, t)
                    sched["KF", ft, ri] = t
            sched["filters_done"] = [sched["KF", ft, ri] for ft in range(2) for ri in range(2)]

        t_all = p.now()
        t_zero1[0] = p.op("dve", lambda e: e.memset(zero, 0.0), after=t_all)
        for n in range(3):
            ring.add(arena[:, KEPT - 4096 * (n + 1):KEPT - 4096 * n], t_all)
        filter_steps = filters()

        def first_filter_step():
            next(filter_steps)
            yield

        run_together(filling, chain(context(), first_filter_step()))
        t_res = []
        w_out = d["w_out"].rearrange("(k p) n -> p k n", p=P)
        for half in range(2):
            w, t_w, slot = ring.load(w_out[:, :, half * 512:(half + 1) * 512])
            for i in range(4):
                bank, free = banks.take()
                t = proj_channels(merged, w, i * P, bank, 0, [t_w] + sched["merged"] + free)
                dt = 4 * half + i
                t1 = p.tt(xT[:, dt, :], xT[:, dt, :], bank[:, 0:S], ALU.add, after=[t])
                banks.give(bank, t1)
                t_res.append(t1)
            ring.release(slot, t)
        show("x1", xT[:, :, :], t_res)
        t_h_of[id(hT)] = modulated_norm(xT[:, :, :], hT, 0, "norm1_g", 0, hT, t_res)
        start2 = p.now()
        for n in range(3):
            ring.drop(N_SLOTS + n)

        R = Arena(arena, ARENA)
        R.at = KEPT
        r_w = R.take(KT, 16)
        weigh = R.take(20)
        r_b = R.take(16)
        t_rw = p.load("act", r_w, d["router_w"].rearrange("(k p) e -> p k e", p=P), "router_w_in", start2)
        t_rb = p.load("act", r_b, d["router_b"].to_broadcast([P, 16]), "router_b_in", start2)
        t_wei = p.load("act", weigh, d["weigh"].to_broadcast([P, 20]), "weigh_in", start2)

        X.at = xh_region
        z_hy = X.take(6, S + 2)
        u_hy = X.take(6, S)
        v_tok, x1_tok = X.take(NT, 256), X.take(NT, 256)
        Uf, Yf = X.take(2, 2, 256), X.take(2, 2, 256)
        prod = X.take(2, 2, 256)
        z_fn = X.take(2, S)
        f1 = X.take(NT, 2, 256)
        y_fn = X.take(2, S)
        hg_region = X.at
        Y = Arena(arena, ARENA)
        Y.at = hg_region
        q_hg = Y.take(HG_HEADS, S)
        pq = [Y.take(HG_HEADS, S) for _ in range(2)]
        pk = [Y.take(HG_HEADS, S) for _ in range(2)]
        k_hg = [Y.take(HG_HEADS, S) for _ in range(2)]
        v_hg = Y.take(NT, W)
        qk_set1 = Y.take(2, HG_HEADS, S)
        masks = Y.take(8 * P // 4).bitcast(U8).rearrange("p (l t) -> p l t", l=8)
        sc = scratch8.rearrange("p k s -> p (k s)").rearrange("p (c h t) -> p c h t", c=4, h=HG_HEADS)

        def channel_norm(src, n, dst, gain, sq, r3, after):
            bank, free = banks.take()
            t = p.act(sq, src, ACT.Square, after=after)
            for k in range(n):
                t1 = p.mm(bank[:, 0:S], ones[:, :], sq[:, k, :], k == 0, k == n - 1, after=[t] + free,
                          signal=k == n - 1)
            t = p.ts(r3[0], bank[:, 0:S], 1.0 / (n * P), EPS, ALU.mult, ALU.add, after=[t1])
            banks.give(bank, t)
            t = rsqrt(r3[0], r3[1], r3[2], [t])
            return [p.stt(dst[:, k, :], src[:, k, :], par_of(gain, k), r3[1], ALU.mult, ALU.mult, after=[t])
                    for k in range(n)]

        def hyena_z():
            t_z = [p.op("pool", lambda e, c=c: e.memset(z_hy[:, :, c:c + 1], 0.0), after=start2) for c in (0, S + 1)]

            def evac(base):
                def f(pair, bank, t):
                    a = base + 2 * pair
                    t = p.act(z_hy[:, a:a + 2, 1:S + 1], bank[:, :].rearrange("p (a s) -> p a s", a=2), ACT.Copy,
                              after=[t] + start2)
                    sched["z", a // 2] = t
                    return [t]
                return f
            yield from channel_block(hT, HY, evac(0), src=w_in2)
            yield from channel_block(hT, HY + 512, evac(4), src=w_in2, n_tiles=2)
            for j in range(6):
                t = p.ts(u_hy[:, j, :], z_hy[:, j, 0:S], par_of("hy_conv_w", j), par_of("hy_conv_b", j), ALU.mult,
                         ALU.add, after=t_z + [sched["z", j // 2]])
                for tap in (1, 2):
                    t = p.stt(u_hy[:, j, :], z_hy[:, j, tap:tap + S], par_of("hy_conv_w", 6 * tap + j), u_hy[:, j, :],
                              ALU.mult, ALU.add, after=[t])
                sched["u_hy", j] = t

        def hyena():
            for n, dst in enumerate((v_tok, x1_tok)):
                bank, free = banks.take()
                for tt in range(NT):
                    for j in range(2):
                        t = p.transpose(bank[:, (2 * tt + j) * P:(2 * tt + j + 1) * P],
                                        u_hy[:, 2 * n + j, tt * P:(tt + 1) * P], ident[:, :],
                                        after=[sched["u_hy", 2 * n + j]] + free, signal=tt == 1 and j == 1)
                t = p.act(dst, bank[:, :].rearrange("p (t c) -> p t c", t=NT), ACT.Copy, after=[t] + start2)
                banks.give(bank, t)
                sched["tok", n] = t
                yield
            t_in = [sched["tok", 0]]
            t_pr = list(start2)
            for o in range(2):
                t_y = []
                for ft in range(2):
                    bank, free = banks.take()
                    for ri, mat in enumerate((cosF, sinF)):
                        for tt in range(NT):
                            t = p.mm(bank[:, ri * 256:(ri + 1) * 256], mat[:, tt, ft * P:(ft + 1) * P], v_tok[:, tt, :],
                                     tt == 0, tt == NT - 1, after=t_in + sched["dft"] + free,
                                     signal=ri == 1 and tt == 1)
                    yield
                    u2 = bank[:, :].rearrange("p (r c) -> p r c", r=2)
                    oc = slice(256 * o, 256 * o + 256)
                    a, b = prod[:, 0], prod[:, 1]
                    t1 = p.tt(a, u2, bcast(KF[:, ft, 0, oc], 1, 2), ALU.mult, after=[t] + t_pr + sched["filters_done"])
                    t2 = p.tt(b, u2, bcast(KF[:, ft, 1, oc], 1, 2), ALU.mult, after=[t])
                    banks.give(bank, t1, t2)
                    t1 = p.tt(Yf[:, ft, 0], a[:, 0], b[:, 1], ALU.subtract, after=[t1, t2] + t_in)
                    t2 = p.tt(Yf[:, ft, 1], a[:, 1], b[:, 0], ALU.add, after=[t2])
                    t_pr = [t1, t2]
                    t_y += t_pr
                if o == 0:
                    bank, free = banks.take()
                    for tt in range(NT):
                        for n in range(4):
                            ft, ri = divmod(n, 2)
                            t = p.mm(bank[:, tt * 256:(tt + 1) * 256], (icos, isin)[ri][:, ft, tt * P:(tt + 1) * P],
                                     Yf[:, ft, ri, :], n == 0, n == 3, after=t_y + free, signal=tt == 1 and n == 3)
                    yield
                    t = p.tt(v_tok, x1_tok, bank[:, :].rearrange("p (t c) -> p t c", t=NT), ALU.mult,
                             after=[t, sched["tok", 1]])
                    banks.give(bank, t)
                    t_in = [t]
                else:
                    bank, free = banks.take()
                    for j in range(2):
                        for n in range(4):
                            ft, ri = divmod(n, 2)
                            t = p.mm(bank[:, j * S:(j + 1) * S], Yf[:, ft, ri, j * P:(j + 1) * P],
                                     (icos, isin)[ri][:, ft, :], n == 0, n == 3, after=t_y + free,
                                     signal=j == 1 and n == 3)
                    yield
                    y = u_hy[:, 4:6, :]
                    t = p.tt(y, y, bank[:, :].rearrange("p (j s) -> p j s", j=2), ALU.mult,
                             after=[t, sched["u_hy", 4], sched["u_hy", 5]])
                    banks.give(bank, t)
                    yield
                    sched["cat_hy"] = channel_norm(y, 2, cat[:, 0:2, :], "hy_norm_g", u_hy[:, 0:2, :],
                                                   (u_hy[:, 2, :], u_hy[:, 3, :], prod[:, 0, 0]), [t])

        def fourier():
            def evac(pair, bank, t):
                t = p.act(z_fn, bank[:, :].rearrange("p (a s) -> p a s", a=2), ACT.Copy, after=[t] + start2)
                sched["z_fn"] = t
                return [t]
            yield from channel_block(hT, FN, evac, src=w_in2, n_tiles=2)
            t_f1 = []
            for tt in range(NT):
                bank, free = banks.take()
                o = bank[:, :].rearrange("p (c j n) -> p c j n", c=2, j=2)
                for j in range(2):
                    t = p.mm(o[:, :, j, :], z_fn[:, j, tt * P:(tt + 1) * P], csC, True, True,
                             after=[sched["z_fn"]] + sched["dftL"] + free, signal=j == 1)
                yield
                t = p.act(f1[:, tt], bank[:, :].rearrange("p (c n) -> p c n", c=2), ACT.Copy, after=[t] + start2)
                banks.give(bank, t)
                t_f1.append(t)
            bank, free = banks.take()
            for j in range(2):
                for n in range(4):
                    tt, cs = divmod(n, 2)
                    t = p.mm(bank[:, j * S:(j + 1) * S], f1[:, tt, cs, j * P:(j + 1) * P], (cosL, sinL)[cs][:, tt, :],
                             n == 0, n == 3, after=t_f1 + free, signal=j == 1 and n == 3)
            yield
            t = p.act(y_fn, bank[:, :].rearrange("p (j s) -> p j s", j=2), ACT.Copy, after=[t] + start2)
            banks.give(bank, t)
            bank, free = banks.take()
            for j in range(2):
                t1 = p.mm(bank[:, j * S:(j + 1) * S], fn_w[:, j, :], y_fn[:, j, :], True, True,
                          after=[t] + sched["fn_w"] + free, signal=j == 1)
            yield
            t = [p.act(z_fn[:, j, :], bank[:, j * S:(j + 1) * S], ACT.Identity, after=[t1], bias=par_of("fn_b", j))
                 for j in range(2)]
            banks.give(bank, *t)
            yield
            sched["cat_fn"] = channel_norm(z_fn, 2, cat[:, 6:8, :], "fn_norm_g", y_fn,
                                           (f1[:, 0, 0], f1[:, 0, 1], f1[:, 1, 0]), t)

        def hgrn_z():
            wide = qk_set1.rearrange("p a h s -> p (a h s)")[:, 0:8 * P].rearrange("p (l t) -> p l t", l=8)
            t = p.load("act", wide, d["masks"], "masks_in", start2)
            sched["masks"] = p.copy(masks, wide, after=[t], eng="pool")
            base_q, base_f, base_v, base_g = HG, HG + 512, HG + 1536, HG + 2048

            def evac_to(dst, func, key):
                def evac(pair, bank, t):
                    t = p.act(dst[:, 2 * pair:2 * pair + 2, :], bank[:, :].rearrange("p (a s) -> p a s", a=2), func,
                              after=[t] + start2)
                    sched[key, pair] = t
                    return [t]
                return evac
            for i in range(2):
                yield from channel_block(hT, base_f + 512 * i, evac_to(pq[i], ACT.Sigmoid, ("f", i)), src=w_in2)
            yield from channel_block(hT, base_q, evac_to(q_hg, ACT.Silu, "q"), src=w_in2)
            for i in range(2):
                sched["k", i] = p.ts(k_hg[i], pq[i], -1.0, 1.0, ALU.mult, ALU.add,
                                     after=[sched[("f", i), 0], sched[("f", i), 1]])
                sched["pk", i] = p.op("pool", lambda e, i=i: e.memset(pk[i], 1.0), after=start2)
            sched["q_hg"] = p.ts(q_hg, q_hg, P ** -0.5, None, ALU.mult, after=[sched["q", 0], sched["q", 1]])

        def hgrn_vg():
            def evac_v(tt, bank, t):
                sched["v_hg", tt] = p.act(v_hg[:, tt, :], bank[:, :], ACT.Copy, after=[t] + start2)
                return [sched["v_hg", tt]]

            def evac_g(pair, bank, t):
                t = p.act(cat[:, 2 + 2 * pair:4 + 2 * pair, :], bank[:, :].rearrange("p (a s) -> p a s", a=2),
                          ACT.Silu, after=[t] + start2)
                sched["g_hg", pair] = t
                return [t]
            yield from token_block(hT, HG + 1536, evac_v, src=w_in2)
            yield from channel_block(hT, HG + 2048, evac_g, src=w_in2)

        def hgrn_scores():
            sets = [[qk_set0, []], [qk_set1, [sched["masks"]]]]
            step = 0

            def products(qv, kv, level_mask, tiles, after):
                for c, s_tile, t_tile in tiles:
                    bank, free = banks.take()
                    for h in range(HG_HEADS):
                        t = p.mm(bank[:, h * P:(h + 1) * P], kv[:, h, s_tile * P:(s_tile + 1) * P],
                                 qv[:, h, t_tile * P:(t_tile + 1) * P], True, True, after=after + free, signal=h == 3)
                    src = bank[:, :].rearrange("p (h t) -> p h t", h=HG_HEADS)
                    dst = sc[:, c]
                    if level_mask is None:
                        t1 = p.act(dst, src, ACT.Copy, after=[t] + start2)
                    else:
                        mask = bcast(masks[:, level_mask, :], 1, HG_HEADS)
                        t1 = p.op("dve", lambda e, dst=dst, mask=mask, src=src: e.copy_predicated(dst, mask, src),
                                  after=[t, sched["masks"], sched["sc", c]])
                    sched["sc", c] = t1
                    banks.give(bank, t1)
                return t

            set_, used = sets[0]
            t = p.tt(set_[:, 1], k_hg[0], k_hg[1], ALU.add, after=[sched["k", 0], sched["k", 1]] + start2)
            t = products(q_hg, set_[:, 1], None, ((0, 0, 0), (1, 1, 1)), [t, sched["q_hg"]])
            sets[0][1] = [t]
            yield
            state = [[sched["k", i], sched["pk", i], sched["q_hg"]] for i in range(2)]
            for level in range(LEVELS + 1):
                m = 2 ** level
                n_blocks = HG_HEADS * S // (2 * m)
                set_, used = sets[(level + 1) % 2]
                t_set = []
                for i in range(2):
                    hi, lo = (1, 0) if i == 0 else (0, 1)
                    edge = m - 1 if i == 0 else 0
                    eng = "dve" if i == 0 else "pool"

                    def halves(v):
                        return v.rearrange("p h s -> p (h s)").rearrange("p (b u m) -> p b u m", u=2, m=m)
                    t_q = p.tt(halves(set_[:, 0])[:, :, hi, :], halves(q_hg)[:, :, hi, :], halves(pq[i])[:, :, hi, :],
                               ALU.mult, after=state[i] + used + start2)
                    t_k = p.tt(halves(set_[:, 1])[:, :, lo, :], halves(k_hg[i])[:, :, lo, :],
                               halves(pk[i])[:, :, lo, :], ALU.mult, after=state[i] + used)
                    t_set += [t_q, t_k]
                    a, b = halves(pq[i]), halves(pk[i])
                    e_hi = a[:, :, hi, edge:edge + 1].to_broadcast([P, n_blocks, m])
                    e_lo = a[:, :, lo, edge:edge + 1].to_broadcast([P, n_blocks, m])
                    t_b = p.tt(b[:, :, lo, :], b[:, :, lo, :], e_hi, ALU.mult, after=[t_q, t_k], eng=eng)
                    t_a = p.tt(a[:, :, hi, :], a[:, :, hi, :], e_lo, ALU.mult, after=[t_q, t_k, t_b], eng=eng)
                    state[i] = [t_a, t_b]
                if level < LEVELS:
                    t = products(set_[:, 0], set_[:, 1], 1 + level, ((0, 0, 0), (1, 1, 1)), t_set)
                else:
                    t = products(set_[:, 0], set_[:, 1], None, ((2, 0, 1), (3, 1, 0)), t_set)
                sets[(level + 1) % 2][1] = [t]
                yield
            yield from until(("v_hg", 1), ("g_hg", 1))
            t_s = []
            for i in range(2):
                set_, used = sets[i]
                t_s.append(p.tt(set_[:, 0], q_hg, pq[i], ALU.mult, after=state[i] + used))
            yield
            out_banks = []
            for pair in range(2):
                bank, free = banks.take()
                for u in range(2):
                    h = 2 * pair + u
                    o = bank[:, u * S:(u + 1) * S]
                    for i in range(2):
                        p.mm(o, s_ctx[:, i, h, :], sets[i][0][:, 0, h, :], i == 0, False, loose=True,
                             after=t_s + free + [sched["s_ctx", 0], sched["s_ctx", 1]])
                    for n, (c, s_tile, t_tile) in enumerate(((0, 0, 0), (3, 1, 0), (2, 0, 1), (1, 1, 1))):
                        t = p.mm(o[:, t_tile * P:(t_tile + 1) * P], v_hg[:, s_tile, h * P:(h + 1) * P], sc[:, c, h, :],
                                 False, n == 3, loose=True, signal=u == 1 and n == 3,
                                 after=[sched["sc", k] for k in range(4)] + [sched["v_hg", k] for k in range(NT)])
                out_banks.append((bank, t))
            yield
            sq_, (v3, r3) = k_hg[0], (k_hg[1], pk[0])
            t_v = []
            for pair, (bank, t) in enumerate(out_banks):
                t = p.act(sq_[:, 2 * pair:2 * pair + 2, :], bank[:, :].rearrange("p (a s) -> p a s", a=2), ACT.Square,
                          after=[t])
                b2, free = banks.take()
                for u in range(2):
                    t1 = p.mm(b2[:, u * S:(u + 1) * S], ones[:, :], sq_[:, 2 * pair + u, :], True, True,
                              after=[t] + free, signal=u == 1)
                t1 = p.ts(v3[:, 2 * pair:2 * pair + 2, :], b2[:, :].rearrange("p (a s) -> p a s", a=2), 1.0 / P, EPS,
                          ALU.mult, ALU.add, after=[t1])
                banks.give(b2, t1)
                t_v.append(t1)
            yield
            t = rsqrt(v3, r3, pk[1], t_v)
            sched["cat_hg"] = []
            for h in range(HG_HEADS):
                bank, _ = out_banks[h // 2]
                t1 = p.stt(r3[:, h, :], bank[:, (h % 2) * S:(h % 2 + 1) * S], par_of("hg_norm_g", h), r3[:, h, :],
                           ALU.mult, ALU.mult, after=[t])
                if h % 2:
                    banks.give(bank, t1)
                sched["cat_hg"].append(p.tt(cat[:, 2 + h, :], cat[:, 2 + h, :], r3[:, h, :], ALU.mult,
                                            after=[t1, sched["g_hg", h // 2]]))

        run_together(hgrn_z(), filter_steps)
        start2[:] = p.now()
        run_together(hgrn_scores(), chain(hgrn_vg(), hyena_z(), fourier()), chain(until(("u_hy", 5)), hyena()))
        show("cat", cat, sched["cat_hy"] + sched["cat_hg"] + sched["cat_fn"])

        t_res2 = []
        w_out2 = d["w_out_2"].rearrange("(k p) n -> p k n", p=P)
        for half in range(2):
            w, t_w, slot = ring.load(w_out2[:, :, half * 512:(half + 1) * 512])
            for i in range(4):
                dt = 4 * half + i
                bank, free = banks.take()
                t = proj_channels(cat, w, i * P, bank, 0, [t_w] + free + sched["cat_hy"] + sched["cat_hg"] + sched["cat_fn"])
                t1 = p.stt(xT[:, dt, :], bank[:, 0:S], mods[:, 16 + dt, 0:1], xT[:, dt, :], ALU.mult, ALU.add, after=[t])
                banks.give(bank, t1)
                t_res2.append(t1)
            ring.release(slot, t)
        show("x2", xT[:, :, :], t_res2)

        t_h2 = modulated_norm(xT[:, :, :], hT, 0, "norm2_g", 3, hT, t_res2)
        start3 = p.now()
        M = Arena(arena, ARENA)
        logit, prob, pick, tmp16, oh1, oh2 = (M.take(NT, 16) for _ in range(6))
        pairs6, grp, grp2, grp3 = M.take(8, 6), M.take(8), M.take(8), M.take(8)
        one2 = M.take(4, 2)
        combT = rms[:, 2, :]
        combine = M.take(N_EXPERTS, S)
        zero3 = M.take(1)
        arena_lifetime.close()
        sb("kept_for_experts", [P, M.at])
        hT_hi, hT_lo = sb("tokens_high", [P, KT, S], F32R), sb("tokens_low", [P, KT, S], F32R)
        h_moe_hi, h_moe_lo = sb("hidden_high", [P, 4, S], F32R), sb("hidden_low", [P, 4, S], F32R)
        w_hi, w_lo = ([sb(f"{k}_weights_{part}", [P, 4096], F32R) for k in ("gate", "up", "down")]
                      for part in ("high", "low"))
        t_zm = p.op("pool", lambda e: e.memset(zero3, 0.0), after=start3)

        bank, free = banks.take()
        for tt in range(NT):
            for k in range(KT):
                t = p.mm(bank[:, tt * 16:(tt + 1) * 16], hT[:, k, tt * P:(tt + 1) * P], r_w[:, k, :], k == 0, k == KT - 1,
                         after=[t_rw] + t_h2 + free, signal=tt == 1 and k == KT - 1)
        before = p.now()
        taken = [banks.take() for _ in range(4)]
        gate_banks, up_banks = [b for b, _ in taken[0:2]], [b for b, _ in taken[2:4]]
        GATE, UP, DOWN = range(3)
        kinds = ("gate", "up", "down")
        w_moe = [ring.slots[i][:, :] for i, _ in ring.free]
        slot_readers = [readers for _, readers in ring.free]
        s_moe = hT[:, 0:4, :]
        tiles = (8, 8, 4)
        w_dram = [d["moe_w_" + n].rearrange("e (k p) n -> p (e k) n", p=P) for n in kinds]
        loaded, hi_done, lo_done, used = ([p.semaphore(f"moe_{n}_{what}") for n in kinds]
                                          for what in ("loaded", "high_part", "low_part", "used"))
        silu_done, prod_done, weighted_done, hid_hi_done, hid_lo_done, x_hi_done, x_lo_done = (
            p.semaphore("moe_" + n) for n in ("silu", "product", "weighted", "hidden_high", "hidden_low",
                                              "tokens_high", "tokens_low"))
        N_PIECES = 4
        piece = 4096 // N_PIECES
        for name in ("act", "dve"):
            p.wait(name, before)
        p.wait("pe", [t for _, free in taken for t in free])

        def load(e, kind, expert):
            n = tiles[kind]
            e.dma_start(w_moe[kind].rearrange("p (k n) -> p k n", k=n), w_dram[kind][:, bass.ds(n * expert, n)])\
                .then_inc(loaded[kind], 16)

        def high(e, kind, expert, reused=True):
            if reused:
                e.wait_ge(used[kind], expert + (1 if kind == DOWN else 0))
            for i in range(N_PIECES):
                part = slice(i * piece, (i + 1) * piece)
                if i == 0:
                    e.wait_ge(loaded[kind], 16 * expert + 16)
                e.activation(w_hi[kind][:, part], w_moe[kind][:, part], ACT.Copy).then_inc(hi_done[kind], 1)

        def low(e, kind, expert):
            for i in range(N_PIECES):
                part = slice(i * piece, (i + 1) * piece)
                e.wait_ge(hi_done[kind], N_PIECES * expert + (i + 1))
                e.tensor_tensor(w_lo[kind][:, part], w_moe[kind][:, part], w_hi[kind][:, part].bitcast(F32),
                                ALU.subtract).then_inc(lo_done[kind], 1)

        def three_passes(e, out, kind, k, c0, x_hi, x_lo, start, stop):
            n = 4096 // tiles[kind]
            hi, lo = (w[:, k * n + c0:k * n + c0 + P] for w in (w_hi[kind], w_lo[kind]))
            e.matmul(out, hi, x_hi, start=start, stop=False, skip_group_check=True)
            e.matmul(out, hi, x_lo, start=False, stop=False, skip_group_check=True)
            return e.matmul(out, lo, x_hi, start=False, stop=stop, skip_group_check=True)

        def pe_in(e, kind, expert):
            e.wait_ge(lo_done[kind], N_PIECES * expert + N_PIECES)
            for ft in range(4):
                bank = (gate_banks if kind == GATE else up_banks)[ft // 2]
                out_ = bank[:, ft % 2 * S:(ft % 2 + 1) * S]
                for k in range(KT):
                    mm = three_passes(e, out_, kind, k, ft * P, hT_hi[:, k, :], hT_lo[:, k, :], k == 0, k == KT - 1)
            mm.then_inc(used[kind], 1)

        def pe_down(e, expert, last=False):
            e.wait_ge(lo_done[DOWN], N_PIECES * expert + N_PIECES)
            e.wait_ge(hid_lo_done, 2 * expert + 2)
            for ft in range(4):
                for dt in range(KT):
                    mm = three_passes(e, acc_banks[dt // 2][:, dt % 2 * S:(dt % 2 + 1) * S], DOWN, ft, dt * P,
                                      h_moe_hi[:, ft, :], h_moe_lo[:, ft, :], False, last and ft == 3)
            mm.then_inc(used[DOWN], 1)

        def act_silu(e, expert):
            e.wait_ge(used[GATE], expert + 1)
            for half in range(2):
                e.activation(s_moe[:, 2 * half:2 * half + 2, :], gate_banks[half][:, :].rearrange("p (a s) -> p a s", a=2),
                             ACT.Silu).then_inc(silu_done, 1)

        def act_hidden(e, expert):
            for half in range(2):
                a = slice(2 * half, 2 * half + 2)
                e.wait_ge(weighted_done, 2 * expert + (half + 1))
                e.activation(h_moe_hi[:, a, :], s_moe[:, a, :], ACT.Copy).then_inc(hid_hi_done, 1)

        def dve_hidden(e, expert):
            e.wait_ge(silu_done, 2 * expert + 2)
            e.wait_ge(used[UP], expert + 1)
            for half in range(2):
                a = slice(2 * half, 2 * half + 2)
                e.tensor_tensor(s_moe[:, a, :], s_moe[:, a, :], up_banks[half][:, :].rearrange("p (a s) -> p a s", a=2),
                                ALU.mult).then_inc(prod_done, 1)
            for half in range(2):
                a = slice(2 * half, 2 * half + 2)
                e.wait_ge(prod_done, 2 * expert + (half + 1))
                e.tensor_tensor(s_moe[:, a, :], s_moe[:, a, :], combine[:, bass.ds(expert, 1), :].to_broadcast([P, 2, S]),
                                ALU.mult).then_inc(weighted_done, 1)
            for half in range(2):
                a = slice(2 * half, 2 * half + 2)
                e.wait_ge(hid_hi_done, 2 * expert + (half + 1))
                e.tensor_tensor(h_moe_lo[:, a, :], s_moe[:, a, :], h_moe_hi[:, a, :].bitcast(F32), ALU.subtract)\
                    .then_inc(hid_lo_done, 1)

        for kind in (GATE, UP, DOWN):
            p.wait("sp", slot_readers[kind])
            p.queues["sp"].append(lambda e, kind=kind: load(e, kind, 0))

        def act_first(e):
            for half in range(2):
                a = slice(4 * half, 4 * half + 4)
                e.activation(hT_hi[:, a, :], hT[:, a, :], ACT.Copy).then_inc(x_hi_done, 1)
            high(e, GATE, 0, reused=False)

        def dve_first(e):
            for half in range(2):
                a = slice(4 * half, 4 * half + 4)
                e.wait_ge(x_hi_done, half + 1)
                e.tensor_tensor(hT_lo[:, a, :], hT[:, a, :], hT_hi[:, a, :].bitcast(F32), ALU.subtract).then_inc(x_lo_done, 1)
            low(e, GATE, 0)

        def pe_first(e):
            e.wait_ge(x_lo_done, 2)
            pe_in(e, GATE, 0)

        for name, first in (("act", act_first), ("dve", dve_first), ("pe", pe_first)):
            p.queues[name].append(first)

        lg = bank[:, 0:32].rearrange("p (t e) -> p t e", t=NT)
        neg_max, total = one2[:, 0], one2[:, 1]
        t1 = p.reduce(neg_max, lg, ALU.max, after=[t] + start3, negate=True)
        t = p.tt(logit, lg, bcast(neg_max, 2, 16), ALU.add, after=[t1])
        banks.give(bank, t)
        t = p.act(prob, logit, ACT.Exp, after=[t])
        t = p.reduce(total, prob, ALU.add, after=[t])
        t = p.recip(total, total, after=[t])
        t = p.tt(prob, prob, bcast(total, 2, 16), ALU.mult, after=[t])
        t = p.tt(pick, prob, bcast(r_b, 1, NT), ALU.add, after=[t, t_rb])
        g4 = pick.rearrange("p t e -> p (t e)").rearrange("p (g e) -> p g e", e=4)
        t1 = p.tt(pairs6[:, :, 0:3], g4[:, :, 0:3], g4[:, :, 1:4], ALU.add, after=[t])
        t2 = p.tt(pairs6[:, :, 3:5], g4[:, :, 0:2], g4[:, :, 2:4], ALU.add, after=[t])
        t3 = p.tt(pairs6[:, :, 5:6], g4[:, :, 0:1], g4[:, :, 3:4], ALU.add, after=[t])
        t = p.reduce(grp, pairs6, ALU.max, after=[t1, t2, t3])

        def first_max(dst, src, n, weights, best, after):
            t = p.reduce(best, src, ALU.max, after=after)
            t = p.tt(dst, src, bcast(best, 2, n), ALU.is_equal, after=[t])
            t = p.tt(dst, dst, bcast(weights, 1, NT), ALU.mult, after=[t, t_wei])
            t = p.reduce(best, dst, ALU.max, after=[t])
            return p.tt(dst, dst, bcast(best, 2, n), ALU.is_equal, after=[t])

        t = first_max(grp2.rearrange("p (t g) -> p t g", t=NT), grp.rearrange("p (t g) -> p t g", t=NT), 4,
                      weigh[:, 16:20], one2[:, 2], [t])
        t1 = p.ts(grp3, grp2, 1.0, 1e30, ALU.subtract, ALU.mult, after=[t])
        t = p.tt(g4, g4, bcast(grp2, 2, 4), ALU.mult, after=[t])
        t = p.tt(g4, g4, bcast(grp3, 2, 4), ALU.add, after=[t, t1])
        t1 = first_max(oh1, pick, 16, weigh[:, 0:16], one2[:, 2], [t])
        t = p.stt(tmp16, oh1, -2e30, pick, ALU.mult, ALU.add, after=[t1])
        t = first_max(oh2, tmp16, 16, weigh[:, 0:16], one2[:, 3], [t])
        t = p.tt(oh1, oh1, oh2, ALU.add, after=[t])
        t = p.tt(oh1, oh1, prob, ALU.mult, after=[t])
        t = p.reduce(total, oh1, ALU.add, after=[t])
        t = p.recip(total, total, after=[t])
        t = p.tt(oh1, oh1, bcast(total, 2, 16), ALU.mult, after=[t])
        show("comb", oh1, [t])
        bank, free = banks.take()
        for tt in range(NT):
            t1 = p.transpose(bank[0:16, tt * P:(tt + 1) * P], oh1[:, tt, :], ident[:, :], after=[t] + free,
                             signal=tt == 1)
        t = p.copy(combT[0:16], bank[0:16, 0:S], after=[t1])
        banks.give(bank, t)
        t_comb = []
        for pair in range(N_EXPERTS // 2):
            bank, free = banks.take()
            for u in range(2):
                e = 2 * pair + u
                t1 = p.mm(bank[:, u * S:(u + 1) * S], ident[0:16, e:e + 1].to_broadcast([16, P]), combT[0:16], True, True,
                          after=[t] + free, signal=u == 1)
            t2 = p.act(combine[:, 2 * pair:2 * pair + 2, :], bank[:, :].rearrange("p (a s) -> p a s", a=2), ACT.Copy,
                       after=[t1])
            banks.give(bank, t2)
            t_comb.append(t2)

        acc_banks, acc_free = zip(*[banks.take() for _ in range(4)])
        p.wait("pe", [t for free in acc_free for t in free] + [t_zm])
        p.wait("dve", t_comb)

        def sp_loop(e):
            with e.Fori(0, N_EXPERTS - 1) as r:
                for kind in (GATE, UP, DOWN):
                    e.wait_ge(lo_done[kind], N_PIECES * r + N_PIECES)
                    load(e, kind, r + 1)

        def pe_loop(e):
            for b in acc_banks:
                mm = e.matmul(b[:, :], zero3.to_broadcast([P, P]), zero3.to_broadcast([P, 512]), start=True, stop=False, skip_group_check=True)
            mm.then_inc(used[DOWN], 1)
            with e.Fori(0, N_EXPERTS - 1) as r:
                pe_in(e, UP, r)
                e.wait_ge(silu_done, 2 * r + 2)
                pe_in(e, GATE, r + 1)
                pe_down(e, r)
            pe_in(e, UP, N_EXPERTS - 1)
            pe_down(e, N_EXPERTS - 1, last=True)

        def act_loop(e):
            high(e, UP, 0, reused=False)
            e.wait_ge(x_lo_done, 2)
            act_silu(e, 0)
            with e.Fori(0, N_EXPERTS - 1) as r:
                high(e, GATE, r + 1)
                act_hidden(e, r)
                high(e, DOWN, r)
                e.wait_ge(hid_lo_done, 2 * r + 2)
                act_silu(e, r + 1)
                high(e, UP, r + 1)
            act_hidden(e, N_EXPERTS - 1)
            high(e, DOWN, N_EXPERTS - 1)

        def dve_loop(e):
            low(e, UP, 0)
            with e.Fori(0, N_EXPERTS - 1) as r:
                low(e, GATE, r + 1)
                dve_hidden(e, r)
                low(e, DOWN, r)
                low(e, UP, r + 1)
            dve_hidden(e, N_EXPERTS - 1)
            low(e, DOWN, N_EXPERTS - 1)

        for name, loop in (("sp", sp_loop), ("pe", pe_loop), ("act", act_loop), ("dve", dve_loop)):
            p.queues[name].append(loop)
        t_moe = [(used[DOWN], N_EXPERTS + 1)]

        t_res3 = [p.stt(xT[:, dt, :], acc_banks[dt // 2][:, dt % 2 * S:(dt % 2 + 1) * S], mods[:, 40 + dt, 0:1],
                        xT[:, dt, :], ALU.mult, ALU.add, after=t_moe) for dt in range(KT)]
        for b in acc_banks + tuple(gate_banks) + tuple(up_banks):
            banks.give(b, t_res3[-1])
        t_r = channel_stats(xT[:, :, :], KT, combine[:, 0:8, :], t_res3)
        s_out = p.semaphore("out_written")
        out_v = out.rearrange("(k p) s -> p k s", p=P)
        for k in range(KT):
            t = p.stt(xT[:, k, :], xT[:, k, :], par_of("final_g", k), rms[:, 1, :], ALU.mult, ALU.mult, after=[t_r])
            if k % 2:
                t_o = p.dma("sp", out_v[:, k - 1:k + 1, :], xT[:, k - 1:k + 1, :], s_out, (k + 1) // 2, [t])
        p.wait("sp", [t_o] + dumps)

        block = ctx.enter_context(nc.Block())
        for name, where in (("sp", block.sync), ("pe", block.tensor), ("act", block.scalar), ("dve", block.vector),
                            ("pool", block.gpsimd)):
            def play(e, name=name):
                for instruction in p.queues[name]:
                    instruction(e)
            where(play)


def shape_constants():
    f = np.float32
    q = np.arange(P)
    c = {"ident": np.eye(P, dtype=f)}
    upper = np.where(q[None, :] > q[:, None], NEG, 0.0)
    c["causal_add"] = np.concatenate([np.zeros((P, P)), upper], axis=1).astype(f)
    c["causal_T"] = (q[:, None] <= q[None, :]).astype(f)
    t = np.arange(S).reshape(NT, P).T[:, :, None]
    b = np.arange(32)[None, None, :]
    ok = (b < 15) & (16 * b + 31 <= t)
    c["cmp_add"] = np.where(ok, 0.0, NEG).astype(f)
    c["cmp_keep"] = ok.astype(f)
    c["sel"] = (q[:, None] % 32 == np.arange(NH)[None, :]).astype(f)
    c["copy_of"] = (q[:, None] // 32 == np.arange(4)[None, :]).astype(f)
    d4 = D // 4
    omega = 1.0 / (10000.0 ** (np.arange(d4) / d4))
    ar, ac = (np.arange(S) // 64)[:, None] * omega, (np.arange(S) % 64)[:, None] * omega
    c["posT"] = np.concatenate([np.sin(ar), np.cos(ar), np.sin(ac), np.cos(ac)], axis=1).T.astype(f)
    tf = 2 * np.pi / (2 * S) * np.outer(np.arange(S), np.arange(256) + 0.5)

    def by_tiles(m):
        return np.ascontiguousarray(m.reshape(-1, P, m.shape[1]).transpose(1, 0, 2)).astype(f)
    c["cosF"], c["sinF"] = by_tiles(np.cos(tf)), by_tiles(-np.sin(tf))
    c["icos"], c["isin"] = by_tiles(np.cos(tf).T / 256), by_tiles(-np.sin(tf).T / 256)
    tk = 2 * np.pi / S * np.outer(np.arange(S), np.arange(S))
    c["cosL"], c["sinL"] = by_tiles(np.cos(tk) / 128), by_tiles(-np.sin(tk) / 128)
    cd = 2 * np.pi / HD * np.outer(np.arange(HD), np.arange(HD))
    c["csC"] = np.stack([np.kron(np.eye(2), np.cos(cd)), np.kron(np.eye(2), np.sin(cd))], axis=1).astype(f)
    pos = np.linspace(0.0, 1.0, S)[:, None]
    w = 2 * np.pi * np.arange(S)[:, None] / S
    bands = np.linspace(1e-4, 15, 16)[None, :]
    c["embT"] = np.concatenate([pos, np.cos(bands * w), -np.sin(bands * w)], axis=1).T.astype(f)
    deltas = np.linspace(math.log(1e-2) / 1.5, math.log(1e-2) / 0.3, 256)
    c["decay"] = by_tiles(np.exp(-pos * np.abs(deltas)[None, :]))
    masks = [np.eye(P, dtype=bool)]
    s_, t_ = q[:, None], q[None, :]
    for level in range(LEVELS):
        m = 2 ** level
        masks.append((s_ // (2 * m) == t_ // (2 * m)) & (s_ // m % 2 != t_ // m % 2))
    c["masks"] = np.stack(masks, axis=1).astype(f)
    c["weigh"] = np.concatenate([16.0 - np.arange(16), 4.0 - np.arange(4)])[None].astype(f)
    return c


def pack_params(i):
    out = np.zeros((P, N_PARAM), np.float32)

    def put(name, cols, rows=slice(0, P)):
        a, b = PARAM_AT[name]
        out[rows, a:b] = cols

    def tiles(v):
        return np.reshape(v, (-1, P)).T
    lo, hi = slice(0, HD), slice(HD, P)
    for name in ("norm_g", "conv_b", "b_rg_a", "b_rg_x"):
        put(name, tiles(i[name]))
    put("lam", tiles(i["lru_lambda"]))
    for name in ("qn_a", "kn_a", "qn_c", "kn_c"):
        for rows in (lo, hi):
            put(name, np.reshape(i[name], (HD, 1)), rows)
    put("conv_w", tiles(i["conv_w"]))
    for half, rows in enumerate((lo, hi)):
        put("cmp_pos", i["cmp_pos"][0][half::2].T, rows)
    for r in range(0, P, 32):
        put("b_forget", np.reshape(i["b_forget"], (NH, 1)), slice(r, r + NH))
    put("cond", np.stack([tiles(i["c_2"]), tiles(i["c_ctx_2"])], axis=2).reshape(P, 16))
    for name, src in (("ada_b", "ada_b_2"), ("norm1_g", "norm1_g_2"), ("norm2_g", "norm2_g_2"),
                      ("hy_conv_w", "hy_conv_w_2"), ("hy_conv_b", "hy_conv_b_2"), ("hy_norm_g", "hy_norm_g_2"),
                      ("hg_norm_g", "hg_norm_g_2"), ("fn_b", "fn_b_2"), ("fn_norm_g", "fn_norm_g_2"),
                      ("final_g", "final_norm_g_2")):
        put(name, tiles(i[src]))
    for name, src in (("filt_b1", "hy_filt_b1_2"), ("filt_b2", "hy_filt_b2_2"), ("filt_fr", "hy_filt_freq_2")):
        put(name, np.reshape(i[src], (HD, 1)), lo)
    put("filt_w1", i["hy_filt_w1_2"][0], slice(0, 33))
    put("filt_w2", i["hy_filt_w2_2"][0], lo)
    return out


DEBUG = False


def kernel(**inputs):
    import concourse.bacc as bacc
    from concourse.bass_utils import run_bass_kernel_spmd

    i = {k: np.asarray(v) for k, v in inputs.items()}
    arrays = dict(shape_constants())
    arrays["params"] = pack_params(i)
    arrays["xT"] = np.ascontiguousarray(i["x"][0].T)
    for name in ("w_in", "w_branch", "w_out", "w_rg_a", "w_rg_x", "cmp_k_w1", "cmp_k_w2", "cmp_v_w1", "cmp_v_w2", "b_spatial"):
        arrays[name] = i[name][0]
    arrays["ln_v_g"] = i["ln_v_g"]
    arrays["ctxT"] = np.ascontiguousarray(i["ctx_2"][0].T)
    for name, src in (("ada_w", "ada_w_2"), ("w_in_2", "w_in_2"), ("w_out_2", "w_out_2"), ("filt_w3", "hy_filt_w3_2"),
                      ("fn_w", "fn_w_2"), ("moe_w_gate", "moe_w_gate_2"), ("moe_w_up", "moe_w_up_2"),
                      ("moe_w_down", "moe_w_down_2")):
        arrays[name] = i[src][0]
    arrays["hy_bias"] = i["hy_bias_2"].reshape(1, 512)
    arrays["router_w"], arrays["router_b"] = i["router_w_2"], i["router_b_2"][None]
    arrays["w_spatial_T"] = np.ascontiguousarray(i["w_spatial"][0].transpose(2, 0, 1))
    nc = bacc.Bacc("TRN2", target_bir_lowering=False, num_devices=1)
    d = {n: nc.dram_tensor("in_" + n, a.shape, mybir.dt.from_np(a.dtype), kind="ExternalInput").ap()
         for n, a in arrays.items()}
    out = nc.dram_tensor("out", (D, S), F32, kind="ExternalOutput").ap()
    dump = [] if DEBUG else None
    build(nc, d, out, dump)
    r = run_bass_kernel_spmd(nc, [{"in_" + n: a for n, a in arrays.items()}], core_ids=[0]).results[0]
    y = np.ascontiguousarray(r["out"].T)[None]
    if DEBUG:
        return (y,) + tuple(r[n] for n, _ in dump)
    return y
```
